# Optimizing a Trainium2 kernel written in Bass

```python
import jax, jax.numpy as jnp
from jax import lax
import numpy as np

D_MODEL = 1024
BATCH = 1
SEQ = 512
DEPTH = 2

CHUNK = 64
ROPE_THETA = 10000.0
EPS = 1e-6
NEG = -1e30
N_BRANCH = 3

A_HEADS = 8
A_KV_HEADS = 2
A_HEAD_DIM = 64
A_WINDOW = 128
A_WIN_CHUNKS = A_WINDOW // CHUNK
A_WIDTH = A_HEADS * A_HEAD_DIM
A_KV_WIDTH = A_KV_HEADS * A_HEAD_DIM

B_HEADS = 4
B_KEY_DIM = 64
B_VAL_DIM = 128
B_GATE_RANK = 16
B_GATE_TAU = 16.0
B_KW = B_HEADS * B_KEY_DIM
B_WIDTH = B_HEADS * B_VAL_DIM

C_HEADS = 8
C_Q_RANK = 256
C_KV_RANK = 128
C_NOPE = 64
C_ROPE = 32
C_V = 64
C_WIDTH = C_HEADS * C_V
Q_BLOCK = 128

IN_SIZES = (
    A_WIDTH, A_KV_WIDTH, A_KV_WIDTH, A_WIDTH,
    B_KW, B_KW, B_WIDTH, B_GATE_RANK, B_WIDTH,
    C_Q_RANK, C_KV_RANK, C_ROPE, C_WIDTH,
    N_BRANCH * D_MODEL,
)
IN_WIDTH = sum(IN_SIZES)

kernel_name = "hybrid_swa_gla_mla_gated_merge"

def rmsnorm(x, g):
    xf = x.astype(jnp.float32)
    y = xf * lax.rsqrt(jnp.mean(xf * xf, axis=-1, keepdims=True) + EPS)
    return (y * g.astype(jnp.float32)).astype(x.dtype)

def rope_tables(seq, dim):
    pos = jnp.arange(seq, dtype=jnp.float32)
    inv = ROPE_THETA ** (-jnp.arange(0, dim, 2, dtype=jnp.float32) / dim)
    ang = pos[:, None] * inv[None, :]
    return jnp.cos(ang), jnp.sin(ang)

def apply_rope(x, cos, sin):
    half = x.shape[-1] // 2
    xf = x.astype(jnp.float32)
    x1, x2 = xf[..., :half], xf[..., half:]
    c = cos[None, :, None, :]
    s = sin[None, :, None, :]
    return jnp.concatenate([x1 * c - x2 * s, x2 * c + x1 * s], axis=-1).astype(x.dtype)

def split_cols(u):
    outs = []
    off = 0
    for n in IN_SIZES:
        outs.append(u[..., off:off + n])
        off += n
    return outs

def swa_sink_attention(q, k, v, sinks):
    B, S = q.shape[0], q.shape[1]
    nC = S // CHUNK
    G = A_HEADS // A_KV_HEADS
    pad = A_WIN_CHUNKS - 1
    qc = q.reshape(B, nC, CHUNK, A_KV_HEADS, G, A_HEAD_DIM)
    kc = k.reshape(B, nC, CHUNK, A_KV_HEADS, A_HEAD_DIM)
    vc = v.reshape(B, nC, CHUNK, A_KV_HEADS, A_HEAD_DIM)
    padw = ((0, 0), (pad, 0), (0, 0), (0, 0), (0, 0))
    kp = jnp.pad(kc, padw)
    vp = jnp.pad(vc, padw)
    kband = jnp.concatenate([kp[:, j:j + nC] for j in range(A_WIN_CHUNKS)], axis=2)
    vband = jnp.concatenate([vp[:, j:j + nC] for j in range(A_WIN_CHUNKS)], axis=2)
    key_chunk = jnp.arange(nC)[:, None] - pad + jnp.repeat(jnp.arange(A_WIN_CHUNKS), CHUNK)[None, :]
    valid = key_chunk >= 0
    s = jnp.einsum('bcqhgd,bckhd->bchgqk', qc, kband).astype(jnp.float32) * (A_HEAD_DIM ** -0.5)
    s = jnp.where(valid[None, :, None, None, None, :], s, NEG)
    sink = jnp.broadcast_to(sinks.astype(jnp.float32).reshape(A_KV_HEADS, G)[None, None, :, :, None, None],
                            s.shape[:-1] + (1,))
    p = jax.nn.softmax(jnp.concatenate([s, sink], axis=-1), axis=-1)[..., :-1].astype(v.dtype)
    o = jnp.einsum('bchgqk,bckhd->bcqhgd', p, vband)
    return o.reshape(B, S, A_WIDTH)

def gla_chunk_readout(q, k, v, log_a):
    B, S = q.shape[0], q.shape[1]
    nC = S // CHUNK
    out_dtype = v.dtype
    qf = q.astype(jnp.float32).reshape(B, nC, CHUNK, B_HEADS, B_KEY_DIM) * (B_KEY_DIM ** -0.5)
    kf = k.astype(jnp.float32).reshape(B, nC, CHUNK, B_HEADS, B_KEY_DIM)
    vf = v.astype(jnp.float32).reshape(B, nC, CHUNK, B_HEADS, B_VAL_DIM)
    g = jnp.cumsum(log_a.astype(jnp.float32).reshape(B, nC, CHUNK, B_HEADS, B_KEY_DIM), axis=2)
    g_end = g[:, :, -1]
    k_dec = kf * jnp.exp(g_end[:, :, None] - g)
    dS = jnp.einsum('bcthk,bcthv->bchkv', k_dec, vf)

    def step(state, inp):
        decay, ds = inp
        new = decay[..., None] * state + ds
        return new, new

    init = jnp.zeros((B, B_HEADS, B_KEY_DIM, B_VAL_DIM), jnp.float32)
    _, S_all = lax.scan(step, init, (jnp.moveaxis(jnp.exp(g_end), 1, 0), jnp.moveaxis(dS, 1, 0)))
    S_all = jnp.moveaxis(S_all, 0, 1)
    o = jnp.einsum('bcthk,bchkv->bcthv', qf, S_all)
    return o.reshape(B, S, B_HEADS, B_VAL_DIM).astype(out_dtype)

def mla_attention(q_nope, q_rope, k_nope, k_rope, v):
    B, S = q_nope.shape[0], q_nope.shape[1]
    nQ = S // Q_BLOCK
    scale = (C_NOPE + C_ROPE) ** -0.5
    key_chunk = jnp.arange(S) // CHUNK
    qn = jnp.moveaxis(q_nope.reshape(B, nQ, Q_BLOCK, C_HEADS, C_NOPE), 1, 0)
    qr = jnp.moveaxis(q_rope.reshape(B, nQ, Q_BLOCK, C_HEADS, C_ROPE), 1, 0)

    def block(args):
        i, qn_b, qr_b = args
        s = (jnp.einsum('bqhd,bkhd->bhqk', qn_b, k_nope).astype(jnp.float32)
             + jnp.einsum('bqhd,bkd->bhqk', qr_b, k_rope).astype(jnp.float32)) * scale
        q_chunk = (i * Q_BLOCK + jnp.arange(Q_BLOCK)) // CHUNK
        mask = key_chunk[None, :] <= q_chunk[:, None]
        s = jnp.where(mask[None, None], s, NEG)
        p = jax.nn.softmax(s, axis=-1).astype(v.dtype)
        return jnp.einsum('bhqk,bkhd->bqhd', p, v)

    out = lax.map(block, (jnp.arange(nQ), qn, qr))
    return jnp.moveaxis(out, 0, 1).reshape(B, S, C_WIDTH)

def hybrid_layer(x, norm_g, w_in, a_sinks, w_oa, w_alpha, b_alpha, b_head_g, w_ob,
                 cq_g, w_uq, ckv_g, w_ukv, w_oc, w_out, cos_a, sin_a, cos_c, sin_c):
    B, S, _ = x.shape
    h = rmsnorm(x, norm_g)
    (qa, ka, va, ga, qb, kb, vb, ab, gb, cq, ckv, kr, gc, mg) = split_cols(h @ w_in)

    qa = apply_rope(qa.reshape(B, S, A_HEADS, A_HEAD_DIM), cos_a, sin_a)
    ka = apply_rope(ka.reshape(B, S, A_KV_HEADS, A_HEAD_DIM), cos_a, sin_a)
    va = va.reshape(B, S, A_KV_HEADS, A_HEAD_DIM)
    ya = swa_sink_attention(qa, ka, va, a_sinks) * jax.nn.silu(ga)
    za = ya @ w_oa

    log_a = jax.nn.log_sigmoid((ab @ w_alpha + b_alpha).astype(jnp.float32)) / B_GATE_TAU
    yb = gla_chunk_readout(qb.reshape(B, S, B_HEADS, B_KEY_DIM), kb.reshape(B, S, B_HEADS, B_KEY_DIM),
                           vb.reshape(B, S, B_HEADS, B_VAL_DIM), log_a.reshape(B, S, B_HEADS, B_KEY_DIM))
    yb = rmsnorm(yb, b_head_g).reshape(B, S, B_WIDTH) * jax.nn.silu(gb)
    zb = yb @ w_ob

    q_c = (rmsnorm(cq, cq_g) @ w_uq).reshape(B, S, C_HEADS, C_NOPE + C_ROPE)
    q_nope = q_c[..., :C_NOPE]
    q_rope = apply_rope(q_c[..., C_NOPE:], cos_c, sin_c)
    kv = (rmsnorm(ckv, ckv_g) @ w_ukv).reshape(B, S, C_HEADS, C_NOPE + C_V)
    k_nope, v_c = kv[..., :C_NOPE], kv[..., C_NOPE:]
    k_rope = apply_rope(kr[:, :, None, :], cos_c, sin_c)[:, :, 0]
    yc = mla_attention(q_nope, q_rope, k_nope, k_rope, v_c) * jax.nn.silu(gc)
    zc = yc @ w_oc

    m = jax.nn.sigmoid(mg).reshape(B, S, N_BRANCH, D_MODEL)
    y = m[:, :, 0] * za + m[:, :, 1] * zb + m[:, :, 2] * zc
    return x + y @ w_out

def setup_inputs(seed: int = 0) -> dict:
    key = jax.random.key(seed)
    ks = jax.random.split(key, 18)
    f32 = jnp.float32

    def nrm(k, shape, scale):
        return jax.random.normal(k, shape, f32) * scale

    return {
        "x": nrm(ks[0], (BATCH, SEQ, D_MODEL), 1.0),
        "norm_g": 1.0 + nrm(ks[1], (DEPTH, D_MODEL), 0.02),
        "w_in": nrm(ks[2], (DEPTH, D_MODEL, IN_WIDTH), D_MODEL ** -0.5),
        "a_sinks": nrm(ks[3], (DEPTH, A_HEADS), 0.5),
        "w_oa": nrm(ks[4], (DEPTH, A_WIDTH, D_MODEL), A_WIDTH ** -0.5),
        "w_alpha": nrm(ks[5], (DEPTH, B_GATE_RANK, B_KW), B_GATE_RANK ** -0.5),
        "b_alpha": nrm(ks[6], (DEPTH, B_KW), 0.1),
        "b_head_g": 1.0 + nrm(ks[7], (DEPTH, B_VAL_DIM), 0.02),
        "w_ob": nrm(ks[8], (DEPTH, B_WIDTH, D_MODEL), B_WIDTH ** -0.5),
        "cq_g": 1.0 + nrm(ks[9], (DEPTH, C_Q_RANK), 0.02),
        "w_uq": nrm(ks[10], (DEPTH, C_Q_RANK, C_HEADS * (C_NOPE + C_ROPE)), C_Q_RANK ** -0.5),
        "ckv_g": 1.0 + nrm(ks[11], (DEPTH, C_KV_RANK), 0.02),
        "w_ukv": nrm(ks[12], (DEPTH, C_KV_RANK, C_HEADS * (C_NOPE + C_V)), C_KV_RANK ** -0.5),
        "w_oc": nrm(ks[13], (DEPTH, C_WIDTH, D_MODEL), C_WIDTH ** -0.5),
        "w_out": nrm(ks[14], (DEPTH, D_MODEL, D_MODEL), D_MODEL ** -0.5),
        "final_g": 1.0 + nrm(ks[15], (D_MODEL,), 0.02),
    }

def reference(x, norm_g, w_in, a_sinks, w_oa, w_alpha, b_alpha, b_head_g, w_ob,
              cq_g, w_uq, ckv_g, w_ukv, w_oc, w_out, final_g):
    S = x.shape[1]
    cos_a, sin_a = rope_tables(S, A_HEAD_DIM)
    cos_c, sin_c = rope_tables(S, C_ROPE)
    for l in range(DEPTH):
        x = hybrid_layer(x, norm_g[l], w_in[l], a_sinks[l], w_oa[l], w_alpha[l], b_alpha[l], b_head_g[l], w_ob[l],
                         cq_g[l], w_uq[l], ckv_g[l], w_ukv[l], w_oc[l], w_out[l], cos_a, sin_a, cos_c, sin_c)
    return rmsnorm(x, final_g)


_drawn_inputs = setup_inputs


def setup_inputs(seed=0):
    import zlib

    import numpy as np

    out = dict(_drawn_inputs(seed))
    spreads = {}
    factors = {'norm_g': 2.807,
     'a_sinks': 64.0,
     'b_alpha': 2.679,
     'b_head_g': 6.168,
     'cq_g': 8.0,
     'ckv_g': 8.0,
     'final_g': 8.214}
    for name, (base, spread) in spreads.items():
        noise = np.random.default_rng([zlib.crc32(name.encode()), seed]).standard_normal(out[name].shape)
        drawn = base * np.exp(spread * noise) if base else spread * noise
        out[name] = __import__('jax').numpy.asarray(drawn.astype(out[name].dtype))
    for name, factor in factors.items():
        out[name] = (out[name] * factor).astype(out[name].dtype)
    return out
```

```python
from contextlib import ExitStack

import numpy as np

import concourse.bass as bass
from concourse import mybir

F32 = mybir.dt.float32
F32R = mybir.dt.float32r
ALU = mybir.AluOpType
ACT = mybir.ActivationFunctionType
AX_X = mybir.AxisListType.X

DEPTH, D, S, CHUNK, P = 2, 1024, 512, 64, 128
EPS, NEG = 1e-6, -1e30
KT = D // P
TT = S // P
NC = S // CHUNK
A_HEADS, A_KV, A_DH = 8, 2, 64
GROUP = A_HEADS // A_KV
B_HEADS, B_DK, B_DV, B_RANK, B_TAU = 4, 64, 128, 16, 16.0
C_HEADS, C_QR, C_KVR, C_NOPE, C_ROPE, C_V = 8, 256, 128, 64, 32, 64
C_DH = C_NOPE + C_ROPE
A_SCALE, C_SCALE = A_DH ** -0.5, C_DH ** -0.5
BR = 512 // P

PX, PY = 0, 1
PQA = 2
PN1 = 6
PQB = 10
PCQ, PCKV = 12, 14
PN2 = 15
PG = [19, 35, 54]
PM = [23, 39, 58]
PO = [31, 50, 66]
PUKV, PUQ = 47, 48
PW = 70
PIECES = 78
RAW, HL = 3, 3


def outputs_of(p):
    if PN1 <= p < PN1 + 4 or PN2 <= p < PN2 + 4:
        return 0
    if any(o <= p < o + 4 for o in PO):
        return 2
    return {PUKV: 8, PUQ: 3, PUQ + 1: 3}.get(p, 1)


def first_output(p):
    return sum(outputs_of(q) for q in range(p))


def signals_before(p):
    return sum(max(outputs_of(q), 1) for q in range(p))


def make_schedule():
    todo = [("split_x", 0)]

    def piece(*ps):
        for p in ps:
            for q in range(4):
                todo.append(("quarter", 4 * p + q))

    def step(*names):
        for name, i in names:
            todo.append((name, i))

    piece(PX, PY)
    step(("rms", 0))
    piece(PQA)
    step(("rstd_nat", 0))
    piece(PQA + 1, PQA + 2)
    step(("gla_gate", 0))
    piece(PQA + 3)
    step(("gla_gate", 1))
    piece(PN1, PN1 + 1)
    step(("gla_decay", 0))
    piece(PN1 + 2)
    step(("gla_decay", 1), ("gla_end", 0))
    piece(PN1 + 3, PQB, PQB + 1, PCQ, PCQ + 1, PCKV, PN2)
    step(("latent", 0))
    piece(PN2 + 1)
    step(("latent", 1))
    piece(PN2 + 2, PN2 + 3)
    g, m = PG[0], PM[0]
    piece(g)
    step(("gla_state", 0), ("gla_state", 1))
    piece(g + 1)
    step(("silu", 0), ("gla_state", 2), ("gla_state", 3))
    piece(g + 2)
    step(("silu", 1))
    piece(g + 3)
    step(("silu", 2), ("gla_read", 0), ("gla_read", 1), ("gla_read", 2), ("gla_read", 3))
    piece(m)
    step(("silu", 3))
    for h in range(B_HEADS):
        step(("gla_norm", h))
        piece(m + 1 + h)
    piece(m + 5, m + 6, m + 7)
    fill = [4 * p + q for p in [*range(PO[0], PO[0] + 4), *range(PG[1], PG[1] + 12)] for q in range(4)]
    silus = {4 * (PG[1] + n + 1) + 3: BR + n for n in range(BR)}

    def quarters(n):
        for _ in range(min(n, len(fill))):
            q = fill.pop(0)
            todo.append(("quarter", q))
            if q in silus:
                todo.append(("silu", silus[q]))

    na = TT * A_KV
    quarters(28)
    for s in range(na + 2):
        if s < na:
            todo.append(("score_a", s))
        quarters(1)
        if 1 <= s < na + 1:
            todo.append(("turn", s - 1))
        quarters(1)
        if s >= 2:
            todo.append(("value_a", s - 2))
            if s % A_KV == 1:
                quarters(1)
                todo.append(("turn_y", (s - 2) // A_KV))
        quarters(1)
    quarters(len(fill))
    piece(PUKV, PUQ, PUQ + 1, *range(PO[1], PO[1] + 4))
    fill = [4 * p + q for p in range(PG[2], PG[2] + 12) for q in range(4)]
    silus = {4 * (PG[2] + n + 1) + 3: 2 * BR + n for n in range(BR)}
    nc_ = TT * C_HEADS
    quarters(10)
    for i in range(nc_ + 2):
        if i < nc_:
            todo.append(("score_c", i))
        if 1 <= i < nc_ + 1:
            todo.append(("turn", na + i - 1))
        if i >= 2:
            todo.append(("value_c", i - 2))
        if i < nc_ // 2 or i % 3:
            quarters(1)
        if i >= 2 and (i - 2) % C_HEADS == C_HEADS - 1:
            quarters(1)
            todo.append(("turn_y", TT + (i - 2) // C_HEADS))
    quarters(len(fill))
    piece(*range(PO[2], PO[2] + 4), *range(PW, PW + KT))
    return todo


SCHEDULE = make_schedule()
AUX = [s for s in SCHEDULE if s[0] in ("rms", "rstd_nat", "gla_gate", "gla_decay", "gla_end", "latent",
                                       "gla_norm", "turn_y")]

G_X, G_BH, G_CQ, G_CKV, SINKS = 0, 8, 9, 11, 12
PARAMS = 20
ONES, IDENT, LATER, MEMBER = 0, 128, 256, 384
CONSTS = 386


class Signal:

    def __init__(self, ctx, nc, name, per_layer, before=0):
        self.sem = ctx.enter_context(nc.semaphore(name))
        self.per_layer, self.before = per_layer, before

    def at(self, layer, n):
        assert n > 0 or self.before > 0, "a wait on a register's value needs it above zero"
        return layer * self.per_layer + (self.before + max(n, 0))


def build_hybrid_trunk(nc, x_t, pieces, params, alpha, tables, consts, final_g, out_t, k_rope_dram, q_rope_dram):
    with ExitStack() as ctx:
        def sb(name, shape, dt=F32):
            return ctx.enter_context(nc.sbuf_tensor(name, shape, dt))

        def sig(name, per_layer, before=0):
            return Signal(ctx, nc, name, per_layer, before)

        xt = sb("xt", [P, KT, S])
        act_hi = sb("act_hi", [P, KT, S], F32R)
        act_lo = sb("act_lo", [P, KT, S], F32R)
        raw = sb("raw", [P, RAW, 1024])
        w_hi = sb("w_hi", [P, HL, 1024], F32R)
        w_lo = sb("w_lo", [P, HL, 1024], F32R)
        gates = sb("gates", [P, 12, S])
        merged = sb("merged", [P, KT, S])
        y_hi = sb("y_hi", [P, BR, S], F32R)
        y_lo = sb("y_lo", [P, BR, S], F32R)
        bank_g = sb("bank_g", [P, 4096])
        bank_a = sb("bank_a", [P, 6144])
        lat_hi = sb("lat_hi", [P, 3, S], F32R)
        lat_lo = sb("lat_lo", [P, 3, S], F32R)
        rope = sb("rope", [P, 4, S])
        rstd = sb("rstd", [P, S])
        work = sb("work", [P, 4, S])
        y_nat = sb("y_nat", [P, S])
        y_pre = sb("y_pre", [P, S])
        con = sb("con", [P, CONSTS])
        par_all = sb("par_all", [P, DEPTH, PARAMS])
        par = sb("par", [P, PARAMS])
        alpha_all = sb("alpha_all", [P, DEPTH, B_HEADS * B_DK])
        w_alpha = sb("w_alpha", [P, B_HEADS * B_DK])
        fin_g = sb("fin_g", [P, KT])
        eps = sb("eps", [P, 1])
        rstd_nat = sb("rstd_nat", [P, TT])
        decay = sb("decay", [P, 2 * NC])
        neg_sink = sb("neg_sink", [P, A_HEADS])
        top = sb("top", [P, 2, GROUP])
        neg_top = sb("neg_top", [P, 2, GROUP])
        sink_in = sb("sink_in", [P, 2, GROUP])
        sink_exp = sb("sink_exp", [P, 2, A_HEADS])
        sums = sb("sums", [P, 2, A_HEADS])
        recip = sb("recip", [P, A_HEADS])

        ones, ident = con[:, ONES:ONES + P], con[:, IDENT:IDENT + P]
        later, member = con[:, LATER:LATER + P], con[:, MEMBER:MEMBER + 2]
        prob = [work[:, 0, :], work[:, 1, :]]
        prob_t = [work[:, 2, :], work[:, 3, :]]
        k_dec = bank_g[:, 0:1024].rearrange("p (t n) -> p t n", t=TT)
        v_b = bank_g[:, 1024:3072].rearrange("p (t n) -> p t n", t=TT)
        q_b = bank_g[:, 3072:4096].rearrange("p (t n) -> p t n", t=2)
        k_c = bank_g[:, :].rearrange("p (h n) -> p h n", h=C_HEADS)
        q_a = bank_a[0:64, 0:4096].rearrange("p (h n) -> p h n", h=A_HEADS)
        k_a = bank_a[0:64, 4096:5120].rearrange("p (t n) -> p t n", t=2)
        v_a = bank_a[:, 5120:5632].rearrange("p (t n) -> p t n", t=TT)
        v_as = bank_a[:, 5632:6144].rearrange("p (t n) -> p t n", t=TT)
        q_c = bank_a[:, 0:4096].rearrange("p (h n) -> p h n", h=C_HEADS)
        v_c = bank_a[:, 4096:6144].rearrange("p (t n) -> p t n", t=TT)
        sq = [merged[:, 0, :], merged[:, 1, :]]
        sq_sum, ln_ms, ab1, second = merged[:, 2, :], merged[:, 3, :], merged[:, 4, :], merged[:, 5, :]
        lat_rstd = merged[:, 6, :]
        state = merged[:, 0:4, :].rearrange("p a (c j v) -> p (a c) j v", c=2, j=2)
        o_sq = [merged[:, 4, :], merged[:, 5, :]]
        o_ln, o_rstd = merged[:, 6, :], merged[:, 7, :]
        cos_r, sin_r = gates[:, 0, :], gates[:, 1, :]
        latent = gates[:, 2:5, :]
        dec = gates[:, 6:8, :].rearrange("p a (t n) -> p (a t) n", t=2)
        soft = gates[:, 8:10, :].rearrange("p a (t n) -> p (a t) n", t=2)
        log_a = gates[:, 10:12, :].rearrange("p a (t n) -> p (a t) n", t=2)

        ring = [ctx.enter_context(nc.psum_tensor(f"ring{i}", [P, S], F32)) for i in range(3)]
        nat = [ctx.enter_context(nc.psum_tensor(f"nat{i}", [P, S], F32)) for i in range(4)]
        aux = ctx.enter_context(nc.psum_tensor("aux", [P, S], F32))
        turn_bank, o_bank = nat[2], nat[3]

        raw_loaded = [sig(f"raw_loaded{i}", 16 * PIECES // RAW) for i in range(RAW)]
        setup_loaded = sig("setup_loaded", 0)
        eps_set = sig("eps_set", 0)
        hi_split, lo_split = sig("hi_split", PIECES), sig("lo_split", PIECES)
        proj_done = sig("proj_done", signals_before(PIECES), 1)
        proj_free = sig("proj_free", first_output(PIECES), 1)
        par_set = sig("par_set", 2)
        x_hi, x_lo, x_sq, x_acc = sig("x_hi", KT), sig("x_lo", KT), sig("x_sq", KT), sig("x_acc", KT)
        aux_ready, aux_free = sig("aux_ready", len(AUX)), sig("aux_free", len(AUX), 1)
        n_norms = 3 + B_HEADS
        log_set, rough_set, newton = sig("log_set", n_norms), sig("rough_set", n_norms), sig("newton", 2 * n_norms)
        rstd_set = sig("rstd_set", 1)
        ones_row = sig("ones_row", 1)
        rope_scaled = sig("rope_scaled", 2)
        rope_prod, rope_out = sig("rope_prod", 14), sig("rope_out", 24)
        halves_out = sig("halves_out", 1)
        k_rope_saved, k_rope_placed = sig("k_rope_saved", 32), sig("k_rope_placed", 16)
        q_rope_saved, q_rope_placed = sig("q_rope_saved", 32), sig("q_rope_placed", 32)
        gla_soft = sig("gla_soft", 6)
        nat_free = sig("nat_free", 8)
        v_cleared, v_shifted = sig("v_cleared", 1), sig("v_shifted", 32)
        lat_sq, lat_acc, lat_rs = sig("lat_sq", 3), sig("lat_acc", 1), sig("lat_rs", 2)
        lat_norm, lat_hi_set, lat_lo_set = sig("lat_norm", 3), sig("lat_hi_set", 3), sig("lat_lo_set", 3)
        state_in, state_set = sig("state_in", 4), sig("state_set", 2 * NC)
        read_done, read_sq, read_rs = sig("read_done", B_HEADS), sig("read_sq", B_HEADS), sig("read_rs", B_HEADS)
        read_norm = sig("read_norm", B_HEADS)
        y_pre_set, y_hi_set, y_lo_set = sig("y_pre_set", 12), sig("y_hi_set", 12), sig("y_lo_set", 12)
        gate_tanh, silu_set = sig("gate_tanh", 36), sig("silu_set", 12)
        n_steps = TT * A_KV + TT * C_HEADS
        scores_done = sig("scores_done", n_steps)
        masked = sig("masked", A_KV + TT * C_HEADS)
        top_set = sig("top_set", 2 * TT * A_KV + TT * C_HEADS)
        neg_top_set, exp_done = sig("neg_top_set", n_steps), sig("exp_done", n_steps)
        turn_done, turn_out, value_done = (sig("turn_done", n_steps), sig("turn_out", n_steps),
                                           sig("value_done", n_steps))
        denom_set, y_nat_set = sig("denom_set", 2 * TT + TT), sig("y_nat_set", 2 * TT, 1)
        sink_neg = sig("sink_neg", 1)
        merged_set = sig("merged_set", 2 * KT)
        merge_hi, merge_lo = sig("merge_hi", KT), sig("merge_lo", KT)
        out_scaled, out_sent = sig("out_scaled", 0), sig("out_sent", 0)

        def gate_index(p):
            for b in range(3):
                if PG[b] <= p < PG[b] + 4:
                    return b, p - PG[b]
                if PM[b] <= p < PM[b] + 8:
                    return b, 4 + p - PM[b]
            return None

        def attention_of(step):
            if step < TT * A_KV:
                return "a", step // A_KV, step % A_KV, step // A_KV
            c = step - TT * A_KV
            return "c", c // C_HEADS, c % C_HEADS, TT + c // C_HEADS

        block = ctx.enter_context(nc.Block())

        @block.sync
        def _(sp):
            for i in range(RAW):
                sp.dma_start(raw[:, i, :], pieces[i]).then_inc(raw_loaded[i].sem, 16)
            with sp.Fori(1, DEPTH * PIECES // RAW) as group:
                for i in range(RAW):
                    sp.wait_ge(lo_split.sem, group * RAW + (i - RAW + 1))
                    sp.dma_start(raw[:, i, :], pieces[group * RAW + i]).then_inc(raw_loaded[i].sem, 16)
            for j in range(KT):
                sp.wait_ge(out_scaled.sem, j + 1)
                sp.dma_start(out_t[:, j, :], gates[:, j, :]).then_inc(out_sent.sem, 16)
            sp.wait_ge(out_sent.sem, 16 * KT)

        @block.gpsimd
        def _(pool):
            with pool.Fori(0, DEPTH * PIECES // RAW) as group:
                for i in range(RAW):
                    pool.wait_ge(hi_split.sem, group * RAW + (i + 1))
                    nc.gpsimd.tensor_tensor(w_lo[:, i, :], raw[:, i, :], w_hi[:, i, :].bitcast(F32),
                                            ALU.subtract).then_inc(lo_split.sem, 1)

        @block.tensor
        def _(pe):
            def project(layer, quarter):
                p, part = divmod(quarter, 4)
                slot = p % HL
                whi, wlo = w_hi[:, slot, :], w_lo[:, slot, :]
                if part == 0:
                    pe.wait_ge(lo_split.sem, lo_split.at(layer, p + 1))
                natural = PN1 <= p < PN1 + 4 or PN2 <= p < PN2 + 4
                n_out = outputs_of(p)
                if natural:
                    first, n_k, width = (PN1, 2, 384) if p < PQB else (PN2, 2, 512)
                    jobs = [(t, 2 * (p - first) + k, k) for k in range(2) for t in range(TT)]
                elif p == PUKV:
                    jobs = [(o, 0, 0) for o in range(8)]
                elif p in (PUQ, PUQ + 1):
                    jobs = [(o, k, k) for o in range(3) for k in range(2)]
                elif n_out == 2:
                    jobs = [(o, k, k) for o in range(2) for k in range(BR)]
                else:
                    jobs = [(0, k, k) for k in range(KT)]
                lo, hi = len(jobs) * part // 4, len(jobs) * (part + 1) // 4
                for n in range(lo, hi):
                    o, k, kw = jobs[n]
                    if natural:
                        bank = nat[o]
                        start, stop = k == 0, k == KT - 1
                        if start:
                            if first == PN2:
                                pe.wait_ge(nat_free.sem, nat_free.at(layer, o + 1))
                            elif o == 0:
                                pe.wait_ge(y_nat_set.sem, y_nat_set.at(layer, 0))
                        dst = bank[:, 0:width]
                        wv = slice(kw * width, (kw + 1) * width)
                        ops = [(act_hi[:, k, o * P:(o + 1) * P], whi[:, wv]),
                               (act_lo[:, k, o * P:(o + 1) * P], whi[:, wv]),
                               (act_hi[:, k, o * P:(o + 1) * P], wlo[:, wv])]
                        done = n == len(jobs) - 1
                    else:
                        r = first_output(p) + o
                        dst = ring[r % 3][:, :]
                        last_k = {PUKV: 0, PUQ: 1, PUQ + 1: 1}.get(p, BR - 1 if n_out == 2 else KT - 1)
                        start, stop = k == 0, k == last_k
                        done = stop
                        if start:
                            pe.wait_ge(proj_free.sem, proj_free.at(layer, r - 2))
                        if p == PUKV and o < 4:
                            ts = slice(o * P, (o + 1) * P)
                            wv = slice(512, 1024)
                            ops = [(lat_hi[:, 2, ts], whi[:, wv]), (lat_lo[:, 2, ts], whi[:, wv]),
                                   (lat_hi[:, 2, ts], wlo[:, wv])]
                        else:
                            if p == PUKV:
                                xh, xl, col = lat_hi[:, 2, :], lat_lo[:, 2, :], (o - 4) * P
                            elif p in (PUQ, PUQ + 1):
                                xh, xl, col = lat_hi[:, k, :], lat_lo[:, k, :], (k * 3 + o) * P
                            elif n_out == 2:
                                xh, xl, col = y_hi[:, k, :], y_lo[:, k, :], (k * 2 + o) * P
                            else:
                                xh, xl, col = act_hi[:, k, :], act_lo[:, k, :], k * P
                            wv = slice(col, col + P)
                            ops = [(whi[:, wv], xh), (whi[:, wv], xl), (wlo[:, wv], xh)]
                    if p == PX:
                        pe.wait_ge(x_lo.sem, x_lo.at(layer, k + 1))
                    elif p == PW:
                        pe.wait_ge(merge_lo.sem, merge_lo.at(layer, k + 1))
                    elif p == PUKV and n == 0:
                        pe.wait_ge(lat_lo_set.sem, lat_lo_set.at(layer, 3))
                    elif p in PO and n == 0:
                        pe.wait_ge(y_lo_set.sem, y_lo_set.at(layer, BR * (PO.index(p) + 1)))
                    for i, (stationary, moving) in enumerate(ops):
                        mm = pe.matmul(dst, stationary, moving, start=start and i == 0, stop=stop and i == 2)
                    if done:
                        mm.then_inc(proj_done.sem, 1)

            def aux_bank(layer, u):
                pe.wait_ge(aux_free.sem, aux_free.at(layer, u))

            pe.wait_ge(setup_loaded.sem, 16 * 7)
            pe.sem_inc(proj_done.sem, 1)
            with pe.Fori(0, DEPTH) as layer:
                u = 0
                for name, i in SCHEDULE:
                    if name == "quarter":
                        project(layer, i)
                        continue
                    if (name, i) == ("rms", 0):
                        aux_bank(layer, u)
                        pe.wait_ge(x_acc.sem, x_acc.at(layer, KT))
                        mm = pe.matmul(aux[:, :], ones, sq_sum, start=True, stop=True)
                    elif name == "rstd_nat":
                        aux_bank(layer, u)
                        pe.wait_ge(rstd_set.sem, rstd_set.at(layer, 1))
                        for t in range(TT):
                            mm = pe.transpose(aux[:, t * P:(t + 1) * P], rstd[:, t * P:(t + 1) * P], ident)
                    elif name == "gla_gate":
                        aux_bank(layer, u)
                        pe.wait_ge(halves_out.sem, halves_out.at(layer, 1))
                        for t in range(2):
                            ts = slice((2 * i + t) * P, (2 * i + t + 1) * P)
                            mm = pe.matmul(aux[:, t * 256:(t + 1) * 256], ab1[96:96 + B_RANK + 1, ts],
                                           w_alpha[96:96 + B_RANK + 1, :], start=True, stop=True)
                    elif name == "gla_decay":
                        aux_bank(layer, u)
                        for t in range(2):
                            mm = pe.matmul(aux[:, t * 256:(t + 1) * 256], later, log_a[:, 2 * i + t, :],
                                           start=True, stop=True)
                    elif name == "gla_end":
                        aux_bank(layer, u)
                        for j in range(2):
                            for t in range(TT):
                                mm = pe.matmul(aux[:, j * NC + 2 * t:j * NC + 2 * t + 2],
                                               log_a[:, t, j * P:(j + 1) * P], member, start=True, stop=True)
                    elif name == "latent":
                        aux_bank(layer, u)
                        if i == 0:
                            pe.wait_ge(lat_acc.sem, lat_acc.at(layer, 1))
                        else:
                            pe.wait_ge(lat_sq.sem, lat_sq.at(layer, 3))
                        mm = pe.matmul(aux[:, :], ones, sq_sum if i == 0 else sq[0], start=True, stop=True)
                    elif name == "gla_state":
                        ready, n = (nat_free, 8) if i < 2 else (state_set, 4 * (i - 1))
                        value = pe.snap(ready.at(layer, n))
                        pe.lower_val(value)
                        pe.wait_ge(setup_loaded.sem, 16 * 7)
                        pe.wait_ge(ready.sem, value)
                        bank = nat[i % 2]
                        for c in range(2):
                            rows = slice(CHUNK * c, CHUNK * (c + 1))
                            bank = nat[2 * (i % 2) + c]
                            for h in range(B_HEADS):
                                half = slice(64 * (h % 2), 64 * (h % 2) + 64)
                                col = (h // 2) * P
                                mm = pe.matmul(bank[half, col:col + P], k_dec[rows, i, h * B_DK:(h + 1) * B_DK],
                                               v_b[rows, i, h * B_DV:(h + 1) * B_DV], start=True, stop=True)
                        mm.then_inc(state_in.sem, 1)
                    elif name == "gla_read":
                        if i == 0:
                            pe.wait_ge(state_set.sem, state_set.at(layer, 2 * NC))
                        half = slice(64 * (i % 2), 64 * (i % 2) + 64)
                        for c in range(NC):
                            cs = slice(CHUNK * c, CHUNK * (c + 1))
                            mm = pe.matmul(nat[i][:, cs], state[half, c, i // 2, :], q_b[half, i // 2, cs],
                                           start=True, stop=True)
                        mm.then_inc(read_done.sem, 1)
                    elif name == "gla_norm":
                        aux_bank(layer, u)
                        pe.wait_ge(read_sq.sem, read_sq.at(layer, i + 1))
                        mm = pe.matmul(aux[:, :], ones, o_sq[i % 2], start=True, stop=True)
                    elif name == "score_a":
                        qt, g = divmod(i, A_KV)
                        ready, n = (read_norm, B_HEADS) if i < 2 else (exp_done, i - 1)
                        value = pe.snap(ready.at(layer, n))
                        pe.lower_val(value)
                        pe.wait_ge(setup_loaded.sem, 16 * 7)
                        pe.wait_ge(ready.sem, value)
                        bank = nat[i % 2]
                        for hh in range(GROUP):
                            h = g * GROUP + hh
                            for c in range(2):
                                q0 = qt * P + c * CHUNK
                                k0, skip = (q0 - CHUNK, 0) if q0 else (0, CHUNK)
                                mm = pe.matmul(bank[c * 64:c * 64 + 64, hh * P + skip:(hh + 1) * P],
                                               q_a[:, h, q0:q0 + CHUNK],
                                               k_a[:, g, k0:q0 + CHUNK], start=True, stop=True)
                        mm.then_inc(scores_done.sem, 1)
                    elif name == "score_c":
                        qt, h = divmod(i, C_HEADS)
                        step, n = TT * A_KV + i, (qt + 1) * P
                        pe.wait_ge(exp_done.sem, exp_done.at(layer, step - 1))
                        if i == 0:
                            pe.wait_ge(proj_free.sem, proj_free.at(layer, first_output(PUQ + 2)))
                            pe.wait_ge(k_rope_placed.sem, k_rope_placed.at(layer, 16))
                            pe.wait_ge(q_rope_placed.sem, q_rope_placed.at(layer, 32))
                        mm = pe.matmul(nat[i % 2][:, 0:n], q_c[0:C_DH, h, qt * P:(qt + 1) * P],
                                       k_c[0:C_DH, h, 0:n], start=True, stop=True)
                        mm.then_inc(scores_done.sem, 1)
                    elif name == "turn":
                        kind, qt, h, _ = attention_of(i)
                        pe.wait_ge(exp_done.sem, exp_done.at(layer, i + 1))
                        if i > 0:
                            pe.wait_ge(turn_out.sem, turn_out.at(layer, i))
                        for b in range(GROUP if kind == "a" else qt + 1):
                            mm = pe.transpose(turn_bank[:, b * P:(b + 1) * P], prob[i % 2][:, b * P:(b + 1) * P], ident)
                        mm.then_inc(turn_done.sem, 1)
                    elif name in ("value_a", "value_c"):
                        step = i if name == "value_a" else TT * A_KV + i
                        kind, qt, h, q_all = attention_of(step)
                        if kind == "a" and step == 0:
                            pe.wait_ge(v_shifted.sem, v_shifted.at(layer, 32))
                        if h == 0 and q_all > 0:
                            pe.wait_ge(y_nat_set.sem, y_nat_set.at(layer, q_all))
                        pe.wait_ge(turn_out.sem, turn_out.at(layer, step + 1))
                        pt = prob_t[step % 2]
                        if kind == "a":
                            for hh in range(GROUP):
                                col = (h * GROUP + hh) * A_DH
                                for c in range(2):
                                    mm = pe.matmul(o_bank[c * 64:c * 64 + 64, col:col + A_DH],
                                                   pt[:, hh * P + c * 64:hh * P + c * 64 + 64],
                                                   (v_as, v_a)[c][:, qt, h * A_DH:(h + 1) * A_DH],
                                                   start=True, stop=True)
                        else:
                            for b in range(qt + 1):
                                mm = pe.matmul(o_bank[:, h * C_V:(h + 1) * C_V], pt[:, b * P:(b + 1) * P],
                                               v_c[:, b, h * C_V:(h + 1) * C_V], start=b == 0, stop=b == qt)
                        mm.then_inc(value_done.sem, 1)
                    elif name == "turn_y":
                        aux_bank(layer, u)
                        pe.wait_ge(y_nat_set.sem, y_nat_set.at(layer, i + 1))
                        for f in range(BR):
                            mm = pe.transpose(aux[:, f * P:(f + 1) * P], y_nat[:, f * P:(f + 1) * P], ident)
                    if (name, i) in AUX:
                        mm.then_inc(aux_ready.sem, 1)
                        u += 1
            pe.wait_ge(x_acc.sem, x_acc.at(DEPTH, KT))
            pe.wait_ge(aux_free.sem, aux_free.at(DEPTH, 0))
            pe.matmul(aux[:, :], ones, sq_sum, start=True, stop=True).then_inc(aux_ready.sem, 1)

        @block.scalar
        def _(act):
            def split_hi(layer, p):
                i = p % RAW
                act.wait_ge(raw_loaded[i].sem, raw_loaded[i].at(layer, 16 * (p // RAW + 1)))
                act.wait_ge(proj_done.sem, proj_done.at(layer, signals_before(p - HL + 1) if p >= HL else 0))
                nc.scalar.activation(w_hi[:, p % HL, :], raw[:, i, :], ACT.Copy).then_inc(hi_split.sem, 1)

            def rms_of(layer, u, place, dst, n, tmp):
                act.wait_ge(aux_ready.sem, aux_ready.at(layer, u + 1))
                nc.scalar.activation(tmp, aux[:, :], ACT.Ln, scale=1.0 / n, bias=eps[:, 0:1]).then_inc(log_set.sem, 1)
                act.wait_ge(log_set.sem, log_set.at(layer, place + 1))
                nc.scalar.activation(dst, tmp, ACT.Exp, scale=-0.5).then_inc(rough_set.sem, 1)

            def squares(layer):
                for j in range(KT):
                    if j >= 2:
                        act.wait_ge(x_acc.sem, x_acc.at(layer, j - 1))
                    nc.scalar.activation(sq[j % 2], xt[:, j, :], ACT.Square).then_inc(x_sq.sem, 1)

            act.dma_start(par_all[:, :, :], params).then_inc(setup_loaded.sem, 16)
            for j in range(2):
                half = slice(j * KT // 2, (j + 1) * KT // 2)
                act.dma_start(xt[:, half, :], x_t[:, half, :]).then_inc(setup_loaded.sem, 16)
            act.dma_start(con[:, :], consts).then_inc(setup_loaded.sem, 16)
            act.dma_start(alpha_all[96:96 + B_RANK + 1, :, :], alpha).then_inc(setup_loaded.sem, 16)
            act.dma_start(rope[:, :, :], tables).then_inc(setup_loaded.sem, 16)
            act.dma_start(fin_g[:, :], final_g).then_inc(setup_loaded.sem, 16)
            act.wait_ge(eps_set.sem, 1)
            act.wait_ge(setup_loaded.sem, 16 * 7)
            with act.Fori(0, DEPTH) as layer:
                u = 0
                for name, i in SCHEDULE:
                    if name == "split_x":
                        act.wait_ge(proj_free.sem, proj_free.at(layer, 0))
                        nc.scalar.activation(par[:, :], par_all[:, bass.ds(layer, 1), :].rearrange("p a n -> p (a n)"),
                                             ACT.Copy).then_inc(par_set.sem, 1)
                        nc.scalar.activation(w_alpha[96:96 + B_RANK + 1, :],
                                             alpha_all[96:96 + B_RANK + 1, bass.ds(layer, 1), :].rearrange(
                                                 "p a n -> p (a n)"), ACT.Copy).then_inc(par_set.sem, 1)
                        split_hi(layer, 0)
                        act.wait_ge(par_set.sem, par_set.at(layer, 1))
                        for j in range(KT):
                            nc.scalar.activation(act_hi[:, j, :], xt[:, j, :], ACT.Copy,
                                                 scale=par[:, G_X + j:G_X + j + 1]).then_inc(x_hi.sem, 1)
                            if j < HL - 1:
                                split_hi(layer, j + 1)
                        squares(layer)
                    elif name == "quarter" and i % 4 == 3:
                        p = i // 4
                        if p + HL < PIECES:
                            split_hi(layer, p + HL)
                        g = gate_index(p)
                        if g is not None:
                            b, j = g
                            act.wait_ge(proj_free.sem, proj_free.at(layer, first_output(p) + 1))
                            nc.scalar.activation(gates[:, j if j >= 4 else 8 + j, :], gates[:, j, :],
                                                 ACT.Tanh).then_inc(gate_tanh.sem, 1)
                        if p in (PCQ, PCQ + 1, PCKV):
                            n = p - PCQ
                            act.wait_ge(proj_free.sem, proj_free.at(layer, first_output(p) + 1))
                            if n == 2:
                                act.wait_ge(lat_acc.sem, lat_acc.at(layer, 1))
                            elif n == 0:
                                act.wait_ge(x_acc.sem, x_acc.at(layer, KT))
                            nc.scalar.activation(sq[n % 2], latent[:, n, :], ACT.Square).then_inc(lat_sq.sem, 1)
                        if p >= PO[2] and p < PO[2] + 4:
                            for o in range(2):
                                j = 2 * (p - PO[2]) + o
                                act.wait_ge(merged_set.sem, merged_set.at(layer, KT + j + 1))
                                nc.scalar.activation(act_hi[:, j, :], merged[:, j, :], ACT.Copy,
                                                     scale=0.5).then_inc(merge_hi.sem, 1)
                        if p == PUKV:
                            act.wait_ge(k_rope_saved.sem, k_rope_saved.at(layer, 32))
                            act.wait_ge(read_done.sem, read_done.at(layer, B_HEADS))
                            act.dma_start(k_c[C_NOPE:C_DH, :, :],
                                          k_rope_dram.unsqueeze(1).broadcast_to([C_ROPE, C_HEADS, S])
                                          ).then_inc(k_rope_placed.sem, 16)
                        if p == PUQ:
                            act.wait_ge(rope_out.sem, rope_out.at(layer, 24))
                            for half in range(2):
                                act.dma_start(q_rope_dram[half], work[:, 2 * half, :]).then_inc(q_rope_saved.sem, 16)
                            act.wait_ge(q_rope_saved.sem, q_rope_saved.at(layer, 32))
                            for half in range(2):
                                rows = slice(C_NOPE + 16 * half, C_NOPE + 16 * half + 16)
                                act.dma_start(q_c[rows, :, :], q_rope_dram[half].rearrange("(h r) n -> r h n", h=C_HEADS)
                                              ).then_inc(q_rope_placed.sem, 16)
                        if p == PQA:
                            act.wait_ge(rope_out.sem, rope_out.at(layer, 6))
                            act.dma_start(k_rope_dram[0:16, :], second[64:80, :]).then_inc(k_rope_saved.sem, 16)
                            act.dma_start(k_rope_dram[16:32, :], work[64:80, 0, :]).then_inc(k_rope_saved.sem, 16)
                        if p == PN1 + 3:
                            act.wait_ge(nat_free.sem, nat_free.at(layer, 4))
                            act.wait_ge(v_cleared.sem, v_cleared.at(layer, 1))
                            act.dma_start(v_as[0:64, 1:TT, :], v_a[64:128, 0:TT - 1, :]).then_inc(v_shifted.sem, 16)
                            act.dma_start(v_as[64:128, :, :], v_a[0:64, :, :]).then_inc(v_shifted.sem, 16)
                    elif name == "rms":
                        rms_of(layer, u, 0, rstd[:, :], D, ln_ms)
                    elif name == "gla_gate":
                        act.wait_ge(aux_ready.sem, aux_ready.at(layer, u + 1))
                        tile = soft[:, 2 * i:2 * i + 2, :].rearrange("p t n -> p (t n)")
                        nc.scalar.activation(tile, aux[:, :], ACT.Abs).then_inc(gla_soft.sem, 1)
                        act.wait_ge(gla_soft.sem, gla_soft.at(layer, 3 * i + 1))
                        nc.scalar.activation(tile, tile, ACT.Exp, scale=-1.0).then_inc(gla_soft.sem, 1)
                        act.wait_ge(gla_soft.sem, gla_soft.at(layer, 3 * i + 2))
                        nc.scalar.activation(tile, tile, ACT.Ln, bias=1.0).then_inc(gla_soft.sem, 1)
                    elif name == "gla_decay":
                        act.wait_ge(aux_ready.sem, aux_ready.at(layer, u + 1))
                        nc.scalar.activation(dec[:, 2 * i:2 * i + 2, :].rearrange("p t n -> p (t n)"), aux[:, :],
                                             ACT.Exp).then_inc(aux_free.sem, 1)
                    elif name == "gla_end":
                        act.wait_ge(aux_ready.sem, aux_ready.at(layer, u + 1))
                        nc.scalar.activation(decay[:, :], aux[:, 0:2 * NC], ACT.Exp).then_inc(aux_free.sem, 1)
                    elif name == "latent":
                        if i == 1:
                            act.wait_ge(lat_norm.sem, lat_norm.at(layer, 2))
                        rms_of(layer, u, 1 + i, lat_rstd, (C_QR, C_KVR)[i], ln_ms)
                        for n in ((0, 1), (2,))[i]:
                            act.wait_ge(lat_norm.sem, lat_norm.at(layer, n + 1))
                            nc.scalar.activation(lat_hi[:, n, :], latent[:, n, :], ACT.Copy).then_inc(lat_hi_set.sem, 1)
                    elif name == "gla_read":
                        act.wait_ge(read_done.sem, read_done.at(layer, i + 1))
                        if i >= 2:
                            continue
                        nc.scalar.activation(o_sq[i % 2], nat[i][:, :], ACT.Square).then_inc(read_sq.sem, 1)
                    elif name == "gla_norm":
                        if i > 0:
                            act.wait_ge(read_norm.sem, read_norm.at(layer, i))
                        rms_of(layer, u, 3 + i, o_rstd, B_DV, o_ln)
                        if i + 2 < B_HEADS:
                            nc.scalar.activation(o_sq[i % 2], nat[i + 2][:, :], ACT.Square).then_inc(read_sq.sem, 1)
                        act.wait_ge(y_pre_set.sem, y_pre_set.at(layer, i + 1))
                        nc.scalar.activation(y_hi[:, i, :], work[:, 2 + i % 2, :], ACT.Copy).then_inc(y_hi_set.sem, 1)
                    elif name in ("score_a", "score_c"):
                        step = i if name == "score_a" else TT * A_KV + i
                        kind, qt, h, q_all = attention_of(step)
                        act.wait_ge(neg_top_set.sem, neg_top_set.at(layer, step + 1))
                        if step >= 2:
                            act.wait_ge(turn_done.sem, turn_done.at(layer, step - 1))
                        if kind == "a":
                            for hh in range(GROUP):
                                nc.scalar.activation(prob[step % 2][:, hh * P:(hh + 1) * P],
                                                     nat[i % 2][:, hh * P:(hh + 1) * P], ACT.Exp, scale=A_SCALE,
                                                     bias=neg_top[:, step % 2, hh:hh + 1],
                                                     accum_out=sums[:, qt % 2, h * GROUP + hh:h * GROUP + hh + 1])
                            nc.scalar.activation(sink_exp[:, qt % 2, h * GROUP:(h + 1) * GROUP], sink_in[:, step % 2, :],
                                                 ACT.Exp).then_inc(exp_done.sem, 1)
                        else:
                            n = (qt + 1) * P
                            nc.scalar.activation(prob[step % 2][:, 0:n], nat[i % 2][:, 0:n], ACT.Exp, scale=C_SCALE,
                                                 bias=neg_top[:, step % 2, 0:1],
                                                 accum_out=sums[:, qt % 2, h:h + 1]).then_inc(exp_done.sem, 1)
                    elif name == "turn":
                        kind, qt, _, _ = attention_of(i)
                        n = (GROUP if kind == "a" else qt + 1) * P
                        act.wait_ge(turn_done.sem, turn_done.at(layer, i + 1))
                        if i >= 2:
                            act.wait_ge(value_done.sem, value_done.at(layer, i - 1))
                        nc.scalar.activation(prob_t[i % 2][:, 0:n], turn_bank[:, 0:n],
                                             ACT.Copy).then_inc(turn_out.sem, 1)
                    elif name == "turn_y":
                        act.wait_ge(y_pre_set.sem, y_pre_set.at(layer, BR + i + 1))
                        if i % TT == 0:
                            act.wait_ge(proj_done.sem, proj_done.at(layer, signals_before(PO[i // TT] + 4)))
                        ts = slice((i % TT) * P, (i % TT + 1) * P)
                        nc.scalar.activation(y_hi[:, :, ts], y_pre[:, :].rearrange("p (f n) -> p f n", f=BR),
                                             ACT.Copy).then_inc(y_hi_set.sem, 1)
                    if (name, i) in AUX:
                        u += 1
            act.wait_ge(proj_free.sem, proj_free.at(DEPTH, 0))
            squares(DEPTH)
            rms_of(DEPTH, 0, 0, rstd[:, :], D, ln_ms)

        @block.vector
        def _(dve):
            def add_squares(layer):
                for j in range(KT):
                    dve.wait_ge(x_sq.sem, x_sq.at(layer, j + 1))
                    if j == 0:
                        nc.vector.tensor_copy(sq_sum, sq[0]).then_inc(x_acc.sem, 1)
                    else:
                        dve.wait_ge(x_acc.sem, x_acc.at(layer, j))
                        nc.vector.tensor_tensor(sq_sum, sq_sum, sq[j % 2], ALU.add).then_inc(x_acc.sem, 1)

            def refine(layer, u, place, y, n):
                dve.wait_ge(rough_set.sem, rough_set.at(layer, place + 1))
                nc.vector.tensor_tensor(y_nat[:, :], y, y, ALU.mult).then_inc(newton.sem, 1)
                dve.wait_ge(newton.sem, newton.at(layer, 2 * place + 1))
                nc.vector.scalar_tensor_tensor(y_nat[:, :], aux[:, :], n * EPS, y_nat[:, :], ALU.add,
                                               ALU.mult).then_inc(aux_free.sem, 1)
                dve.wait_ge(aux_free.sem, aux_free.at(layer, u + 1))
                nc.vector.tensor_scalar(y_nat[:, :], y_nat[:, :], -0.5 / n, 1.5, ALU.mult,
                                        ALU.add).then_inc(newton.sem, 1)
                dve.wait_ge(newton.sem, newton.at(layer, 2 * place + 2))
                return nc.vector.tensor_tensor(y, y_nat[:, :], y, ALU.mult)

            def rotary_products(layer, before, first, second_half, cos, sin, rows, last_reader=None):
                if before:
                    dve.wait_ge(rope_out.sem, rope_out.at(layer, before))
                ops = [(0, first, cos), (1, second_half, sin), (2, second_half, cos), (3, first, sin)]
                for n, (slot, half, table) in enumerate(ops):
                    last = nc.vector.tensor_tensor(work[rows, slot, :], half, table, ALU.mult)
                    last.then_inc(rope_prod.sem, 1)

            def evacuated(layer, p, n=1):
                dve.wait_ge(proj_done.sem, proj_done.at(layer, signals_before(p) + n))

            nc.vector.memset(eps[:, :], EPS).then_inc(eps_set.sem, 1)
            dve.wait_ge(setup_loaded.sem, 16 * 7)
            for free in (proj_free, aux_free, y_nat_set):
                dve.sem_inc(free.sem, 1)
            with dve.Fori(0, DEPTH) as layer:
                u = 0
                for name, i in SCHEDULE:
                    if name == "split_x":
                        for j in range(KT):
                            dve.wait_ge(x_hi.sem, x_hi.at(layer, j + 1))
                            nc.vector.scalar_tensor_tensor(act_lo[:, j, :], xt[:, j, :], par[:, G_X + j:G_X + j + 1],
                                                           act_hi[:, j, :].bitcast(F32), ALU.mult,
                                                           ALU.subtract).then_inc(x_lo.sem, 1)
                        add_squares(layer)
                        nc.vector.tensor_scalar(neg_sink[:, :], par[:, SINKS:SINKS + A_HEADS], -1.0, None,
                                                ALU.mult).then_inc(sink_neg.sem, 1)
                        nc.vector.memset(ab1[96:128, :], 1.0).then_inc(ones_row.sem, 1)
                        nc.vector.memset(v_as[0:64, 0, :], 0.0).then_inc(v_cleared.sem, 1)
                    elif name == "rms":
                        refine(layer, u, 0, rstd[:, :], D).then_inc(rstd_set.sem, 1)
                        dve.wait_ge(rstd_set.sem, rstd_set.at(layer, 1))
                        nc.vector.tensor_tensor(cos_r, rope[:, 0, :], rstd[:, :], ALU.mult).then_inc(rope_scaled.sem, 1)
                        nc.vector.tensor_tensor(sin_r, rope[:, 1, :], rstd[:, :], ALU.mult).then_inc(rope_scaled.sem, 1)
                        dve.wait_ge(rope_scaled.sem, rope_scaled.at(layer, 2))
                        evacuated(layer, PY)
                        rx, ry = ring[first_output(PX) % 3], ring[first_output(PY) % 3]
                        rotary_products(layer, 0, rx[0:64, :], ry[0:64, :], cos_r[0:64, :], sin_r[0:64, :], slice(0, 64))
                        dve.wait_ge(ones_row.sem, ones_row.at(layer, 1))
                        nc.vector.tensor_tensor(ab1[64:112, :], rx[64:112, :], rstd[64:112, :],
                                                ALU.mult).then_inc(proj_free.sem, 1)
                        nc.vector.tensor_tensor(second[64:80, :], ry[64:80, :], rstd[64:80, :],
                                                ALU.mult).then_inc(proj_free.sem, 1)
                        dve.wait_ge(proj_free.sem, proj_free.at(layer, 2))
                        for g in range(A_KV):
                            rows = slice(32 * g, 32 * g + 32)
                            nc.vector.tensor_tensor(k_a[0:32, g, :], work[rows, 0, :], work[rows, 1, :],
                                                    ALU.subtract).then_inc(rope_out.sem, 1)
                            nc.vector.tensor_tensor(k_a[32:64, g, :], work[rows, 2, :], work[rows, 3, :],
                                                    ALU.add).then_inc(rope_out.sem, 1)
                        rows = slice(64, 80)
                        rotary_products(layer, 4, ab1[rows, :], second[rows, :], rope[rows, 2, :], rope[rows, 3, :], rows)
                        dve.wait_ge(rope_prod.sem, rope_prod.at(layer, 8))
                        nc.vector.tensor_tensor(second[rows, :], work[rows, 0, :], work[rows, 1, :],
                                                ALU.subtract).then_inc(rope_out.sem, 1)
                        dve.wait_ge(rope_out.sem, rope_out.at(layer, 5))
                        nc.vector.tensor_tensor(work[rows, 0, :], work[rows, 2, :], work[rows, 3, :],
                                                ALU.add).then_inc(rope_out.sem, 1)
                        nc.vector.tensor_copy(neg_sink[:, 0:1], neg_sink[:, 0:1]).then_inc(halves_out.sem, 1)
                    elif name == "rstd_nat":
                        dve.wait_ge(aux_ready.sem, aux_ready.at(layer, u + 1))
                        nc.vector.tensor_copy(rstd_nat[:, :], aux[:, :].rearrange("p (t n) -> p t n", t=TT)[:, :, 0]
                                              ).then_inc(aux_free.sem, 1)
                    elif name == "gla_gate":
                        dve.wait_ge(gla_soft.sem, gla_soft.at(layer, 3 * i + 3))
                        nc.vector.scalar_tensor_tensor(
                            log_a[:, 2 * i:2 * i + 2, :].rearrange("p t n -> p (t n)"), aux[:, :], 0.0,
                            soft[:, 2 * i:2 * i + 2, :].rearrange("p t n -> p (t n)"), ALU.min,
                            ALU.subtract).then_inc(aux_free.sem, 1)
                    elif name == "latent":
                        refine(layer, u, 1 + i, lat_rstd, (C_QR, C_KVR)[i]).then_inc(lat_rs.sem, 1)
                        dve.wait_ge(lat_rs.sem, lat_rs.at(layer, i + 1))
                        for n in ((0, 1), (2,))[i]:
                            col = G_CQ + n
                            nc.vector.scalar_tensor_tensor(latent[:, n, :], latent[:, n, :], par[:, col:col + 1],
                                                           lat_rstd, ALU.mult, ALU.mult).then_inc(lat_norm.sem, 1)
                        for n in ((0, 1), (2,))[i]:
                            dve.wait_ge(lat_hi_set.sem, lat_hi_set.at(layer, n + 1))
                            nc.vector.tensor_tensor(lat_lo[:, n, :], latent[:, n, :], lat_hi[:, n, :].bitcast(F32),
                                                    ALU.subtract).then_inc(lat_lo_set.sem, 1)
                    elif name == "gla_state":
                        dve.wait_ge(state_in.sem, state_in.at(layer, i + 1))
                        if i == 0:
                            end = AUX.index(("gla_end", 0))
                            dve.wait_ge(aux_free.sem, aux_free.at(layer, end + 1))
                        for c in range(2 * i, 2 * i + 2):
                            for j in range(2):
                                new = nat[2 * (i % 2) + c % 2][:, j * P:(j + 1) * P]
                                if c == 0:
                                    nc.vector.tensor_copy(state[:, 0, j, :], new).then_inc(state_set.sem, 1)
                                else:
                                    dve.wait_ge(state_set.sem, state_set.at(layer, 2 * (c - 1) + j + 1))
                                    nc.vector.scalar_tensor_tensor(
                                        state[:, c, j, :], state[:, c - 1, j, :], decay[:, j * NC + c:j * NC + c + 1],
                                        new, ALU.mult, ALU.add).then_inc(state_set.sem, 1)
                    elif name == "silu":
                        b, j = divmod(i, BR)
                        dve.wait_ge(gate_tanh.sem, gate_tanh.at(layer, 12 * b + j + 1))
                        nc.vector.scalar_tensor_tensor(gates[:, j, :], gates[:, 8 + j, :], 1.0, gates[:, j, :], ALU.add,
                                                       ALU.mult).then_inc(silu_set.sem, 1)
                    elif name == "gla_norm":
                        refine(layer, u, 3 + i, o_rstd, B_DV).then_inc(read_rs.sem, 1)
                        dve.wait_ge(read_rs.sem, read_rs.at(layer, i + 1))
                        nc.vector.tensor_tensor(work[:, i % 2, :], nat[i][:, :], o_rstd, ALU.mult
                                                ).then_inc(read_norm.sem, 1)
                        dve.wait_ge(read_norm.sem, read_norm.at(layer, i + 1))
                        if i == 0:
                            dve.wait_ge(silu_set.sem, silu_set.at(layer, BR))
                        nc.vector.scalar_tensor_tensor(work[:, 2 + i % 2, :], work[:, i % 2, :], par[:, G_BH:G_BH + 1],
                                                       gates[:, i, :], ALU.mult, ALU.mult).then_inc(y_pre_set.sem, 1)
                        dve.wait_ge(y_hi_set.sem, y_hi_set.at(layer, i + 1))
                        nc.vector.tensor_tensor(y_lo[:, i, :], work[:, 2 + i % 2, :], y_hi[:, i, :].bitcast(F32),
                                                ALU.subtract).then_inc(y_lo_set.sem, 1)
                    elif name in ("score_a", "score_c"):
                        step = i if name == "score_a" else TT * A_KV + i
                        kind, qt, h, q_all = attention_of(step)
                        par2 = step % 2
                        bank = nat[i % 2]
                        dve.wait_ge(scores_done.sem, scores_done.at(layer, step + 1))
                        if kind == "a":
                            sc = bank[:, :].rearrange("p (h n) -> p h n", h=GROUP)
                            if qt == 0:
                                nc.vector.memset(sc[0:64, :, 0:64], NEG).then_inc(masked.sem, 1)
                                dve.wait_ge(masked.sem, masked.at(layer, step + 1))
                            nc.vector.tensor_reduce(top[:, par2, :], sc, AX_X, ALU.max,
                                                    negate=True).then_inc(top_set.sem, 1)
                            dve.wait_ge(top_set.sem, top_set.at(layer, 2 * step + 1))
                            heads = slice(h * GROUP, (h + 1) * GROUP)
                            nc.vector.scalar_tensor_tensor(neg_top[:, par2, :], top[:, par2, :], A_SCALE,
                                                           neg_sink[:, heads], ALU.mult,
                                                           ALU.min).then_inc(top_set.sem, 1)
                            dve.wait_ge(top_set.sem, top_set.at(layer, 2 * step + 2))
                            nc.vector.tensor_tensor(sink_in[:, par2, :], neg_top[:, par2, :], neg_sink[:, heads],
                                                    ALU.subtract).then_inc(neg_top_set.sem, 1)
                        else:
                            n = (qt + 1) * P
                            nc.vector.memset(bank[0:64, n - 64:n], NEG).then_inc(masked.sem, 1)
                            dve.wait_ge(masked.sem, masked.at(layer, A_KV + i + 1))
                            nc.vector.tensor_reduce(top[:, par2, 0:1], bank[:, 0:n], AX_X, ALU.max,
                                                    negate=True).then_inc(top_set.sem, 1)
                            dve.wait_ge(top_set.sem, top_set.at(layer, 2 * TT * A_KV + i + 1))
                            nc.vector.tensor_scalar(neg_top[:, par2, 0:1], top[:, par2, 0:1], C_SCALE, None,
                                                    ALU.mult).then_inc(neg_top_set.sem, 1)
                    elif name == "turn_y":
                        b = 1 + i // TT
                        dve.wait_ge(aux_ready.sem, aux_ready.at(layer, u + 1))
                        dve.wait_ge(silu_set.sem, silu_set.at(layer, BR * (b + 1)))
                        if i > 0:
                            dve.wait_ge(y_hi_set.sem, y_hi_set.at(layer, BR + i))
                        ts = slice((i % TT) * P, (i % TT + 1) * P)
                        pre = y_pre[:, :].rearrange("p (f n) -> p f n", f=BR)
                        nc.vector.tensor_tensor(pre, aux[:, :].rearrange("p (f n) -> p f n", f=BR),
                                                gates[:, 0:BR, ts], ALU.mult).then_inc(aux_free.sem, 1)
                        dve.wait_ge(aux_free.sem, aux_free.at(layer, u + 1))
                        nc.vector.tensor_copy(recip[:, 0:1], recip[:, 0:1]).then_inc(y_pre_set.sem, 1)
                        dve.wait_ge(y_hi_set.sem, y_hi_set.at(layer, BR + i + 1))
                        nc.vector.tensor_tensor(y_lo[:, :, ts], pre, y_hi[:, :, ts].bitcast(F32),
                                                ALU.subtract).then_inc(y_lo_set.sem, 1)
                    elif name in ("value_a", "value_c"):
                        step = i if name == "value_a" else TT * A_KV + i
                        kind, qt, h, q_all = attention_of(step)
                        if h == (A_KV if kind == "a" else C_HEADS) - 1:
                            dve.wait_ge(value_done.sem, value_done.at(layer, step + 1))
                            total = sums[:, qt % 2, :]
                            if kind == "a":
                                nc.vector.tensor_tensor(recip[:, :], total, sink_exp[:, qt % 2, :],
                                                        ALU.add).then_inc(denom_set.sem, 1)
                                dve.wait_ge(denom_set.sem, denom_set.at(layer, 2 * qt + 1))
                                nc.vector.reciprocal(recip[:, :], recip[:, :]).then_inc(denom_set.sem, 1)
                                dve.wait_ge(denom_set.sem, denom_set.at(layer, 2 * qt + 2))
                            else:
                                nc.vector.reciprocal(recip[:, :], total).then_inc(denom_set.sem, 1)
                                dve.wait_ge(denom_set.sem, denom_set.at(layer, 2 * TT + qt + 1))
                            if q_all > 0:
                                v = AUX.index(("turn_y", q_all - 1))
                                dve.wait_ge(aux_ready.sem, aux_ready.at(layer, v + 1))
                            nc.vector.tensor_tensor(y_nat[:, :].rearrange("p (h n) -> p h n", h=A_HEADS),
                                                    o_bank[:, :].rearrange("p (h n) -> p h n", h=A_HEADS),
                                                    recip[:, :].unsqueeze(2).broadcast_to([P, A_HEADS, A_DH]),
                                                    ALU.mult).then_inc(y_nat_set.sem, 1)
                    elif name == "quarter" and i % 4 == 3:
                        p = i // 4
                        res = ring[first_output(p) % 3][:, :]
                        g = gate_index(p)
                        if g is not None:
                            b, j = g
                            evacuated(layer, p)
                            if j >= 8:
                                dve.wait_ge(silu_set.sem, silu_set.at(layer, BR * b + j - 8 + 1))
                            nc.vector.scalar_tensor_tensor(gates[:, j, :], res, 0.5, rstd[:, :], ALU.mult,
                                                           ALU.mult).then_inc(proj_free.sem, 1)
                        elif p in (PQA + 1, PQA + 3):
                            n = (p - PQA) // 2
                            evacuated(layer, p)
                            ra, rb = (ring[first_output(q) % 3][:, :] for q in (p - 1, p))
                            if n == 0:
                                dve.wait_ge(k_rope_saved.sem, k_rope_saved.at(layer, 32))
                            dve.wait_ge(rope_out.sem, rope_out.at(layer, 6 + 8 * n))
                            nc.vector.tensor_tensor(work[:, 0, :], ra, cos_r, ALU.mult).then_inc(rope_prod.sem, 1)
                            nc.vector.tensor_tensor(work[:, 3, :], ra, sin_r, ALU.mult).then_inc(proj_free.sem, 1)
                            nc.vector.tensor_tensor(work[:, 1, :], rb, sin_r, ALU.mult).then_inc(rope_prod.sem, 1)
                            nc.vector.tensor_tensor(work[:, 2, :], rb, cos_r, ALU.mult).then_inc(proj_free.sem, 1)
                            dve.wait_ge(proj_free.sem, proj_free.at(layer, first_output(p) + 1))
                            for hh in range(4):
                                h = 4 * n + hh
                                rows = slice(32 * hh, 32 * hh + 32)
                                nc.vector.tensor_tensor(q_a[0:32, h, :], work[rows, 0, :],
                                                        work[rows, 1, :], ALU.subtract).then_inc(rope_out.sem, 1)
                                nc.vector.tensor_tensor(q_a[32:64, h, :], work[rows, 2, :],
                                                        work[rows, 3, :], ALU.add).then_inc(rope_out.sem, 1)
                        elif p == PN1 + 3:
                            evacuated(layer, p)
                            for t in range(TT):
                                nc.vector.scalar_tensor_tensor(k_dec[:, t, :], nat[t][:, 0:256], rstd_nat[:, t:t + 1],
                                                               dec[:, t, :], ALU.mult, ALU.mult)
                                nc.vector.tensor_scalar(v_a[:, t, :], nat[t][:, 256:384], rstd_nat[:, t:t + 1], None,
                                                        ALU.mult).then_inc(nat_free.sem, 1)
                        elif p == PN2 + 3:
                            evacuated(layer, p)
                            for t in range(TT):
                                nc.vector.tensor_scalar(v_b[:, t, :], nat[t][:, :], rstd_nat[:, t:t + 1], None,
                                                        ALU.mult).then_inc(nat_free.sem, 1)
                        elif PQB <= p < PQB + 2:
                            evacuated(layer, p)
                            nc.vector.scalar_tensor_tensor(q_b[:, p - PQB, :], res, B_DK ** -0.5, rstd[:, :], ALU.mult,
                                                           ALU.mult).then_inc(proj_free.sem, 1)
                        elif PCQ <= p <= PCKV:
                            evacuated(layer, p)
                            nc.vector.tensor_tensor(latent[:, p - PCQ, :], res, rstd[:, :],
                                                    ALU.mult).then_inc(proj_free.sem, 1)
                            if p == PCQ + 1:
                                dve.wait_ge(lat_sq.sem, lat_sq.at(layer, 2))
                                nc.vector.tensor_tensor(sq_sum, sq[0], sq[1], ALU.add).then_inc(lat_acc.sem, 1)
                        elif p in range(PO[0], PO[0] + 4) or p in range(PO[1], PO[1] + 4) or p in range(PO[2], PO[2] + 4):
                            b = [o <= p < o + 4 for o in PO].index(True)
                            for o in range(2):
                                j = 2 * (p - PO[b]) + o
                                evacuated(layer, p, o + 1)
                                z = ring[(first_output(p) + o) % 3][:, :]
                                dve.wait_ge(gate_tanh.sem, gate_tanh.at(layer, 12 * b + 4 + j + 1))
                                tile = gates[:, 4 + j, :]
                                nc.vector.scalar_tensor_tensor(merged[:, j, :] if b == 0 else tile, tile, 1.0, z,
                                                               ALU.add, ALU.mult).then_inc(proj_free.sem, 1)
                                dve.wait_ge(proj_free.sem, proj_free.at(layer, first_output(p) + o + 1))
                                if b > 0:
                                    nc.vector.tensor_tensor(merged[:, j, :], merged[:, j, :], tile,
                                                            ALU.add).then_inc(merged_set.sem, 1)
                            if b == 2:
                                for o in range(2):
                                    j = 2 * (p - PO[b]) + o
                                    dve.wait_ge(merge_hi.sem, merge_hi.at(layer, j + 1))
                                    nc.vector.scalar_tensor_tensor(act_lo[:, j, :], merged[:, j, :], 0.5,
                                                                   act_hi[:, j, :].bitcast(F32), ALU.mult,
                                                                   ALU.subtract).then_inc(merge_lo.sem, 1)
                        elif p == PUKV:
                            dve.wait_ge(read_done.sem, read_done.at(layer, B_HEADS))
                            dve.wait_ge(value_done.sem, value_done.at(layer, TT * A_KV))
                            for o in range(8):
                                evacuated(layer, p, o + 1)
                                r = ring[(first_output(p) + o) % 3]
                                if o < 4:
                                    nc.vector.tensor_copy(v_c[:, o, :], r[:, :]).then_inc(proj_free.sem, 1)
                                else:
                                    h = 2 * (o - 4)
                                    nc.vector.tensor_copy(k_c[0:64, h, :], r[0:64, :])
                                    nc.vector.tensor_copy(k_c[0:64, h + 1, :], r[64:128, :]).then_inc(proj_free.sem, 1)
                        elif p in (PUQ, PUQ + 1):
                            if p == PUQ:
                                evacuated(layer, p, 2)
                                f = first_output(p)
                                ra, rb = ring[f % 3][:, :], ring[(f + 1) % 3][:, :]
                                cos, sin = rope[:, 2, :], rope[:, 3, :]
                                nc.vector.tensor_tensor(work[:, 0, :], ra, cos, ALU.mult).then_inc(rope_prod.sem, 1)
                                nc.vector.tensor_tensor(work[:, 3, :], ra, sin, ALU.mult).then_inc(proj_free.sem, 1)
                                nc.vector.tensor_tensor(work[:, 1, :], rb, sin, ALU.mult).then_inc(rope_prod.sem, 1)
                                nc.vector.tensor_tensor(work[:, 2, :], rb, cos, ALU.mult).then_inc(proj_free.sem, 1)
                                dve.wait_ge(proj_free.sem, proj_free.at(layer, f + 2))
                                nc.vector.tensor_tensor(work[:, 0, :], work[:, 0, :], work[:, 1, :],
                                                        ALU.subtract).then_inc(rope_out.sem, 1)
                                nc.vector.tensor_tensor(work[:, 2, :], work[:, 2, :], work[:, 3, :],
                                                        ALU.add).then_inc(rope_out.sem, 1)
                            for o in ((2,) if p == PUQ else (0, 1, 2)):
                                evacuated(layer, p, o + 1)
                                r = ring[(first_output(p) + o) % 3]
                                h = 0 if p == PUQ else 2 * (o + 1)
                                nc.vector.tensor_copy(q_c[0:64, h, :], r[0:64, :])
                                nc.vector.tensor_copy(q_c[0:64, h + 1, :], r[64:128, :]).then_inc(proj_free.sem, 1)
                        elif p >= PW:
                            evacuated(layer, p)
                            nc.vector.tensor_tensor(xt[:, p - PW, :], xt[:, p - PW, :], res,
                                                    ALU.add).then_inc(proj_free.sem, 1)
                    if (name, i) in AUX:
                        u += 1
            add_squares(DEPTH)
            refine(DEPTH, 0, 0, rstd[:, :], D).then_inc(rstd_set.sem, 1)
            dve.wait_ge(rstd_set.sem, rstd_set.at(DEPTH, 1))
            for j in range(KT):
                nc.vector.scalar_tensor_tensor(gates[:, j, :], xt[:, j, :], fin_g[:, j:j + 1], rstd[:, :], ALU.mult,
                                               ALU.mult).then_inc(out_scaled.sem, 1)


def pack_pieces(w_in, w_oa, w_ob, w_oc, w_uq, w_ukv, w_out):
    off = dict(zip(("qa", "ka", "va", "ga", "qb", "kb", "vb", "ab", "gb", "cq", "ckv", "kr", "gc", "mg"),
                   np.cumsum([0, 512, 128, 128, 512, 256, 256, 512, 16, 512, 256, 128, 32, 512])))
    out = np.zeros((DEPTH, PIECES, P, 1024), w_in.dtype)

    def put(layer, p, w, cols, tiles=None):
        w = w[:, cols].reshape(-1, P, len(cols))
        w = w if tiles is None else w[tiles]
        out[layer, p, :, :w.shape[0] * w.shape[2]] = w.transpose(1, 0, 2).reshape(P, -1)

    for l in range(DEPTH):
        w = w_in[l]
        for p, half in ((PX, 0), (PY, 1)):
            ka = [off["ka"] + 64 * g + 32 * half + r for g in range(A_KV) for r in range(32)]
            kr = [off["kr"] + 16 * half + r for r in range(16)]
            tile = out[l, p].reshape(P, KT, P)
            src = w.reshape(KT, P, -1).transpose(1, 0, 2)
            tile[:, :, 0:64] = src[:, :, ka]
            tile[:, :, 64:80] = src[:, :, kr]
            if half == 0:
                tile[:, :, 96:112] = src[:, :, off["ab"]:off["ab"] + B_RANK]
        for n in range(2):
            for half in range(2):
                put(l, PQA + 2 * n + half, w, [off["qa"] + 64 * (4 * n + h) + 32 * half + r
                                               for h in range(4) for r in range(32)])
        for n in range(4):
            put(l, PN1 + n, w, [*range(off["kb"], off["kb"] + 256), *range(off["va"], off["va"] + 128)],
                slice(2 * n, 2 * n + 2))
            put(l, PN2 + n, w, list(range(off["vb"], off["vb"] + 512)), slice(2 * n, 2 * n + 2))
        for n in range(2):
            put(l, PQB + n, w, list(range(off["qb"] + P * n, off["qb"] + P * n + P)))
            put(l, PCQ + n, w, list(range(off["cq"] + P * n, off["cq"] + P * n + P)))
        put(l, PCKV, w, list(range(off["ckv"], off["ckv"] + P)))
        for b, (gate, branch, wo) in enumerate((("gb", 1, w_ob), ("ga", 0, w_oa), ("gc", 2, w_oc))):
            for n in range(4):
                put(l, PG[b] + n, w, list(range(off[gate] + P * n, off[gate] + P * n + P)))
                put(l, PO[b] + n, wo[l], list(range(256 * n, 256 * n + 256)))
            for n in range(8):
                c = off["mg"] + D * branch + P * n
                put(l, PM[b] + n, w, list(range(c, c + P)))
        kv = C_NOPE + C_V
        put(l, PUKV, w_ukv[l], [kv * h + C_NOPE + r for h in range(C_HEADS) for r in range(C_V)]
            and [kv * h + r for h in range(C_HEADS) for r in range(C_NOPE)]
            + [kv * h + C_NOPE + r for h in range(C_HEADS) for r in range(C_V)])
        first = [C_DH * h + C_NOPE + r for h in range(C_HEADS) for r in range(16)]
        nope = [C_DH * h + r for h in range(C_HEADS) for r in range(C_NOPE)]
        put(l, PUQ, w_uq[l], first + [c + 16 for c in first] + nope[0:P])
        put(l, PUQ + 1, w_uq[l], nope[P:])
        for n in range(KT):
            put(l, PW + n, w_out[l], list(range(P * n, P * n + P)))
    return out.reshape(DEPTH * PIECES, P, 1024)


def rotary_tables():
    out = np.zeros((P, 4, S), np.float32)
    pos = np.arange(S, dtype=np.float32)
    for n, dim in enumerate((A_DH, C_ROPE)):
        inv = (10000.0 ** (-np.arange(0, dim, 2) / dim)).astype(np.float32)
        ang = (inv[:, None] * pos[None, :]).astype(np.float32)
        reps = P // len(inv)
        out[:, 2 * n] = np.tile(np.cos(ang), (reps, 1))
        out[:, 2 * n + 1] = np.tile(np.sin(ang), (reps, 1))
    return out


def constant_table():
    t = np.arange(P)
    same = t[:, None] // CHUNK == t[None, :] // CHUNK
    out = np.zeros((P, CONSTS), np.float32)
    out[:, ONES:ONES + P] = 1.0
    out[:, IDENT:IDENT + P] = np.eye(P)
    out[:, LATER:LATER + P] = (same & (t[:, None] > t[None, :])) / B_TAU
    out[:, MEMBER:MEMBER + 2] = (t[:, None] // CHUNK == np.arange(2)[None, :]) / B_TAU
    return out


def kernel(x, norm_g, w_in, a_sinks, w_oa, w_alpha, b_alpha, b_head_g, w_ob, cq_g, w_uq, ckv_g, w_ukv, w_oc, w_out,
           final_g):
    import concourse.bacc as bacc
    from concourse.bass_utils import run_bass_kernel_spmd

    (x, norm_g, w_in, a_sinks, w_oa, w_alpha, b_alpha, b_head_g, w_ob, cq_g, w_uq, ckv_g, w_ukv, w_oc, w_out,
     final_g) = (np.asarray(a) for a in (x, norm_g, w_in, a_sinks, w_oa, w_alpha, b_alpha, b_head_g, w_ob, cq_g, w_uq,
                                         ckv_g, w_ukv, w_oc, w_out, final_g))
    params = np.zeros((P, DEPTH, PARAMS), x.dtype)
    for l in range(DEPTH):
        params[:, l, G_X:G_X + KT] = norm_g[l].reshape(KT, P).T
        params[:, l, G_BH] = b_head_g[l]
        params[:, l, G_CQ:G_CQ + 2] = cq_g[l].reshape(2, P).T
        params[:, l, G_CKV] = ckv_g[l]
        params[:, l, SINKS:SINKS + A_HEADS] = a_sinks[l][None, :]
    arrays = {
        "x_t": np.ascontiguousarray(x[0].T.reshape(KT, P, S).transpose(1, 0, 2)),
        "pieces": pack_pieces(w_in, w_oa, w_ob, w_oc, w_uq, w_ukv, w_out),
        "params": params,
        "alpha": np.ascontiguousarray(np.concatenate([w_alpha, b_alpha[:, None, :]], axis=1).transpose(1, 0, 2)),
        "tables": rotary_tables(),
        "consts": constant_table(),
        "final_gain": np.ascontiguousarray(final_g.reshape(KT, P).T),
    }
    nc = bacc.Bacc("TRN2", target_bir_lowering=False, num_devices=1, dynamic_dma_scratch_size=1024)
    aps = [nc.dram_tensor(name, a.shape, mybir.dt.from_np(a.dtype), kind="ExternalInput").ap()
           for name, a in arrays.items()]
    out_t = nc.dram_tensor("out_t", (P, KT, S), F32, kind="ExternalOutput").ap()
    k_rope_dram = nc.dram_tensor("k_rope_dram", (C_ROPE, S), F32, kind="Internal").ap()
    q_rope_dram = nc.dram_tensor("q_rope_dram", (2, P, S), F32, kind="Internal").ap()
    build_hybrid_trunk(nc, *aps, out_t, k_rope_dram, q_rope_dram)
    r = run_bass_kernel_spmd(nc, [arrays], core_ids=[0])
    got = r.results[0]["out_t"]
    return np.ascontiguousarray(got.transpose(1, 0, 2).reshape(D, S).T)[None]
```

```python
from contextlib import ExitStack

import numpy as np

import concourse.bass as bass
from concourse import mybir

F32 = mybir.dt.float32
F32R = mybir.dt.float32r
ALU = mybir.AluOpType
ACT = mybir.ActivationFunctionType
AX_X = mybir.AxisListType.X

DEPTH, D, S, CHUNK, P = 2, 1024, 512, 64, 128
EPS, NEG = 1e-6, -1e30
KT = D // P
TT = S // P
NC = S // CHUNK
A_HEADS, A_KV, A_DH = 8, 2, 64
GROUP = A_HEADS // A_KV
B_HEADS, B_DK, B_DV, B_RANK, B_TAU = 4, 64, 128, 16, 16.0
C_HEADS, C_QR, C_KVR, C_NOPE, C_ROPE, C_V = 8, 256, 128, 64, 32, 64
C_DH = C_NOPE + C_ROPE
A_SCALE, C_SCALE = A_DH ** -0.5, C_DH ** -0.5
BR = 512 // P

PX, PY = 0, 1
PQA = 2
PN1 = 6
PQB = 10
PCQ, PCKV = 12, 14
PN2 = 15
PG = [19, 35, 54]
PM = [23, 39, 58]
PO = [31, 50, 66]
PUKV, PUQ = 47, 48
PW = 70
PIECES = 78
RAW, HL = 3, 3


def outputs_of(p):
    if PN1 <= p < PN1 + 4 or PN2 <= p < PN2 + 4:
        return 0
    if any(o <= p < o + 4 for o in PO):
        return 2
    return {PUKV: 8, PUQ: 3, PUQ + 1: 3}.get(p, 1)


def first_output(p):
    return sum(outputs_of(q) for q in range(p))


def signals_before(p):
    return sum(max(outputs_of(q), 1) for q in range(p))


def gate_index(p):
    for b in range(3):
        if PG[b] <= p < PG[b] + 4:
            return b, p - PG[b]
        if PM[b] <= p < PM[b] + 8:
            return b, 4 + p - PM[b]
    return None


def make_schedule():
    todo = [("split_x", 0)]

    def piece(*ps):
        for p in ps:
            for q in range(4):
                todo.append(("quarter", 4 * p + q))

    def step(*names):
        for name, i in names:
            todo.append((name, i))

    piece(PX)
    step(("rms", 0))
    piece(PY)
    step(("rope_k", 0))
    piece(PQA)
    step(("rstd_nat", 0))
    piece(PQA + 1, PQA + 2)
    step(("gla_gate", 0))
    piece(PQA + 3)
    step(("gla_gate", 1))
    piece(PN1, PN1 + 1)
    step(("gla_decay", 0))
    piece(PN1 + 2)
    step(("gla_decay", 1), ("gla_end", 0))
    piece(PN1 + 3, PQB, PQB + 1, PCQ, PCQ + 1, PCKV, PN2)
    step(("latent", 0))
    piece(PN2 + 1)
    step(("latent_norm", 0), ("latent", 1), ("latent_hi", 0))
    piece(PN2 + 2)
    step(("latent_norm", 1), ("latent_lo", 0), ("latent_hi", 1))
    piece(PN2 + 3)
    g, m = PG[0], PM[0]
    piece(g)
    step(("latent_lo", 1), ("tanh", 0), ("gla_state", 0), ("gla_state", 1))
    piece(g + 1)
    step(("tanh", 1), ("silu", 0), ("gla_state", 2), ("gla_state", 3))
    piece(g + 2)
    step(("tanh", 2), ("silu", 1))
    piece(g + 3)
    step(("tanh", 3), ("silu", 2), ("gla_read", 0), ("gla_read", 1), ("gla_read", 2), ("gla_read", 3))
    piece(m)
    step(("silu", 3))
    for h in range(B_HEADS + 1):
        if h < B_HEADS:
            step(("gla_norm", h))
        quarters_of = [("quarter", 4 * (m + 1 + h) + q) for q in range(4)]
        todo.extend(quarters_of[:3])
        if h < B_HEADS:
            step(("gla_out", h))
        step(quarters_of[3])
        if h < B_HEADS:
            step(("gla_hi", h))
        if h >= 1:
            step(("gla_lo", h - 1))
    step(*(("tanh", 4 + j) for j in range(6)))
    piece(m + 6)
    step(("tanh", 10))
    piece(m + 7)
    step(("tanh", 11))

    def quarters(n):
        for _ in range(min(n, len(fill))):
            q = fill.pop(0)
            todo.append(("quarter", q))
            g = gate_index(q // 4)
            if q % 4 == 3 and g is not None:
                b, j = g
                todo.append(("tanh", 12 * b + j))
                if 1 <= j <= BR:
                    todo.append(("silu", BR * b + j - 1))

    fill = [4 * p + q for p in [*range(PO[0], PO[0] + 4), *range(PG[1], PG[1] + 12)] for q in range(4)]
    na = TT * A_KV
    quarters(28)
    for s in range(na + 3):
        y, last = divmod(s - 3, A_KV)
        if s < na:
            todo.append(("score_a", s))
        quarters(1)
        if y >= 1 and last == 0:
            todo.append(("y_lo", y - 1))
        if s >= 3:
            todo.append(("value_a", s - 3))
        if 2 <= s < na + 2:
            todo.append(("turn", s - 2))
        quarters(1)
        if y >= 0 and last:
            todo.append(("turn_y", y))
        quarters(1)
        if y >= 0 and last:
            todo.append(("y_hi", y))
    quarters(len(fill))
    todo.append(("y_lo", TT - 1))
    piece(PUKV, PUQ, PUQ + 1, *range(PO[1], PO[1] + 4))
    fill = [4 * p + q for p in range(PG[2], PG[2] + 12) for q in range(4)]
    nc_ = TT * C_HEADS
    quarters(10)
    for i in range(nc_ + 3):
        if i < nc_:
            todo.append(("score_c", i))
        if i >= 3:
            todo.append(("value_c", i - 3))
        if 2 <= i < nc_ + 2:
            todo.append(("turn", na + i - 2))
        if i not in (12, 14):
            quarters(1)
        y, h = divmod(i - 3 + 1, C_HEADS)
        if y >= 1 and h < 3:
            todo.append((("turn_y", "y_hi", "y_lo")[h], TT + y - 1))
    quarters(1)
    todo.append(("y_hi", 2 * TT - 1))
    quarters(len(fill))
    todo.append(("y_lo", 2 * TT - 1))
    piece(*range(PO[2], PO[2] + 4), *range(PW, PW + KT))
    return todo


SCHEDULE = make_schedule()
AUX = [s for s in SCHEDULE if s[0] in ("rms", "rstd_nat", "gla_gate", "gla_decay", "gla_end", "latent",
                                       "gla_norm", "turn_y")]

G_X, G_BH, G_CQ, G_CKV, SINKS = 0, 8, 9, 11, 12
PARAMS = 20
ONES, IDENT, LATER, MEMBER = 0, 128, 256, 384
CONSTS = 386


class Signal:

    def __init__(self, ctx, nc, name, per_layer, before=0):
        self.sem = ctx.enter_context(nc.semaphore(name))
        self.per_layer, self.before = per_layer, before

    def at(self, layer, n):
        assert n > 0 or self.before > 0, "a wait on a register's value needs it above zero"
        return layer * self.per_layer + (self.before + max(n, 1 - self.before))


def build_hybrid_trunk(nc, x_t, pieces, params, alpha, tables, consts, final_g, out_t, k_rope_dram, q_rope_dram):
    with ExitStack() as ctx:
        def sb(name, shape, dt=F32):
            return ctx.enter_context(nc.sbuf_tensor(name, shape, dt))

        def sig(name, per_layer, before=0):
            return Signal(ctx, nc, name, per_layer, before)

        xt = sb("xt", [P, KT, S])
        act_hi = sb("act_hi", [P, KT, S], F32R)
        act_lo = sb("act_lo", [P, KT, S], F32R)
        raw = sb("raw", [P, RAW, 1024])
        w_hi = sb("w_hi", [P, HL, 1024], F32R)
        w_lo = sb("w_lo", [P, HL, 1024], F32R)
        gates = sb("gates", [P, 12, S])
        merged = sb("merged", [P, KT, S])
        y_hi = sb("y_hi", [P, BR, S], F32R)
        y_lo = sb("y_lo", [P, BR, S], F32R)
        bank_g = sb("bank_g", [P, 4096])
        bank_a = sb("bank_a", [P, 6144])
        lat_hi = sb("lat_hi", [P, 3, S], F32R)
        lat_lo = sb("lat_lo", [P, 3, S], F32R)
        rope = sb("rope", [P, 4, S])
        rstd = sb("rstd", [P, S])
        work = sb("work", [P, 4, S])
        y_nat = sb("y_nat", [P, S])
        y_pre = sb("y_pre", [P, S])
        con = sb("con", [P, CONSTS])
        par_all = sb("par_all", [P, DEPTH, PARAMS])
        par = sb("par", [P, PARAMS])
        alpha_all = sb("alpha_all", [P, DEPTH, B_HEADS * B_DK])
        w_alpha = sb("w_alpha", [P, B_HEADS * B_DK])
        fin_g = sb("fin_g", [P, KT])
        eps = sb("eps", [P, 1])
        rstd_nat = sb("rstd_nat", [P, TT])
        decay = sb("decay", [P, 2 * NC])
        neg_sink = sb("neg_sink", [P, A_HEADS])
        top = sb("top", [P, 2, GROUP])
        neg_top = sb("neg_top", [P, 2, GROUP])
        sink_in = sb("sink_in", [P, 2, GROUP])
        sink_exp = sb("sink_exp", [P, TT, A_HEADS])
        sums = sb("sums", [P, TT, A_HEADS])
        recip = sb("recip", [P, A_HEADS])

        ones, ident = con[:, ONES:ONES + P], con[:, IDENT:IDENT + P]
        later, member = con[:, LATER:LATER + P], con[:, MEMBER:MEMBER + 2]
        prob, prob_t = [work[:, i, :] for i in range(3)], work[:, 3, :]
        k_dec = bank_g[:, 0:1024].rearrange("p (t n) -> p t n", t=TT)
        v_b = bank_g[:, 1024:3072].rearrange("p (t n) -> p t n", t=TT)
        q_b = bank_g[:, 3072:4096].rearrange("p (t n) -> p t n", t=2)
        k_c = bank_g[:, :].rearrange("p (h n) -> p h n", h=C_HEADS)
        q_a = bank_a[0:64, 0:4096].rearrange("p (h n) -> p h n", h=A_HEADS)
        k_a = bank_a[0:64, 4096:5120].rearrange("p (t n) -> p t n", t=2)
        v_a = bank_a[:, 5120:5632].rearrange("p (t n) -> p t n", t=TT)
        v_as = bank_a[:, 5632:6144].rearrange("p (t n) -> p t n", t=TT)
        q_c = bank_a[:, 0:4096].rearrange("p (h n) -> p h n", h=C_HEADS)
        v_c = bank_a[:, 4096:6144].rearrange("p (t n) -> p t n", t=TT)
        sq = [merged[:, 0, :], merged[:, 1, :]]
        sq_sum, ln_ms, ab1, second = merged[:, 2, :], merged[:, 3, :], merged[:, 4, :], merged[:, 5, :]
        lat_rstd = merged[:, 6, :]
        state = merged[:, 0:4, :].rearrange("p a (c j v) -> p (a c) j v", c=2, j=2)
        o_sq = [merged[:, 4, :], merged[:, 5, :]]
        o_ln, o_rstd = merged[:, 6, :], merged[:, 7, :]
        cos_r, sin_r = gates[:, 0, :], gates[:, 1, :]
        latent = gates[:, 2:5, :]
        dec = gates[:, 6:8, :].rearrange("p a (t n) -> p (a t) n", t=2)
        soft = gates[:, 8:10, :].rearrange("p a (t n) -> p (a t) n", t=2)
        log_a = gates[:, 10:12, :].rearrange("p a (t n) -> p (a t) n", t=2)

        ring = [ctx.enter_context(nc.psum_tensor(f"ring{i}", [P, S], F32)) for i in range(3)]
        nat = [ctx.enter_context(nc.psum_tensor(f"nat{i}", [P, S], F32)) for i in range(4)]
        aux = ctx.enter_context(nc.psum_tensor("aux", [P, S], F32))
        turn_bank, o_bank = nat[2], nat[3]

        raw_loaded = [sig(f"raw_loaded{i}", 16 * PIECES // RAW) for i in range(RAW)]
        par_loaded, setup_loaded = sig("par_loaded", 0), sig("setup_loaded", 0)
        x_loaded = [sig(f"x_loaded{i}", 0) for i in range(KT // 2)]
        eps_set = sig("eps_set", 0)
        hi_split, lo_split = sig("hi_split", PIECES), sig("lo_split", PIECES)
        proj_done = sig("proj_done", signals_before(PIECES), HL + 1)
        proj_free = sig("proj_free", first_output(PIECES), KT)
        par_set = sig("par_set", 2)
        x_hi, x_lo = sig("x_hi", KT), sig("x_lo", KT)
        x_sq, x_acc = sig("x_sq", KT, KT - 1), sig("x_acc", KT, KT - 1)
        act_used = sig("act_used", 3, 3)
        aux_ready, aux_free = sig("aux_ready", len(AUX)), sig("aux_free", len(AUX), 1)
        n_norms = 3 + B_HEADS
        log_set, rough_set, newton = sig("log_set", n_norms), sig("rough_set", n_norms), sig("newton", 2 * n_norms)
        rstd_set = sig("rstd_set", 1)
        ones_row = sig("ones_row", 1)
        rope_scaled = sig("rope_scaled", 2)
        rope_prod, rope_out = sig("rope_prod", 14), sig("rope_out", 24)
        k_rope_saved, k_rope_placed = sig("k_rope_saved", 32), sig("k_rope_placed", 16)
        q_rope_saved, q_rope_placed = sig("q_rope_saved", 32), sig("q_rope_placed", 32)
        gla_soft = sig("gla_soft", 6)
        nat_free = sig("nat_free", 8)
        v_cleared, v_shifted = sig("v_cleared", 1), sig("v_shifted", 32)
        lat_sq, lat_acc, lat_rs = sig("lat_sq", 3), sig("lat_acc", 1), sig("lat_rs", 2)
        lat_norm, lat_hi_set, lat_lo_set = sig("lat_norm", 3), sig("lat_hi_set", 3), sig("lat_lo_set", 3)
        state_in, state_set = sig("state_in", 4), sig("state_set", 2 * NC)
        read_done, read_sq, read_rs = sig("read_done", B_HEADS), sig("read_sq", B_HEADS), sig("read_rs", B_HEADS)
        read_norm = sig("read_norm", B_HEADS)
        y_pre_set, y_hi_set, y_lo_set = sig("y_pre_set", B_HEADS), sig("y_hi_set", 12), sig("y_lo_set", 12)
        gate_tanh, silu_set = sig("gate_tanh", 36), sig("silu_set", 12)
        n_steps = TT * A_KV + TT * C_HEADS
        scores_done = sig("scores_done", n_steps)
        masked = sig("masked", A_KV + TT * C_HEADS)
        top_set = sig("top_set", 2 * TT * A_KV + TT * C_HEADS)
        neg_top_set, exp_done = sig("neg_top_set", n_steps), sig("exp_done", n_steps)
        turn_done, turn_out, value_done = (sig("turn_done", n_steps), sig("turn_out", n_steps),
                                           sig("value_done", n_steps))
        denom_set, y_nat_set = sig("denom_set", 2 * TT + TT), sig("y_nat_set", 2 * TT, 1)
        sink_neg = sig("sink_neg", 1)
        merged_set = sig("merged_set", 2 * KT)
        merge_hi, merge_lo = sig("merge_hi", KT), sig("merge_lo", KT)
        gained, scaled_dve, scaled_pool = sig("gained", 0), sig("scaled_dve", 0), sig("scaled_pool", 0)
        out_sent = [sig("out_sent_sp", 0), sig("out_sent_act", 0)]
        DVE_TILES = 6

        def attention_of(step):
            if step < TT * A_KV:
                return "a", step // A_KV, step % A_KV, step // A_KV
            c = step - TT * A_KV
            return "c", c // C_HEADS, c % C_HEADS, TT + c // C_HEADS

        LN_EXP = "natural_log_exp_and_others"
        SETUP = 16 * 4
        block = ctx.enter_context(nc.Block())

        @block.sync
        def _(sp):
            for i in range(RAW):
                if i == 1:
                    sp.wait_ge(x_loaded[-1].sem, 16)
                sp.dma_start(raw[:, i, :], pieces[i]).then_inc(raw_loaded[i].sem, 16)
            with sp.Fori(1, DEPTH * PIECES // RAW) as group:
                for i in range(RAW):
                    sp.wait_ge(lo_split.sem, group * RAW + (i - RAW + 1))
                    sp.dma_start(raw[:, i, :], pieces[group * RAW + i]).then_inc(raw_loaded[i].sem, 16)
            for j in range(DVE_TILES):
                sp.wait_ge(scaled_dve.sem, j + 1)
                sp.dma_start(out_t[:, j, :], gates[:, j, :]).then_inc(out_sent[0].sem, 16)
            sp.wait_ge(out_sent[0].sem, 16 * DVE_TILES)
            sp.wait_ge(out_sent[1].sem, 16 * (KT - DVE_TILES))

        @block.gpsimd
        def _(pool):
            with pool.Fori(0, DEPTH * PIECES // RAW) as group:
                for i in range(RAW):
                    pool.wait_ge(hi_split.sem, group * RAW + (i + 1))
                    nc.gpsimd.tensor_tensor(w_lo[:, i, :], raw[:, i, :], w_hi[:, i, :].bitcast(F32),
                                            ALU.subtract).then_inc(lo_split.sem, 1)
            pool.wait_ge(rstd_set.sem, rstd_set.at(DEPTH, 1))
            for j in range(DVE_TILES, KT):
                pool.wait_ge(gained.sem, j + 1)
                nc.gpsimd.tensor_tensor(gates[:, j, :], gates[:, j, :], rstd[:, :], ALU.mult).then_inc(scaled_pool.sem, 1)

        @block.tensor
        def _(pe):
            def project(layer, quarter):
                p, part = divmod(quarter, 4)
                slot = p % HL
                whi, wlo = w_hi[:, slot, :], w_lo[:, slot, :]
                if part == 0:
                    pe.wait_ge(lo_split.sem, lo_split.at(layer, p + 1))
                natural = PN1 <= p < PN1 + 4 or PN2 <= p < PN2 + 4
                n_out = outputs_of(p)
                if natural:
                    first, n_k, width = (PN1, 2, 384) if p < PQB else (PN2, 2, 512)
                    jobs = [(t, 2 * (p - first) + k, k) for k in range(2) for t in range(TT)]
                elif p == PUKV:
                    jobs = [(o, 0, 0) for o in range(8)]
                elif p in (PUQ, PUQ + 1):
                    jobs = [(o, k, k) for o in range(3) for k in range(2)]
                elif n_out == 2:
                    jobs = [(o, k, k) for o in range(2) for k in range(BR)]
                else:
                    jobs = [(0, k, k) for k in range(KT)]
                lo, hi = len(jobs) * part // 4, len(jobs) * (part + 1) // 4
                for n in range(lo, hi):
                    o, k, kw = jobs[n]
                    if natural:
                        bank = nat[o]
                        start, stop = k == 0, k == KT - 1
                        if start:
                            if first == PN2:
                                pe.wait_ge(nat_free.sem, nat_free.at(layer, o + 1))
                            elif o == 0:
                                pe.wait_ge(y_nat_set.sem, y_nat_set.at(layer, 0))
                        dst = bank[:, 0:width]
                        wv = slice(kw * width, (kw + 1) * width)
                        ops = [(act_hi[:, k, o * P:(o + 1) * P], whi[:, wv]),
                               (act_lo[:, k, o * P:(o + 1) * P], whi[:, wv]),
                               (act_hi[:, k, o * P:(o + 1) * P], wlo[:, wv])]
                        done = n == len(jobs) - 1
                    else:
                        r = first_output(p) + o
                        dst = ring[r % 3][:, :]
                        last_k = {PUKV: 0, PUQ: 1, PUQ + 1: 1}.get(p, BR - 1 if n_out == 2 else KT - 1)
                        start, stop = k == 0, k == last_k
                        done = stop
                        if start:
                            pe.wait_ge(proj_free.sem, proj_free.at(layer, r - 2))
                        if p == PUKV and o < 4:
                            ts = slice(o * P, (o + 1) * P)
                            wv = slice(512, 1024)
                            ops = [(lat_hi[:, 2, ts], whi[:, wv]), (lat_lo[:, 2, ts], whi[:, wv]),
                                   (lat_hi[:, 2, ts], wlo[:, wv])]
                        else:
                            if p == PUKV:
                                xh, xl, col = lat_hi[:, 2, :], lat_lo[:, 2, :], (o - 4) * P
                            elif p in (PUQ, PUQ + 1):
                                xh, xl, col = lat_hi[:, k, :], lat_lo[:, k, :], (k * 3 + o) * P
                            elif n_out == 2:
                                xh, xl, col = y_hi[:, k, :], y_lo[:, k, :], (k * 2 + o) * P
                            else:
                                xh, xl, col = act_hi[:, k, :], act_lo[:, k, :], k * P
                            wv = slice(col, col + P)
                            ops = [(whi[:, wv], xh), (whi[:, wv], xl), (wlo[:, wv], xh)]
                    if p == PX:
                        pe.wait_ge(x_lo.sem, x_lo.at(layer, k + 1))
                    elif p == PW:
                        pe.wait_ge(merge_lo.sem, merge_lo.at(layer, k + 1))
                    elif p == PUKV and n == 0:
                        pe.wait_ge(lat_lo_set.sem, lat_lo_set.at(layer, 3))
                    elif p in PO and n == 0:
                        pe.wait_ge(y_lo_set.sem, y_lo_set.at(layer, BR * (PO.index(p) + 1)))
                    for i, (stationary, moving) in enumerate(ops):
                        mm = pe.matmul(dst, stationary, moving, start=start and i == 0, stop=stop and i == 2)
                    if done:
                        mm.then_inc(proj_done.sem, 1)
                if p == PIECES - 1 and part < 3:
                    mm.then_inc(act_used.sem, 1)

            def aux_bank(layer, u):
                pe.wait_ge(aux_free.sem, aux_free.at(layer, u))

            pe.sem_inc(proj_done.sem, proj_done.before)
            pe.sem_inc(act_used.sem, act_used.before)
            with pe.Fori(0, DEPTH) as layer:
                u = 0
                for name, i in SCHEDULE:
                    if name == "quarter":
                        project(layer, i)
                        continue
                    if (name, i) == ("rms", 0):
                        aux_bank(layer, u)
                        pe.wait_ge(setup_loaded.sem, SETUP)
                        pe.wait_ge(x_acc.sem, x_acc.at(layer, 1))
                        mm = pe.matmul(aux[:, :], ones, sq_sum, start=True, stop=True)
                    elif name == "rstd_nat":
                        aux_bank(layer, u)
                        pe.wait_ge(rstd_set.sem, rstd_set.at(layer, 1))
                        for t in range(TT):
                            mm = pe.transpose(aux[:, t * P:(t + 1) * P], rstd[:, t * P:(t + 1) * P], ident)
                    elif name == "gla_gate":
                        aux_bank(layer, u)
                        pe.wait_ge(proj_free.sem, proj_free.at(layer, first_output(PX) + 1))
                        for t in range(2):
                            ts = slice((2 * i + t) * P, (2 * i + t + 1) * P)
                            mm = pe.matmul(aux[:, t * 256:(t + 1) * 256], ab1[96:96 + B_RANK + 1, ts],
                                           w_alpha[96:96 + B_RANK + 1, :], start=True, stop=True)
                    elif name == "gla_decay":
                        aux_bank(layer, u)
                        for t in range(2):
                            mm = pe.matmul(aux[:, t * 256:(t + 1) * 256], later, log_a[:, 2 * i + t, :],
                                           start=True, stop=True)
                    elif name == "gla_end":
                        aux_bank(layer, u)
                        for j in range(2):
                            for t in range(TT):
                                mm = pe.matmul(aux[:, j * NC + 2 * t:j * NC + 2 * t + 2],
                                               log_a[:, t, j * P:(j + 1) * P], member, start=True, stop=True)
                    elif name == "latent":
                        aux_bank(layer, u)
                        if i == 0:
                            pe.wait_ge(lat_acc.sem, lat_acc.at(layer, 1))
                        else:
                            pe.wait_ge(lat_sq.sem, lat_sq.at(layer, 3))
                        mm = pe.matmul(aux[:, :], ones, sq_sum if i == 0 else sq[0], start=True, stop=True)
                    elif name == "gla_state":
                        ready, n = (nat_free, 8) if i < 2 else (state_set, 4 * (i - 1))
                        value = pe.snap(ready.at(layer, n))
                        pe.lower_val(value)
                        pe.wait_ge(setup_loaded.sem, SETUP)
                        pe.wait_ge(ready.sem, value)
                        bank = nat[i % 2]
                        for c in range(2):
                            rows = slice(CHUNK * c, CHUNK * (c + 1))
                            bank = nat[2 * (i % 2) + c]
                            for h in range(B_HEADS):
                                half = slice(64 * (h % 2), 64 * (h % 2) + 64)
                                col = (h // 2) * P
                                mm = pe.matmul(bank[half, col:col + P], k_dec[rows, i, h * B_DK:(h + 1) * B_DK],
                                               v_b[rows, i, h * B_DV:(h + 1) * B_DV], start=True, stop=True)
                        mm.then_inc(state_in.sem, 1)
                    elif name == "gla_read":
                        if i == 0:
                            pe.wait_ge(state_set.sem, state_set.at(layer, 2 * NC))
                        half = slice(64 * (i % 2), 64 * (i % 2) + 64)
                        for c in range(NC):
                            cs = slice(CHUNK * c, CHUNK * (c + 1))
                            mm = pe.matmul(nat[i][:, cs], state[half, c, i // 2, :], q_b[half, i // 2, cs],
                                           start=True, stop=True)
                        mm.then_inc(read_done.sem, 1)
                    elif name == "gla_norm":
                        aux_bank(layer, u)
                        pe.wait_ge(read_sq.sem, read_sq.at(layer, i + 1))
                        mm = pe.matmul(aux[:, :], ones, o_sq[i % 2], start=True, stop=True)
                    elif name == "score_a":
                        qt, g = divmod(i, A_KV)
                        ready, n = (read_norm, B_HEADS) if i < 2 else (exp_done, i - 1)
                        value = pe.snap(ready.at(layer, n))
                        pe.lower_val(value)
                        pe.wait_ge(setup_loaded.sem, SETUP)
                        pe.wait_ge(ready.sem, value)
                        bank = nat[i % 2]
                        for hh in range(GROUP):
                            h = g * GROUP + hh
                            for c in range(2):
                                q0 = qt * P + c * CHUNK
                                k0, skip = (q0 - CHUNK, 0) if q0 else (0, CHUNK)
                                mm = pe.matmul(bank[c * 64:c * 64 + 64, hh * P + skip:(hh + 1) * P],
                                               q_a[:, h, q0:q0 + CHUNK],
                                               k_a[:, g, k0:q0 + CHUNK], start=True, stop=True)
                        mm.then_inc(scores_done.sem, 1)
                    elif name == "score_c":
                        qt, h = divmod(i, C_HEADS)
                        step, n = TT * A_KV + i, (qt + 1) * P
                        pe.wait_ge(exp_done.sem, exp_done.at(layer, step - 1))
                        if i == 0:
                            pe.wait_ge(proj_free.sem, proj_free.at(layer, first_output(PUQ + 2)))
                            pe.wait_ge(k_rope_placed.sem, k_rope_placed.at(layer, 16))
                            pe.wait_ge(q_rope_placed.sem, q_rope_placed.at(layer, 32))
                        mm = pe.matmul(nat[i % 2][:, 0:n], q_c[0:C_DH, h, qt * P:(qt + 1) * P],
                                       k_c[0:C_DH, h, 0:n], start=True, stop=True)
                        mm.then_inc(scores_done.sem, 1)
                    elif name == "turn":
                        kind, qt, h, _ = attention_of(i)
                        pe.wait_ge(exp_done.sem, exp_done.at(layer, i + 1))
                        if i > 0:
                            pe.wait_ge(turn_out.sem, turn_out.at(layer, i))
                        for b in range(GROUP if kind == "a" else qt + 1):
                            mm = pe.transpose(turn_bank[:, b * P:(b + 1) * P], prob[i % 3][:, b * P:(b + 1) * P], ident)
                        mm.then_inc(turn_done.sem, 1)
                    elif name in ("value_a", "value_c"):
                        step = i if name == "value_a" else TT * A_KV + i
                        kind, qt, h, q_all = attention_of(step)
                        if kind == "a" and step == 0:
                            pe.wait_ge(v_shifted.sem, v_shifted.at(layer, 32))
                        if h == 0 and q_all > 0:
                            pe.wait_ge(y_nat_set.sem, y_nat_set.at(layer, q_all))
                        pe.wait_ge(turn_out.sem, turn_out.at(layer, step + 1))
                        pt = prob_t
                        if kind == "a":
                            for hh in range(GROUP):
                                col = (h * GROUP + hh) * A_DH
                                for c in range(2):
                                    mm = pe.matmul(o_bank[c * 64:c * 64 + 64, col:col + A_DH],
                                                   pt[:, hh * P + c * 64:hh * P + c * 64 + 64],
                                                   (v_as, v_a)[c][:, qt, h * A_DH:(h + 1) * A_DH],
                                                   start=True, stop=True)
                        else:
                            for b in range(qt + 1):
                                mm = pe.matmul(o_bank[:, h * C_V:(h + 1) * C_V], pt[:, b * P:(b + 1) * P],
                                               v_c[:, b, h * C_V:(h + 1) * C_V], start=b == 0, stop=b == qt)
                        mm.then_inc(value_done.sem, 1)
                    elif name == "turn_y":
                        aux_bank(layer, u)
                        pe.wait_ge(y_nat_set.sem, y_nat_set.at(layer, i + 1))
                        for f in range(BR):
                            mm = pe.transpose(aux[:, f * P:(f + 1) * P], y_nat[:, f * P:(f + 1) * P], ident)
                    if (name, i) in AUX:
                        mm.then_inc(aux_ready.sem, 1)
                        u += 1
            pe.wait_ge(x_acc.sem, x_acc.at(DEPTH, 1))
            pe.wait_ge(aux_free.sem, aux_free.at(DEPTH, 0))
            pe.matmul(aux[:, :], ones, sq_sum, start=True, stop=True).then_inc(aux_ready.sem, 1)

        @block.scalar
        def _(act):
            def split_hi(layer, p):
                i = p % RAW
                act.wait_ge(raw_loaded[i].sem, raw_loaded[i].at(layer, 16 * (p // RAW + 1)))
                act.wait_ge(proj_done.sem, proj_done.at(layer, signals_before(p - HL + 1) if p >= HL else 0))
                nc.scalar.activation(w_hi[:, p % HL, :], raw[:, i, :], ACT.Copy).then_inc(hi_split.sem, 1)

            def rms_of(layer, u, place, dst, n, tmp):
                act.wait_ge(aux_ready.sem, aux_ready.at(layer, u + 1))
                nc.scalar.activation(tmp, aux[:, :], ACT.Ln, scale=1.0 / n, bias=eps[:, 0:1]).then_inc(log_set.sem, 1)
                act.wait_ge(log_set.sem, log_set.at(layer, place + 1))
                nc.scalar.activation(dst, tmp, ACT.Exp, scale=-0.5).then_inc(rough_set.sem, 1)

            def square(layer, n, buffer_used=True):
                if buffer_used:
                    act.wait_ge(x_acc.sem, x_acc.at(layer, n - 2))
                nc.scalar.activation(sq[n % 2], xt[:, (n - 2) % KT, :], ACT.Square).then_inc(x_sq.sem, 1)

            act.dma_start(par_all[:, :, :], params).then_inc(par_loaded.sem, 16)
            for j in range(KT // 2):
                act.dma_start(xt[:, 2 * j:2 * j + 2, :], x_t[:, 2 * j:2 * j + 2, :]).then_inc(x_loaded[j].sem, 16)
            act.dma_start(con[:, :], consts).then_inc(setup_loaded.sem, 16)
            act.dma_start(alpha_all[96:96 + B_RANK + 1, :, :], alpha).then_inc(setup_loaded.sem, 16)
            act.dma_start(rope[:, :, :], tables).then_inc(setup_loaded.sem, 16)
            act.dma_start(fin_g[:, :], final_g).then_inc(setup_loaded.sem, 16)
            act.wait_ge(par_loaded.sem, 16)
            for n in range(2, KT + 1):
                if n % 2 == 0:
                    act.wait_ge(x_loaded[(n - 2) // 2].sem, 16)
                square(-1, n, buffer_used=n > 3)
            with act.Fori(0, DEPTH) as layer:
                u = 0
                for name, i in SCHEDULE:
                    if name == "split_x":
                        split_hi(layer, 0)
                        nc.scalar.activation(par[:, :], par_all[:, bass.ds(layer, 1), :].rearrange("p a n -> p (a n)"),
                                             ACT.Copy).then_inc(par_set.sem, 1)
                        act.wait_ge(par_set.sem, par_set.at(layer, 1))
                        for j in range(KT):
                            act.wait_ge(x_loaded[j // 2].sem, 16)
                            act.wait_ge(proj_free.sem, proj_free.at(layer, j + 1 - KT))
                            if j < 6:
                                act.wait_ge(act_used.sem, act_used.at(layer, j // 2 - 2))
                            nc.scalar.activation(act_hi[:, j, :], xt[:, j, :], ACT.Copy,
                                                 scale=par[:, G_X + j:G_X + j + 1]).then_inc(x_hi.sem, 1)
                            if j == 2:
                                split_hi(layer, 1)
                        square(layer, 1)
                        split_hi(layer, 2)
                        act.wait_ge(setup_loaded.sem, SETUP)
                        nc.scalar.activation(w_alpha[96:96 + B_RANK + 1, :],
                                             alpha_all[96:96 + B_RANK + 1, bass.ds(layer, 1), :].rearrange(
                                                 "p a n -> p (a n)"), ACT.Copy).then_inc(par_set.sem, 1)
                    elif name == "quarter" and i % 4 == 3:
                        p = i // 4
                        if p + HL < PIECES:
                            split_hi(layer, p + HL)
                        if p in (PCQ, PCQ + 1, PCKV):
                            n = p - PCQ
                            act.wait_ge(proj_free.sem, proj_free.at(layer, first_output(p) + 1))
                            if n == 2:
                                act.wait_ge(lat_acc.sem, lat_acc.at(layer, 1))
                            elif n == 0:
                                act.wait_ge(x_acc.sem, x_acc.at(layer, 1))
                            nc.scalar.activation(sq[n % 2], latent[:, n, :], ACT.Square).then_inc(lat_sq.sem, 1)
                        if p >= PO[2] and p < PO[2] + 4:
                            for o in range(2):
                                j = 2 * (p - PO[2]) + o
                                act.wait_ge(merged_set.sem, merged_set.at(layer, KT + j + 1))
                                nc.scalar.activation(act_hi[:, j, :], merged[:, j, :], ACT.Copy,
                                                     scale=0.5).then_inc(merge_hi.sem, 1)
                        if p > PW:
                            act.wait_ge(proj_free.sem, proj_free.at(layer, first_output(p)))
                            square(layer, p - PW + 1)
                        if p == PUKV:
                            act.wait_ge(k_rope_saved.sem, k_rope_saved.at(layer, 32))
                            act.wait_ge(read_done.sem, read_done.at(layer, B_HEADS))
                            act.dma_start(k_c[C_NOPE:C_DH, :, :],
                                          k_rope_dram.unsqueeze(1).broadcast_to([C_ROPE, C_HEADS, S])
                                          ).then_inc(k_rope_placed.sem, 16)
                        if p == PUQ:
                            act.wait_ge(rope_out.sem, rope_out.at(layer, 24))
                            for half in range(2):
                                act.dma_start(q_rope_dram[half], work[:, 2 * half, :]).then_inc(q_rope_saved.sem, 16)
                            act.wait_ge(q_rope_saved.sem, q_rope_saved.at(layer, 32))
                            for half in range(2):
                                rows = slice(C_NOPE + 16 * half, C_NOPE + 16 * half + 16)
                                act.dma_start(q_c[rows, :, :], q_rope_dram[half].rearrange("(h r) n -> r h n", h=C_HEADS)
                                              ).then_inc(q_rope_placed.sem, 16)
                        if p == PQA:
                            act.wait_ge(rope_out.sem, rope_out.at(layer, 6))
                            act.dma_start(k_rope_dram[0:16, :], second[64:80, :]).then_inc(k_rope_saved.sem, 16)
                            act.dma_start(k_rope_dram[16:32, :], work[64:80, 0, :]).then_inc(k_rope_saved.sem, 16)
                        if p == PN1 + 3:
                            act.wait_ge(nat_free.sem, nat_free.at(layer, 4))
                            act.wait_ge(v_cleared.sem, v_cleared.at(layer, 1))
                            act.dma_start(v_as[0:64, 1:TT, :], v_a[64:128, 0:TT - 1, :]).then_inc(v_shifted.sem, 16)
                            act.dma_start(v_as[64:128, :, :], v_a[0:64, :, :]).then_inc(v_shifted.sem, 16)
                    elif name == "tanh":
                        b, j = divmod(i, 12)
                        p = PG[b] + j if j < 4 else PM[b] + j - 4
                        act.wait_ge(proj_free.sem, proj_free.at(layer, first_output(p) + 1))
                        nc.scalar.activation(gates[:, j if j >= 4 else 8 + j, :], gates[:, j, :],
                                             ACT.Tanh).then_inc(gate_tanh.sem, 1)
                    elif name == "rms":
                        nc.scalar.preload_act_table_set(LN_EXP)
                        rms_of(layer, u, 0, rstd[:, :], D, ln_ms)
                    elif name == "gla_gate":
                        act.wait_ge(aux_ready.sem, aux_ready.at(layer, u + 1))
                        tile = soft[:, 2 * i:2 * i + 2, :].rearrange("p t n -> p (t n)")
                        nc.scalar.activation(tile, aux[:, :], ACT.Abs).then_inc(gla_soft.sem, 1)
                        act.wait_ge(gla_soft.sem, gla_soft.at(layer, 3 * i + 1))
                        nc.scalar.activation(tile, tile, ACT.Exp, scale=-1.0).then_inc(gla_soft.sem, 1)
                        act.wait_ge(gla_soft.sem, gla_soft.at(layer, 3 * i + 2))
                        nc.scalar.activation(tile, tile, ACT.Ln, bias=1.0).then_inc(gla_soft.sem, 1)
                    elif name == "gla_decay":
                        act.wait_ge(aux_ready.sem, aux_ready.at(layer, u + 1))
                        nc.scalar.activation(dec[:, 2 * i:2 * i + 2, :].rearrange("p t n -> p (t n)"), aux[:, :],
                                             ACT.Exp).then_inc(aux_free.sem, 1)
                    elif name == "gla_end":
                        act.wait_ge(aux_ready.sem, aux_ready.at(layer, u + 1))
                        nc.scalar.activation(decay[:, :], aux[:, 0:2 * NC], ACT.Exp).then_inc(aux_free.sem, 1)
                    elif name == "latent":
                        if i == 1:
                            act.wait_ge(lat_norm.sem, lat_norm.at(layer, 2))
                        rms_of(layer, u, 1 + i, lat_rstd, (C_QR, C_KVR)[i], ln_ms)
                    elif name == "latent_hi":
                        for n in ((0, 1), (2,))[i]:
                            act.wait_ge(lat_norm.sem, lat_norm.at(layer, n + 1))
                            nc.scalar.activation(lat_hi[:, n, :], latent[:, n, :], ACT.Copy).then_inc(lat_hi_set.sem, 1)
                    elif name == "gla_read":
                        act.wait_ge(read_done.sem, read_done.at(layer, i + 1))
                        if i >= 2:
                            continue
                        nc.scalar.activation(o_sq[i % 2], nat[i][:, :], ACT.Square).then_inc(read_sq.sem, 1)
                    elif name == "gla_norm":
                        if i == 0:
                            nc.scalar.preload_act_table_set(LN_EXP)
                        else:
                            act.wait_ge(read_norm.sem, read_norm.at(layer, i))
                        rms_of(layer, u, 3 + i, o_rstd, B_DV, o_ln)
                        if i + 2 < B_HEADS:
                            nc.scalar.activation(o_sq[i % 2], nat[i + 2][:, :], ACT.Square).then_inc(read_sq.sem, 1)
                    elif name == "gla_hi":
                        act.wait_ge(y_pre_set.sem, y_pre_set.at(layer, i + 1))
                        nc.scalar.activation(y_hi[:, i, :], work[:, 2 + i % 2, :], ACT.Copy).then_inc(y_hi_set.sem, 1)
                    elif name in ("score_a", "score_c"):
                        step = i if name == "score_a" else TT * A_KV + i
                        kind, qt, h, q_all = attention_of(step)
                        act.wait_ge(neg_top_set.sem, neg_top_set.at(layer, step + 1))
                        if step >= 3:
                            act.wait_ge(turn_done.sem, turn_done.at(layer, step - 2))
                        if kind == "a":
                            for hh in range(GROUP):
                                nc.scalar.activation(prob[step % 3][:, hh * P:(hh + 1) * P],
                                                     nat[i % 2][:, hh * P:(hh + 1) * P], ACT.Exp, scale=A_SCALE,
                                                     bias=neg_top[:, step % 2, hh:hh + 1],
                                                     accum_out=sums[:, qt, h * GROUP + hh:h * GROUP + hh + 1])
                            nc.scalar.activation(sink_exp[:, qt, h * GROUP:(h + 1) * GROUP], sink_in[:, step % 2, :],
                                                 ACT.Exp).then_inc(exp_done.sem, 1)
                        else:
                            n = (qt + 1) * P
                            nc.scalar.activation(prob[step % 3][:, 0:n], nat[i % 2][:, 0:n], ACT.Exp, scale=C_SCALE,
                                                 bias=neg_top[:, step % 2, 0:1],
                                                 accum_out=sums[:, qt, h:h + 1]).then_inc(exp_done.sem, 1)
                    elif name == "turn":
                        kind, qt, _, _ = attention_of(i)
                        n = (GROUP if kind == "a" else qt + 1) * P
                        act.wait_ge(turn_done.sem, turn_done.at(layer, i + 1))
                        if i >= 1:
                            act.wait_ge(value_done.sem, value_done.at(layer, i))
                        nc.scalar.activation(prob_t[:, 0:n], turn_bank[:, 0:n],
                                             ACT.Copy).then_inc(turn_out.sem, 1)
                    elif name == "y_hi":
                        act.wait_ge(aux_free.sem, aux_free.at(layer, AUX.index(("turn_y", i)) + 1))
                        if i % TT == 0:
                            act.wait_ge(proj_done.sem, proj_done.at(layer, signals_before(PO[i // TT] + 4)))
                        ts = slice((i % TT) * P, (i % TT + 1) * P)
                        nc.scalar.activation(y_hi[:, :, ts], y_pre[:, :].rearrange("p (f n) -> p f n", f=BR),
                                             ACT.Copy).then_inc(y_hi_set.sem, 1)
                    if (name, i) in AUX:
                        u += 1
            for j in range(KT):
                act.wait_ge(proj_free.sem, proj_free.at(DEPTH, j + 1 - KT))
                if j == KT - 1:
                    square(DEPTH, 1)
                nc.scalar.activation(gates[:, j, :], xt[:, j, :], ACT.Copy,
                                     scale=fin_g[:, j:j + 1]).then_inc(gained.sem, 1)
            rms_of(DEPTH, 0, 0, rstd[:, :], D, ln_ms)
            for j in range(DVE_TILES, KT):
                act.wait_ge(scaled_pool.sem, j - DVE_TILES + 1)
                act.dma_start(out_t[:, j, :], gates[:, j, :]).then_inc(out_sent[1].sem, 16)

        @block.vector
        def _(dve):
            def add_square(layer, n):
                dve.wait_ge(x_sq.sem, x_sq.at(layer, n))
                if n == 2:
                    nc.vector.tensor_copy(sq_sum, sq[0]).then_inc(x_acc.sem, 1)
                else:
                    dve.wait_ge(x_acc.sem, x_acc.at(layer, n - 1))
                    nc.vector.tensor_tensor(sq_sum, sq_sum, sq[n % 2], ALU.add).then_inc(x_acc.sem, 1)

            def refine(layer, u, place, y, n):
                dve.wait_ge(rough_set.sem, rough_set.at(layer, place + 1))
                nc.vector.tensor_tensor(y_nat[:, :], y, y, ALU.mult).then_inc(newton.sem, 1)
                dve.wait_ge(newton.sem, newton.at(layer, 2 * place + 1))
                nc.vector.scalar_tensor_tensor(y_nat[:, :], aux[:, :], n * EPS, y_nat[:, :], ALU.add,
                                               ALU.mult).then_inc(aux_free.sem, 1)
                dve.wait_ge(aux_free.sem, aux_free.at(layer, u + 1))
                nc.vector.tensor_scalar(y_nat[:, :], y_nat[:, :], -0.5 / n, 1.5, ALU.mult,
                                        ALU.add).then_inc(newton.sem, 1)
                dve.wait_ge(newton.sem, newton.at(layer, 2 * place + 2))
                return nc.vector.tensor_tensor(y, y_nat[:, :], y, ALU.mult)

            def rotary_products(layer, before, first, second_half, cos, sin, rows, last_reader=None):
                if before:
                    dve.wait_ge(rope_out.sem, rope_out.at(layer, before))
                ops = [(0, first, cos), (1, second_half, sin), (2, second_half, cos), (3, first, sin)]
                for n, (slot, half, table) in enumerate(ops):
                    last = nc.vector.tensor_tensor(work[rows, slot, :], half, table, ALU.mult)
                    last.then_inc(rope_prod.sem, 1)

            def evacuated(layer, p, n=1):
                dve.wait_ge(proj_done.sem, proj_done.at(layer, signals_before(p) + n))

            nc.vector.memset(eps[:, :], EPS).then_inc(eps_set.sem, 1)
            for free in (proj_free, aux_free, y_nat_set):
                dve.sem_inc(free.sem, free.before)
            for n in range(2, KT + 1):
                add_square(-1, n)
            with dve.Fori(0, DEPTH) as layer:
                u = 0
                for name, i in SCHEDULE:
                    if name == "split_x":
                        for j in range(KT):
                            dve.wait_ge(x_hi.sem, x_hi.at(layer, j + 1))
                            nc.vector.scalar_tensor_tensor(act_lo[:, j, :], xt[:, j, :], par[:, G_X + j:G_X + j + 1],
                                                           act_hi[:, j, :].bitcast(F32), ALU.mult,
                                                           ALU.subtract).then_inc(x_lo.sem, 1)
                        add_square(layer, 1)
                        nc.vector.tensor_scalar(neg_sink[:, :], par[:, SINKS:SINKS + A_HEADS], -1.0, None,
                                                ALU.mult).then_inc(sink_neg.sem, 1)
                        nc.vector.memset(ab1[96:128, :], 1.0).then_inc(ones_row.sem, 1)
                        nc.vector.memset(v_as[0:64, 0, :], 0.0).then_inc(v_cleared.sem, 1)
                    elif name == "rms":
                        refine(layer, u, 0, rstd[:, :], D).then_inc(rstd_set.sem, 1)
                        dve.wait_ge(rstd_set.sem, rstd_set.at(layer, 1))
                        dve.wait_ge(setup_loaded.sem, SETUP)
                        nc.vector.tensor_tensor(cos_r, rope[:, 0, :], rstd[:, :], ALU.mult).then_inc(rope_scaled.sem, 1)
                        nc.vector.tensor_tensor(sin_r, rope[:, 1, :], rstd[:, :], ALU.mult).then_inc(rope_scaled.sem, 1)
                    elif name == "rope_k":
                        dve.wait_ge(rope_scaled.sem, rope_scaled.at(layer, 2))
                        evacuated(layer, PY)
                        rx, ry = ring[first_output(PX) % 3], ring[first_output(PY) % 3]
                        rotary_products(layer, 0, rx[0:64, :], ry[0:64, :], cos_r[0:64, :], sin_r[0:64, :], slice(0, 64))
                        dve.wait_ge(ones_row.sem, ones_row.at(layer, 1))
                        nc.vector.tensor_tensor(ab1[64:112, :], rx[64:112, :], rstd[64:112, :],
                                                ALU.mult).then_inc(proj_free.sem, 1)
                        nc.vector.tensor_tensor(second[64:80, :], ry[64:80, :], rstd[64:80, :],
                                                ALU.mult).then_inc(proj_free.sem, 1)
                        dve.wait_ge(proj_free.sem, proj_free.at(layer, 2))
                        for g in range(A_KV):
                            rows = slice(32 * g, 32 * g + 32)
                            nc.vector.tensor_tensor(k_a[0:32, g, :], work[rows, 0, :], work[rows, 1, :],
                                                    ALU.subtract).then_inc(rope_out.sem, 1)
                            nc.vector.tensor_tensor(k_a[32:64, g, :], work[rows, 2, :], work[rows, 3, :],
                                                    ALU.add).then_inc(rope_out.sem, 1)
                        rows = slice(64, 80)
                        rotary_products(layer, 4, ab1[rows, :], second[rows, :], rope[rows, 2, :], rope[rows, 3, :], rows)
                        dve.wait_ge(rope_prod.sem, rope_prod.at(layer, 8))
                        nc.vector.tensor_tensor(second[rows, :], work[rows, 0, :], work[rows, 1, :],
                                                ALU.subtract).then_inc(rope_out.sem, 1)
                        dve.wait_ge(rope_out.sem, rope_out.at(layer, 5))
                        nc.vector.tensor_tensor(work[rows, 0, :], work[rows, 2, :], work[rows, 3, :],
                                                ALU.add).then_inc(rope_out.sem, 1)
                    elif name == "rstd_nat":
                        dve.wait_ge(aux_ready.sem, aux_ready.at(layer, u + 1))
                        nc.vector.tensor_copy(rstd_nat[:, :], aux[:, :].rearrange("p (t n) -> p t n", t=TT)[:, :, 0]
                                              ).then_inc(aux_free.sem, 1)
                    elif name == "gla_gate":
                        dve.wait_ge(gla_soft.sem, gla_soft.at(layer, 3 * i + 3))
                        nc.vector.scalar_tensor_tensor(
                            log_a[:, 2 * i:2 * i + 2, :].rearrange("p t n -> p (t n)"), aux[:, :], 0.0,
                            soft[:, 2 * i:2 * i + 2, :].rearrange("p t n -> p (t n)"), ALU.min,
                            ALU.subtract).then_inc(aux_free.sem, 1)
                    elif name == "latent_norm":
                        refine(layer, AUX.index(("latent", i)), 1 + i, lat_rstd, (C_QR, C_KVR)[i]).then_inc(lat_rs.sem, 1)
                        dve.wait_ge(lat_rs.sem, lat_rs.at(layer, i + 1))
                        for n in ((0, 1), (2,))[i]:
                            col = G_CQ + n
                            nc.vector.scalar_tensor_tensor(latent[:, n, :], latent[:, n, :], par[:, col:col + 1],
                                                           lat_rstd, ALU.mult, ALU.mult).then_inc(lat_norm.sem, 1)
                    elif name == "latent_lo":
                        for n in ((0, 1), (2,))[i]:
                            dve.wait_ge(lat_hi_set.sem, lat_hi_set.at(layer, n + 1))
                            nc.vector.tensor_tensor(lat_lo[:, n, :], latent[:, n, :], lat_hi[:, n, :].bitcast(F32),
                                                    ALU.subtract).then_inc(lat_lo_set.sem, 1)
                    elif name == "gla_state":
                        dve.wait_ge(state_in.sem, state_in.at(layer, i + 1))
                        if i == 0:
                            end = AUX.index(("gla_end", 0))
                            dve.wait_ge(aux_free.sem, aux_free.at(layer, end + 1))
                        for c in range(2 * i, 2 * i + 2):
                            for j in range(2):
                                new = nat[2 * (i % 2) + c % 2][:, j * P:(j + 1) * P]
                                if c == 0:
                                    nc.vector.tensor_copy(state[:, 0, j, :], new).then_inc(state_set.sem, 1)
                                else:
                                    dve.wait_ge(state_set.sem, state_set.at(layer, 2 * (c - 1) + j + 1))
                                    nc.vector.scalar_tensor_tensor(
                                        state[:, c, j, :], state[:, c - 1, j, :], decay[:, j * NC + c:j * NC + c + 1],
                                        new, ALU.mult, ALU.add).then_inc(state_set.sem, 1)
                    elif name == "silu":
                        b, j = divmod(i, BR)
                        dve.wait_ge(gate_tanh.sem, gate_tanh.at(layer, 12 * b + j + 1))
                        nc.vector.scalar_tensor_tensor(gates[:, j, :], gates[:, 8 + j, :], 1.0, gates[:, j, :], ALU.add,
                                                       ALU.mult).then_inc(silu_set.sem, 1)
                    elif name == "gla_out":
                        refine(layer, AUX.index(("gla_norm", i)), 3 + i, o_rstd, B_DV).then_inc(read_rs.sem, 1)
                        dve.wait_ge(read_rs.sem, read_rs.at(layer, i + 1))
                        nc.vector.tensor_tensor(work[:, i % 2, :], nat[i][:, :], o_rstd, ALU.mult
                                                ).then_inc(read_norm.sem, 1)
                        dve.wait_ge(read_norm.sem, read_norm.at(layer, i + 1))
                        if i == 0:
                            dve.wait_ge(silu_set.sem, silu_set.at(layer, BR))
                        nc.vector.scalar_tensor_tensor(work[:, 2 + i % 2, :], work[:, i % 2, :], par[:, G_BH:G_BH + 1],
                                                       gates[:, i, :], ALU.mult, ALU.mult).then_inc(y_pre_set.sem, 1)
                    elif name == "gla_lo":
                        dve.wait_ge(y_hi_set.sem, y_hi_set.at(layer, i + 1))
                        nc.vector.tensor_tensor(y_lo[:, i, :], work[:, 2 + i % 2, :], y_hi[:, i, :].bitcast(F32),
                                                ALU.subtract).then_inc(y_lo_set.sem, 1)
                    elif name in ("score_a", "score_c"):
                        step = i if name == "score_a" else TT * A_KV + i
                        kind, qt, h, q_all = attention_of(step)
                        par2 = step % 2
                        bank = nat[i % 2]
                        dve.wait_ge(scores_done.sem, scores_done.at(layer, step + 1))
                        if kind == "a":
                            sc = bank[:, :].rearrange("p (h n) -> p h n", h=GROUP)
                            if qt == 0:
                                nc.vector.memset(sc[0:64, :, 0:64], NEG).then_inc(masked.sem, 1)
                                dve.wait_ge(masked.sem, masked.at(layer, step + 1))
                            nc.vector.tensor_reduce(top[:, par2, :], sc, AX_X, ALU.max,
                                                    negate=True).then_inc(top_set.sem, 1)
                            dve.wait_ge(top_set.sem, top_set.at(layer, 2 * step + 1))
                            heads = slice(h * GROUP, (h + 1) * GROUP)
                            nc.vector.scalar_tensor_tensor(neg_top[:, par2, :], top[:, par2, :], A_SCALE,
                                                           neg_sink[:, heads], ALU.mult,
                                                           ALU.min).then_inc(top_set.sem, 1)
                            dve.wait_ge(top_set.sem, top_set.at(layer, 2 * step + 2))
                            nc.vector.tensor_tensor(sink_in[:, par2, :], neg_top[:, par2, :], neg_sink[:, heads],
                                                    ALU.subtract).then_inc(neg_top_set.sem, 1)
                        else:
                            n = (qt + 1) * P
                            nc.vector.memset(bank[0:64, n - 64:n], NEG).then_inc(masked.sem, 1)
                            dve.wait_ge(masked.sem, masked.at(layer, A_KV + i + 1))
                            nc.vector.tensor_reduce(top[:, par2, 0:1], bank[:, 0:n], AX_X, ALU.max,
                                                    negate=True).then_inc(top_set.sem, 1)
                            dve.wait_ge(top_set.sem, top_set.at(layer, 2 * TT * A_KV + i + 1))
                            nc.vector.tensor_scalar(neg_top[:, par2, 0:1], top[:, par2, 0:1], C_SCALE, None,
                                                    ALU.mult).then_inc(neg_top_set.sem, 1)
                    elif name == "turn_y":
                        b = 1 + i // TT
                        dve.wait_ge(aux_ready.sem, aux_ready.at(layer, u + 1))
                        dve.wait_ge(silu_set.sem, silu_set.at(layer, BR * (b + 1)))
                        if i > 0:
                            dve.wait_ge(y_hi_set.sem, y_hi_set.at(layer, BR + i))
                        ts = slice((i % TT) * P, (i % TT + 1) * P)
                        pre = y_pre[:, :].rearrange("p (f n) -> p f n", f=BR)
                        nc.vector.tensor_tensor(pre, aux[:, :].rearrange("p (f n) -> p f n", f=BR),
                                                gates[:, 0:BR, ts], ALU.mult).then_inc(aux_free.sem, 1)
                    elif name == "y_lo":
                        ts = slice((i % TT) * P, (i % TT + 1) * P)
                        pre = y_pre[:, :].rearrange("p (f n) -> p f n", f=BR)
                        dve.wait_ge(y_hi_set.sem, y_hi_set.at(layer, BR + i + 1))
                        nc.vector.tensor_tensor(y_lo[:, :, ts], pre, y_hi[:, :, ts].bitcast(F32),
                                                ALU.subtract).then_inc(y_lo_set.sem, 1)
                    elif name in ("value_a", "value_c"):
                        step = i if name == "value_a" else TT * A_KV + i
                        kind, qt, h, q_all = attention_of(step)
                        if h == (A_KV if kind == "a" else C_HEADS) - 1:
                            dve.wait_ge(value_done.sem, value_done.at(layer, step + 1))
                            total = sums[:, qt, :]
                            if kind == "a":
                                nc.vector.tensor_tensor(recip[:, :], total, sink_exp[:, qt, :],
                                                        ALU.add).then_inc(denom_set.sem, 1)
                                dve.wait_ge(denom_set.sem, denom_set.at(layer, 2 * qt + 1))
                                nc.vector.reciprocal(recip[:, :], recip[:, :]).then_inc(denom_set.sem, 1)
                                dve.wait_ge(denom_set.sem, denom_set.at(layer, 2 * qt + 2))
                            else:
                                nc.vector.reciprocal(recip[:, :], total).then_inc(denom_set.sem, 1)
                                dve.wait_ge(denom_set.sem, denom_set.at(layer, 2 * TT + qt + 1))
                            if q_all > 0:
                                v = AUX.index(("turn_y", q_all - 1))
                                dve.wait_ge(aux_ready.sem, aux_ready.at(layer, v + 1))
                            nc.vector.tensor_tensor(y_nat[:, :].rearrange("p (h n) -> p h n", h=A_HEADS),
                                                    o_bank[:, :].rearrange("p (h n) -> p h n", h=A_HEADS),
                                                    recip[:, :].unsqueeze(2).broadcast_to([P, A_HEADS, A_DH]),
                                                    ALU.mult).then_inc(y_nat_set.sem, 1)
                    elif name == "quarter" and i % 4 == 3:
                        p = i // 4
                        res = ring[first_output(p) % 3][:, :]
                        g = gate_index(p)
                        if g is not None:
                            b, j = g
                            evacuated(layer, p)
                            if j >= 8:
                                dve.wait_ge(silu_set.sem, silu_set.at(layer, BR * b + j - 8 + 1))
                            nc.vector.scalar_tensor_tensor(gates[:, j, :], res, 0.5, rstd[:, :], ALU.mult,
                                                           ALU.mult).then_inc(proj_free.sem, 1)
                        elif p in (PQA + 1, PQA + 3):
                            n = (p - PQA) // 2
                            evacuated(layer, p)
                            ra, rb = (ring[first_output(q) % 3][:, :] for q in (p - 1, p))
                            if n == 0:
                                dve.wait_ge(k_rope_saved.sem, k_rope_saved.at(layer, 32))
                            dve.wait_ge(rope_out.sem, rope_out.at(layer, 6 + 8 * n))
                            nc.vector.tensor_tensor(work[:, 0, :], ra, cos_r, ALU.mult).then_inc(rope_prod.sem, 1)
                            nc.vector.tensor_tensor(work[:, 3, :], ra, sin_r, ALU.mult).then_inc(proj_free.sem, 1)
                            nc.vector.tensor_tensor(work[:, 1, :], rb, sin_r, ALU.mult).then_inc(rope_prod.sem, 1)
                            nc.vector.tensor_tensor(work[:, 2, :], rb, cos_r, ALU.mult).then_inc(proj_free.sem, 1)
                            dve.wait_ge(proj_free.sem, proj_free.at(layer, first_output(p) + 1))
                            for hh in range(4):
                                h = 4 * n + hh
                                rows = slice(32 * hh, 32 * hh + 32)
                                nc.vector.tensor_tensor(q_a[0:32, h, :], work[rows, 0, :],
                                                        work[rows, 1, :], ALU.subtract).then_inc(rope_out.sem, 1)
                                nc.vector.tensor_tensor(q_a[32:64, h, :], work[rows, 2, :],
                                                        work[rows, 3, :], ALU.add).then_inc(rope_out.sem, 1)
                        elif p == PN1 + 3:
                            evacuated(layer, p)
                            for t in range(TT):
                                nc.vector.scalar_tensor_tensor(k_dec[:, t, :], nat[t][:, 0:256], rstd_nat[:, t:t + 1],
                                                               dec[:, t, :], ALU.mult, ALU.mult)
                                nc.vector.tensor_scalar(v_a[:, t, :], nat[t][:, 256:384], rstd_nat[:, t:t + 1], None,
                                                        ALU.mult).then_inc(nat_free.sem, 1)
                        elif p == PN2 + 3:
                            evacuated(layer, p)
                            for t in range(TT):
                                nc.vector.tensor_scalar(v_b[:, t, :], nat[t][:, :], rstd_nat[:, t:t + 1], None,
                                                        ALU.mult).then_inc(nat_free.sem, 1)
                        elif PQB <= p < PQB + 2:
                            evacuated(layer, p)
                            nc.vector.scalar_tensor_tensor(q_b[:, p - PQB, :], res, B_DK ** -0.5, rstd[:, :], ALU.mult,
                                                           ALU.mult).then_inc(proj_free.sem, 1)
                        elif PCQ <= p <= PCKV:
                            evacuated(layer, p)
                            nc.vector.tensor_tensor(latent[:, p - PCQ, :], res, rstd[:, :],
                                                    ALU.mult).then_inc(proj_free.sem, 1)
                            if p == PCQ + 1:
                                dve.wait_ge(lat_sq.sem, lat_sq.at(layer, 2))
                                nc.vector.tensor_tensor(sq_sum, sq[0], sq[1], ALU.add).then_inc(lat_acc.sem, 1)
                        elif p in range(PO[0], PO[0] + 4) or p in range(PO[1], PO[1] + 4) or p in range(PO[2], PO[2] + 4):
                            b = [o <= p < o + 4 for o in PO].index(True)
                            for o in range(2):
                                j = 2 * (p - PO[b]) + o
                                evacuated(layer, p, o + 1)
                                z = ring[(first_output(p) + o) % 3][:, :]
                                dve.wait_ge(gate_tanh.sem, gate_tanh.at(layer, 12 * b + 4 + j + 1))
                                tile = gates[:, 4 + j, :]
                                nc.vector.scalar_tensor_tensor(merged[:, j, :] if b == 0 else tile, tile, 1.0, z,
                                                               ALU.add, ALU.mult).then_inc(proj_free.sem, 1)
                                dve.wait_ge(proj_free.sem, proj_free.at(layer, first_output(p) + o + 1))
                                if b > 0:
                                    nc.vector.tensor_tensor(merged[:, j, :], merged[:, j, :], tile,
                                                            ALU.add).then_inc(merged_set.sem, 1)
                            if b == 2:
                                for o in range(2):
                                    j = 2 * (p - PO[b]) + o
                                    dve.wait_ge(merge_hi.sem, merge_hi.at(layer, j + 1))
                                    nc.vector.scalar_tensor_tensor(act_lo[:, j, :], merged[:, j, :], 0.5,
                                                                   act_hi[:, j, :].bitcast(F32), ALU.mult,
                                                                   ALU.subtract).then_inc(merge_lo.sem, 1)
                        elif p == PUKV:
                            dve.wait_ge(read_done.sem, read_done.at(layer, B_HEADS))
                            dve.wait_ge(value_done.sem, value_done.at(layer, TT * A_KV))
                            for o in range(8):
                                evacuated(layer, p, o + 1)
                                r = ring[(first_output(p) + o) % 3]
                                if o < 4:
                                    nc.vector.tensor_copy(v_c[:, o, :], r[:, :]).then_inc(proj_free.sem, 1)
                                else:
                                    h = 2 * (o - 4)
                                    nc.vector.tensor_copy(k_c[0:64, h, :], r[0:64, :])
                                    nc.vector.tensor_copy(k_c[0:64, h + 1, :], r[64:128, :]).then_inc(proj_free.sem, 1)
                        elif p in (PUQ, PUQ + 1):
                            if p == PUQ:
                                evacuated(layer, p, 2)
                                f = first_output(p)
                                ra, rb = ring[f % 3][:, :], ring[(f + 1) % 3][:, :]
                                cos, sin = rope[:, 2, :], rope[:, 3, :]
                                nc.vector.tensor_tensor(work[:, 0, :], ra, cos, ALU.mult).then_inc(rope_prod.sem, 1)
                                nc.vector.tensor_tensor(work[:, 3, :], ra, sin, ALU.mult).then_inc(proj_free.sem, 1)
                                nc.vector.tensor_tensor(work[:, 1, :], rb, sin, ALU.mult).then_inc(rope_prod.sem, 1)
                                nc.vector.tensor_tensor(work[:, 2, :], rb, cos, ALU.mult).then_inc(proj_free.sem, 1)
                                dve.wait_ge(proj_free.sem, proj_free.at(layer, f + 2))
                                nc.vector.tensor_tensor(work[:, 0, :], work[:, 0, :], work[:, 1, :],
                                                        ALU.subtract).then_inc(rope_out.sem, 1)
                                nc.vector.tensor_tensor(work[:, 2, :], work[:, 2, :], work[:, 3, :],
                                                        ALU.add).then_inc(rope_out.sem, 1)
                            for o in ((2,) if p == PUQ else (0, 1, 2)):
                                evacuated(layer, p, o + 1)
                                r = ring[(first_output(p) + o) % 3]
                                h = 0 if p == PUQ else 2 * (o + 1)
                                nc.vector.tensor_copy(q_c[0:64, h, :], r[0:64, :])
                                nc.vector.tensor_copy(q_c[0:64, h + 1, :], r[64:128, :]).then_inc(proj_free.sem, 1)
                        elif p >= PW:
                            evacuated(layer, p)
                            nc.vector.tensor_tensor(xt[:, p - PW, :], xt[:, p - PW, :], res,
                                                    ALU.add).then_inc(proj_free.sem, 1)
                            if p > PW:
                                add_square(layer, p - PW + 1)
                    if (name, i) in AUX:
                        u += 1
            add_square(DEPTH, 1)
            refine(DEPTH, 0, 0, rstd[:, :], D).then_inc(rstd_set.sem, 1)
            dve.wait_ge(rstd_set.sem, rstd_set.at(DEPTH, 1))
            for j in range(DVE_TILES):
                dve.wait_ge(gained.sem, j + 1)
                nc.vector.tensor_tensor(gates[:, j, :], gates[:, j, :], rstd[:, :], ALU.mult).then_inc(scaled_dve.sem, 1)


def pack_pieces(w_in, w_oa, w_ob, w_oc, w_uq, w_ukv, w_out):
    off = dict(zip(("qa", "ka", "va", "ga", "qb", "kb", "vb", "ab", "gb", "cq", "ckv", "kr", "gc", "mg"),
                   np.cumsum([0, 512, 128, 128, 512, 256, 256, 512, 16, 512, 256, 128, 32, 512])))
    out = np.zeros((DEPTH, PIECES, P, 1024), w_in.dtype)

    def put(layer, p, w, cols, tiles=None):
        w = w[:, cols].reshape(-1, P, len(cols))
        w = w if tiles is None else w[tiles]
        out[layer, p, :, :w.shape[0] * w.shape[2]] = w.transpose(1, 0, 2).reshape(P, -1)

    for l in range(DEPTH):
        w = w_in[l]
        for p, half in ((PX, 0), (PY, 1)):
            ka = [off["ka"] + 64 * g + 32 * half + r for g in range(A_KV) for r in range(32)]
            kr = [off["kr"] + 16 * half + r for r in range(16)]
            tile = out[l, p].reshape(P, KT, P)
            src = w.reshape(KT, P, -1).transpose(1, 0, 2)
            tile[:, :, 0:64] = src[:, :, ka]
            tile[:, :, 64:80] = src[:, :, kr]
            if half == 0:
                tile[:, :, 96:112] = src[:, :, off["ab"]:off["ab"] + B_RANK]
        for n in range(2):
            for half in range(2):
                put(l, PQA + 2 * n + half, w, [off["qa"] + 64 * (4 * n + h) + 32 * half + r
                                               for h in range(4) for r in range(32)])
        for n in range(4):
            put(l, PN1 + n, w, [*range(off["kb"], off["kb"] + 256), *range(off["va"], off["va"] + 128)],
                slice(2 * n, 2 * n + 2))
            put(l, PN2 + n, w, list(range(off["vb"], off["vb"] + 512)), slice(2 * n, 2 * n + 2))
        for n in range(2):
            put(l, PQB + n, w, list(range(off["qb"] + P * n, off["qb"] + P * n + P)))
            put(l, PCQ + n, w, list(range(off["cq"] + P * n, off["cq"] + P * n + P)))
        put(l, PCKV, w, list(range(off["ckv"], off["ckv"] + P)))
        for b, (gate, branch, wo) in enumerate((("gb", 1, w_ob), ("ga", 0, w_oa), ("gc", 2, w_oc))):
            for n in range(4):
                put(l, PG[b] + n, w, list(range(off[gate] + P * n, off[gate] + P * n + P)))
                put(l, PO[b] + n, wo[l], list(range(256 * n, 256 * n + 256)))
            for n in range(8):
                c = off["mg"] + D * branch + P * n
                put(l, PM[b] + n, w, list(range(c, c + P)))
        kv = C_NOPE + C_V
        put(l, PUKV, w_ukv[l], [kv * h + C_NOPE + r for h in range(C_HEADS) for r in range(C_V)]
            and [kv * h + r for h in range(C_HEADS) for r in range(C_NOPE)]
            + [kv * h + C_NOPE + r for h in range(C_HEADS) for r in range(C_V)])
        first = [C_DH * h + C_NOPE + r for h in range(C_HEADS) for r in range(16)]
        nope = [C_DH * h + r for h in range(C_HEADS) for r in range(C_NOPE)]
        put(l, PUQ, w_uq[l], first + [c + 16 for c in first] + nope[0:P])
        put(l, PUQ + 1, w_uq[l], nope[P:])
        for n in range(KT):
            put(l, PW + n, w_out[l], list(range(P * n, P * n + P)))
    return out.reshape(DEPTH * PIECES, P, 1024)


def rotary_tables():
    out = np.zeros((P, 4, S), np.float32)
    pos = np.arange(S, dtype=np.float32)
    for n, dim in enumerate((A_DH, C_ROPE)):
        inv = (10000.0 ** (-np.arange(0, dim, 2) / dim)).astype(np.float32)
        ang = (inv[:, None] * pos[None, :]).astype(np.float32)
        reps = P // len(inv)
        out[:, 2 * n] = np.tile(np.cos(ang), (reps, 1))
        out[:, 2 * n + 1] = np.tile(np.sin(ang), (reps, 1))
    return out


def constant_table():
    t = np.arange(P)
    same = t[:, None] // CHUNK == t[None, :] // CHUNK
    out = np.zeros((P, CONSTS), np.float32)
    out[:, ONES:ONES + P] = 1.0
    out[:, IDENT:IDENT + P] = np.eye(P)
    out[:, LATER:LATER + P] = (same & (t[:, None] > t[None, :])) / B_TAU
    out[:, MEMBER:MEMBER + 2] = (t[:, None] // CHUNK == np.arange(2)[None, :]) / B_TAU
    return out


def kernel(x, norm_g, w_in, a_sinks, w_oa, w_alpha, b_alpha, b_head_g, w_ob, cq_g, w_uq, ckv_g, w_ukv, w_oc, w_out,
           final_g):
    import concourse.bacc as bacc
    from concourse.bass_utils import run_bass_kernel_spmd

    (x, norm_g, w_in, a_sinks, w_oa, w_alpha, b_alpha, b_head_g, w_ob, cq_g, w_uq, ckv_g, w_ukv, w_oc, w_out,
     final_g) = (np.asarray(a) for a in (x, norm_g, w_in, a_sinks, w_oa, w_alpha, b_alpha, b_head_g, w_ob, cq_g, w_uq,
                                         ckv_g, w_ukv, w_oc, w_out, final_g))
    params = np.zeros((P, DEPTH, PARAMS), x.dtype)
    for l in range(DEPTH):
        params[:, l, G_X:G_X + KT] = norm_g[l].reshape(KT, P).T
        params[:, l, G_BH] = b_head_g[l]
        params[:, l, G_CQ:G_CQ + 2] = cq_g[l].reshape(2, P).T
        params[:, l, G_CKV] = ckv_g[l]
        params[:, l, SINKS:SINKS + A_HEADS] = a_sinks[l][None, :]
    arrays = {
        "x_t": np.ascontiguousarray(x[0].T.reshape(KT, P, S).transpose(1, 0, 2)),
        "pieces": pack_pieces(w_in, w_oa, w_ob, w_oc, w_uq, w_ukv, w_out),
        "params": params,
        "alpha": np.ascontiguousarray(np.concatenate([w_alpha, b_alpha[:, None, :]], axis=1).transpose(1, 0, 2)),
        "tables": rotary_tables(),
        "consts": constant_table(),
        "final_gain": np.ascontiguousarray(final_g.reshape(KT, P).T),
    }
    nc = bacc.Bacc("TRN2", target_bir_lowering=False, num_devices=1, dynamic_dma_scratch_size=1024)
    aps = [nc.dram_tensor(name, a.shape, mybir.dt.from_np(a.dtype), kind="ExternalInput").ap()
           for name, a in arrays.items()]
    out_t = nc.dram_tensor("out_t", (P, KT, S), F32, kind="ExternalOutput").ap()
    k_rope_dram = nc.dram_tensor("k_rope_dram", (C_ROPE, S), F32, kind="Internal").ap()
    q_rope_dram = nc.dram_tensor("q_rope_dram", (2, P, S), F32, kind="Internal").ap()
    build_hybrid_trunk(nc, *aps, out_t, k_rope_dram, q_rope_dram)
    r = run_bass_kernel_spmd(nc, [arrays], core_ids=[0])
    got = r.results[0]["out_t"]
    return np.ascontiguousarray(got.transpose(1, 0, 2).reshape(D, S).T)[None]
```

```python
from contextlib import ExitStack

import numpy as np

import concourse.bass as bass
from concourse import mybir

F32 = mybir.dt.float32
F32R = mybir.dt.float32r
ALU = mybir.AluOpType
ACT = mybir.ActivationFunctionType
AX_X = mybir.AxisListType.X

DEPTH, D, S, CHUNK, P = 2, 1024, 512, 64, 128
EPS, NEG = 1e-6, -1e30
KT = D // P
TT = S // P
NC = S // CHUNK
A_HEADS, A_KV, A_DH = 8, 2, 64
GROUP = A_HEADS // A_KV
B_HEADS, B_DK, B_DV, B_RANK, B_TAU = 4, 64, 128, 16, 16.0
C_HEADS, C_QR, C_KVR, C_NOPE, C_ROPE, C_V = 8, 256, 128, 64, 32, 64
C_DH = C_NOPE + C_ROPE
A_SCALE, C_SCALE = A_DH ** -0.5, C_DH ** -0.5
BR = 512 // P

PX, PY = 0, 1
PQA = 2
PN1 = 6
PQB = 10
PCQ, PCKV = 12, 14
PN2 = 15
PG = [19, 35, 54]
PM = [23, 39, 58]
PO = [31, 50, 66]
PUKV, PUQ = 47, 48
PW = 70
PIECES = 78
RAW = HL = 3
assert PIECES % RAW == 0
LATE = 2
WARM = 20


def outputs_of(p):
    if PN1 <= p < PN1 + 4 or PN2 <= p < PN2 + 4:
        return 0
    if any(o <= p < o + 4 for o in PO):
        return 2
    return {PUKV: 8, PUQ: 3, PUQ + 1: 3}.get(p, 1)


def first_output(p):
    return sum(outputs_of(q) for q in range(p))


def signals_before(p):
    return sum(max(outputs_of(q), 1) for q in range(p))


def gate_index(p):
    for b in range(3):
        if PG[b] <= p < PG[b] + 4:
            return b, p - PG[b]
        if PM[b] <= p < PM[b] + 8:
            return b, 4 + p - PM[b]
    return None


def make_schedule():
    todo = [("split_x", 0)]

    def piece(*ps):
        for p in ps:
            for q in range(4):
                todo.append(("quarter", 4 * p + q))

    def half(p, n):
        todo.extend(("quarter", 4 * p + 2 * n + q) for q in range(2))

    def step(*names):
        for name, i in names:
            todo.append((name, i))

    piece(PX)
    step(("rms", 0))
    piece(PY)
    step(("rope_k", 0))
    piece(PQA)
    step(("rstd_nat", 0))
    piece(PQA + 1, PQA + 2)
    step(("gla_gate", 0))
    piece(PQA + 3)
    step(("gla_gate", 1))
    piece(PN1, PN1 + 1)
    step(("gla_decay", 0))
    piece(PN1 + 2)
    step(("gla_decay", 1))
    piece(PN1 + 3)
    step(("gla_end", 0))
    piece(PQB, PQB + 1, PCQ, PCQ + 1, PCKV, PN2)
    step(("latent", 0))
    piece(PN2 + 1)
    step(("latent_norm", 0), ("latent", 1), ("latent_hi", 0))
    piece(PN2 + 2)
    step(("latent_norm", 1), ("latent_lo", 0), ("latent_hi", 1))
    piece(PN2 + 3)
    g, m = PG[0], PM[0]
    piece(g)
    step(("latent_lo", 1), ("tanh", 0), ("gla_state", 0))
    half(g + 1, 0)
    step(("gla_state", 1))
    half(g + 1, 1)
    step(("tanh", 1), ("silu", 0), ("gla_state", 2))
    half(g + 2, 0)
    step(("gla_state", 3))
    half(g + 2, 1)
    step(("tanh", 2), ("silu", 1))
    piece(g + 3)
    step(("tanh", 3), ("silu", 2))
    for q in range(4):
        step(("gla_read", q), ("quarter", 4 * m + q))
    step(("silu", 3))
    for h in range(B_HEADS + 1):
        if h < B_HEADS:
            step(("gla_norm", h))
        quarters_of = [("quarter", 4 * (m + 1 + h) + q) for q in range(4)]
        todo.extend(quarters_of[:3])
        if h < B_HEADS:
            step(("gla_out", h))
        step(quarters_of[3])
        if h < B_HEADS:
            step(("gla_hi", h))
        if h >= 1:
            step(("gla_lo", h - 1))
    step(*(("tanh", 4 + j) for j in range(6)))
    piece(m + 6)
    step(("tanh", 10))
    piece(m + 7)
    step(("tanh", 11))

    def quarters(n):
        for _ in range(min(n, len(fill))):
            q = fill.pop(0)
            todo.append(("quarter", q))
            g = gate_index(q // 4)
            if q % 4 == 3 and g is not None:
                b, j = g
                todo.append(("tanh", 12 * b + j))
                if 1 <= j <= BR:
                    todo.append(("silu", BR * b + j - 1))

    fill = [4 * p + q for p in [*range(PO[0], PO[0] + 4), *range(PG[1], PG[1] + 12)] for q in range(4)]
    na = TT * A_KV
    quarters(28)
    for s in range(na + 3):
        y, last = divmod(s - 3, A_KV)
        if s >= 3:
            todo.append(("value_a", s - 3))
        if 2 <= s < na + 2:
            todo.append(("turn", s - 2))
        if s < na:
            todo.append(("score_a", s))
        quarters(1)
        if y >= 1 and last == 0:
            todo.append(("y_lo", y - 1))
        quarters(1)
        if y >= 0 and last:
            todo.append(("y_hi", y))
        quarters(1)
        if s < na:
            todo.append(("divide", s))
    quarters(len(fill))
    todo.append(("y_lo", TT - 1))
    piece(PUKV, PUQ, PUQ + 1, *range(PO[1], PO[1] + 4))
    fill = [4 * p + q for p in range(PG[2], PG[2] + 12) for q in range(4)]
    nc_ = TT * C_HEADS
    quarters(10)
    for i in range(nc_ + 3):
        if 2 <= i < nc_ + 2:
            todo.append(("turn", na + i - 2))
        if 1 <= i <= nc_:
            todo.append(("divide", na + i - 1))
        if i < nc_:
            todo.append(("score_c", i))
        if i >= 4 and i % 2 == 0:
            todo.append(("value_c", (i - 4) // 2))
        quarters(1)
        y, h = divmod(i - 3 + 1, C_HEADS)
        if y >= 1 and h < 2:
            todo.append((("y_hi", "y_lo")[h], TT + y - 1))
    quarters(len(fill) - 1)
    todo.append(("y_lo", 2 * TT - 1))
    quarters(1)
    piece(*range(PO[2], PO[2] + 4), *range(PW, PW + KT))
    return todo


SCHEDULE = make_schedule()
AUX = [s for s in SCHEDULE if s[0] in ("rms", "rstd_nat", "gla_gate", "gla_decay", "gla_end", "latent",
                                       "gla_norm")]

G_X, G_BH, G_CQ, G_CKV, SINKS = 0, 8, 9, 11, 12
PARAMS = 20
ONES, IDENT, LATER, MEMBER = 0, 128, 256, 384
CONSTS = 386


class Signal:

    def __init__(self, ctx, nc, name, per_layer, before=0):
        self.sem = ctx.enter_context(nc.semaphore(name))
        self.per_layer, self.before = per_layer, before

    def at(self, layer, n):
        assert n > 0 or self.before > 0, "a wait on a register's value needs it above zero"
        return layer * self.per_layer + (self.before + max(n, 1 - self.before))


def build_hybrid_trunk(nc, x_t, pieces, params, alpha, tables, consts, final_g, out_t, k_rope_dram, q_rope_dram):
    with ExitStack() as ctx:
        def sb(name, shape, dt=F32):
            return ctx.enter_context(nc.sbuf_tensor(name, shape, dt))

        def sig(name, per_layer, before=0):
            return Signal(ctx, nc, name, per_layer, before)

        xt = sb("xt", [P, KT, S])
        act_hi = sb("act_hi", [P, KT, S], F32R)
        act_lo = sb("act_lo", [P, KT, S], F32R)
        raw = sb("raw", [P, RAW, 1024])
        w_hi = sb("w_hi", [P, HL, 1024], F32R)
        w_lo = sb("w_lo", [P, HL, 1024], F32R)
        gates = sb("gates", [P, 12, S])
        merged = sb("merged", [P, KT, S])
        y_hi = sb("y_hi", [P, BR, S], F32R)
        y_lo = sb("y_lo", [P, BR, S], F32R)
        bank_g = sb("bank_g", [P, 4096])
        bank_a = sb("bank_a", [P, 6144])
        lat_hi = sb("lat_hi", [P, 3, S], F32R)
        lat_lo = sb("lat_lo", [P, 3, S], F32R)
        rope = sb("rope", [P, 4, S])
        rstd = sb("rstd", [P, S])
        work = sb("work", [P, 7, S])
        y_pre = sb("y_pre", [P, S])
        con = sb("con", [P, CONSTS])
        par_all = sb("par_all", [P, DEPTH, PARAMS])
        par = sb("par", [P, PARAMS])
        alpha_all = sb("alpha_all", [P, DEPTH, B_HEADS * B_DK])
        fin_g = sb("fin_g", [P, KT])
        eps = sb("eps", [P, 1])
        rstd_nat = sb("rstd_nat", [P, TT])
        decay = sb("decay", [P, 2 * NC])
        neg_sink = sb("neg_sink", [P, A_HEADS])
        top = sb("top", [P, 2, GROUP])
        neg_top = sb("neg_top", [P, 2, GROUP])
        sink_in = sb("sink_in", [P, 2, GROUP])
        sink_exp = sb("sink_exp", [P, TT, A_HEADS])
        sums = sb("sums", [P, TT, A_HEADS])
        recip = sb("recip", [P, A_HEADS])

        ones, ident = con[:, ONES:ONES + P], con[:, IDENT:IDENT + P]
        later, member = con[:, LATER:LATER + P], con[:, MEMBER:MEMBER + 2]
        prob, prob_t = [work[:, i, :] for i in range(3)], [work[:, 3 + i, :] for i in range(4)]
        k_dec = bank_g[:, 0:1024].rearrange("p (t n) -> p t n", t=TT)
        v_b = bank_g[:, 1024:3072].rearrange("p (t n) -> p t n", t=TT)
        q_b = bank_g[:, 3072:4096].rearrange("p (t n) -> p t n", t=2)
        k_c = bank_g[:, :].rearrange("p (h n) -> p h n", h=C_HEADS)
        q_a = bank_a[0:64, 0:4096].rearrange("p (h n) -> p h n", h=A_HEADS)
        k_a = bank_a[0:64, 4096:5120].rearrange("p (t n) -> p t n", t=2)
        v_a = bank_a[:, 5120:5632].rearrange("p (t n) -> p t n", t=TT)
        v_as = bank_a[:, 5632:6144].rearrange("p (t n) -> p t n", t=TT)
        q_c = bank_a[:, 0:4096].rearrange("p (h n) -> p h n", h=C_HEADS)
        v_c = bank_a[:, 4096:6144].rearrange("p (t n) -> p t n", t=TT)
        sq = [merged[:, 0, :], merged[:, 1, :]]
        sq_sum, ln_ms, ab1, second = merged[:, 2, :], merged[:, 3, :], merged[:, 4, :], merged[:, 5, :]
        lat_rstd = merged[:, 6, :]
        state = merged[:, 0:4, :].rearrange("p a (c j v) -> p (a c) j v", c=2, j=2)
        o_sq = [merged[:, 4, :], merged[:, 5, :]]
        o_ln, o_rstd = merged[:, 6, :], merged[:, 7, :]
        cos_r, sin_r = gates[:, 0, :], gates[:, 1, :]
        latent = gates[:, 2:5, :]
        w_alpha = gates[:, 5, 0:B_HEADS * B_DK]
        dec = gates[:, 6:8, :].rearrange("p a (t n) -> p (a t) n", t=2)
        soft = gates[:, 8:10, :].rearrange("p a (t n) -> p (a t) n", t=2)
        log_a = gates[:, 10:12, :].rearrange("p a (t n) -> p (a t) n", t=2)

        ring = [ctx.enter_context(nc.psum_tensor(f"ring{i}", [P, S], F32)) for i in range(3)]
        nat = [ctx.enter_context(nc.psum_tensor(f"nat{i}", [P, S], F32)) for i in range(4)]
        aux = ctx.enter_context(nc.psum_tensor("aux", [P, S], F32))
        turn_bank, o_bank = nat[2], nat[3]
        o_t = o_bank[:, :].rearrange("p (f n) -> p f n", f=BR)

        raw_loaded = [sig(f"raw_loaded{i}", 16 * PIECES // RAW) for i in range(RAW)]
        par_loaded, setup_loaded = sig("par_loaded", 0), sig("setup_loaded", 0)
        x_loaded = [sig(f"x_loaded{i}", 0) for i in range(KT // 2)]
        eps_set = sig("eps_set", 0)
        hi_split, lo_split = sig("hi_split", PIECES), sig("lo_split", PIECES)
        proj_done = sig("proj_done", signals_before(PIECES), HL + 1)
        proj_free = sig("proj_free", first_output(PIECES), KT)
        par_set = sig("par_set", 2)
        x_hi, x_lo = sig("x_hi", KT), sig("x_lo", KT)
        ACT_TILES = 4
        x_sq, x_acc = sig("x_sq", KT, ACT_TILES), sig("x_acc", KT, KT - LATE)
        dve_sq = sig("dve_sq", 0)
        warm_set = sig("warm_set", 0)
        act_used = sig("act_used", 3, 3)
        aux_ready, aux_free = sig("aux_ready", len(AUX)), sig("aux_free", len(AUX), 1)
        n_norms = 3 + B_HEADS
        log_set, rough_set, newton = sig("log_set", n_norms), sig("rough_set", n_norms), sig("newton", 2 * n_norms)
        rstd_set = sig("rstd_set", 1)
        ones_row = sig("ones_row", 1)
        rope_scaled = sig("rope_scaled", 2)
        rope_prod, rope_out = sig("rope_prod", 14), sig("rope_out", 24)
        k_rope_saved, k_rope_placed = sig("k_rope_saved", 32), sig("k_rope_placed", 16)
        q_rope_saved, q_rope_placed = sig("q_rope_saved", 32), sig("q_rope_placed", 32)
        gla_soft = sig("gla_soft", 6)
        nat_free = sig("nat_free", 8)
        v_cleared, v_shifted = sig("v_cleared", 1), sig("v_shifted", 32)
        lat_sq, lat_acc, lat_rs = sig("lat_sq", 3), sig("lat_acc", 1), sig("lat_rs", 2)
        lat_norm, lat_hi_set, lat_lo_set = sig("lat_norm", 3), sig("lat_hi_set", 3), sig("lat_lo_set", 3)
        state_in, state_set = sig("state_in", 4), sig("state_set", 2 * NC)
        read_done, read_sq, read_rs = sig("read_done", 4), sig("read_sq", B_HEADS), sig("read_rs", B_HEADS)
        read_norm = sig("read_norm", B_HEADS)
        y_pre_set, y_hi_set, y_lo_set = sig("y_pre_set", B_HEADS), sig("y_hi_set", 12), sig("y_lo_set", 12)
        gate_tanh, silu_set = sig("gate_tanh", 36), sig("silu_set", 12)
        n_steps = TT * A_KV + TT * C_HEADS
        scores_done = sig("scores_done", n_steps)
        masked = sig("masked", A_KV + TT * C_HEADS)
        top_set = sig("top_set", 2 * TT * A_KV + TT * C_HEADS)
        neg_top_set, exp_done = sig("neg_top_set", n_steps), sig("exp_done", n_steps)
        turn_done, turn_out, value_done = (sig("turn_done", n_steps), sig("turn_out", n_steps),
                                           sig("value_done", TT * A_KV + TT * C_HEADS // 2))
        denom_set, divided = sig("denom_set", 2 * TT * A_KV + TT * C_HEADS), sig("divided", n_steps)
        o_read = sig("o_read", 2 * TT, 1)
        sink_neg = sig("sink_neg", 1)
        merged_set = sig("merged_set", 2 * KT)
        merge_hi, merge_lo = sig("merge_hi", KT), sig("merge_lo", KT)
        gained, scaled_dve, scaled_pool = sig("gained", 0), sig("scaled_dve", 0), sig("scaled_pool", 0)
        out_sent = [sig("out_sent_sp", 0), sig("out_sent_act", 0)]
        DVE_TILES = 6

        def attention_of(step):
            if step < TT * A_KV:
                return "a", step // A_KV, step % A_KV, step // A_KV
            c = step - TT * A_KV
            return "c", c // C_HEADS, c % C_HEADS, TT + c // C_HEADS

        LN_EXP = "natural_log_exp_and_others"
        SETUP = 16 * 4
        block = ctx.enter_context(nc.Block())

        @block.sync
        def _(sp):
            for i in range(RAW):
                if i == 1:
                    sp.wait_ge(x_loaded[0].sem, 16)
                sp.dma_start(raw[:, i, :], pieces[i]).then_inc(raw_loaded[i].sem, 16)
                if i == 1:
                    sp.dma_start(rope[:, :, :], tables).then_inc(setup_loaded.sem, 16)
            with sp.Fori(1, DEPTH * PIECES // RAW) as group:
                for i in range(RAW):
                    sp.wait_ge(lo_split.sem, group * RAW + (i - RAW + 1))
                    sp.dma_start(raw[:, i, :], pieces[group * RAW + i]).then_inc(raw_loaded[i].sem, 16)
            for j in range(DVE_TILES):
                sp.wait_ge(scaled_dve.sem, j + 1)
                sp.dma_start(out_t[:, j, :], gates[:, j, :]).then_inc(out_sent[0].sem, 16)
            sp.wait_ge(out_sent[0].sem, 16 * DVE_TILES)
            sp.wait_ge(out_sent[1].sem, 16 * (KT - DVE_TILES))

        @block.gpsimd
        def _(pool):
            with pool.Fori(0, DEPTH * PIECES // RAW) as group:
                for i in range(RAW):
                    pool.wait_ge(hi_split.sem, group * RAW + (i + 1))
                    nc.gpsimd.tensor_tensor(w_lo[:, i, :], raw[:, i, :], w_hi[:, i, :].bitcast(F32),
                                            ALU.subtract).then_inc(lo_split.sem, 1)
            pool.wait_ge(rstd_set.sem, rstd_set.at(DEPTH, 1))
            for j in range(DVE_TILES, KT):
                pool.wait_ge(gained.sem, j + 1)
                nc.gpsimd.tensor_tensor(gates[:, j, :], gates[:, j, :], rstd[:, :],
                                        ALU.mult).then_inc(scaled_pool.sem, 1)

        @block.tensor
        def _(pe):
            def project(layer, quarter):
                p, part = divmod(quarter, 4)
                slot = p % HL
                whi, wlo = w_hi[:, slot, :], w_lo[:, slot, :]
                if part == 0:
                    pe.wait_ge(lo_split.sem, lo_split.at(layer, p + 1))
                natural = PN1 <= p < PN1 + 4 or PN2 <= p < PN2 + 4
                n_out = outputs_of(p)
                if natural:
                    first, n_k, width = (PN1, 2, 384) if p < PQB else (PN2, 2, 512)
                    jobs = [(t, 2 * (p - first) + k, k) for k in range(2) for t in range(TT)]
                elif p == PUKV:
                    jobs = [(o, 0, 0) for o in range(8)]
                elif p in (PUQ, PUQ + 1):
                    jobs = [(o, k, k) for o in range(3) for k in range(2)]
                elif n_out == 2:
                    jobs = [(o, k, k) for o in range(2) for k in range(BR)]
                else:
                    jobs = [(0, k, k) for k in range(KT)]
                lo, hi = len(jobs) * part // 4, len(jobs) * (part + 1) // 4
                for n in range(lo, hi):
                    o, k, kw = jobs[n]
                    if natural:
                        bank = nat[o]
                        start, stop = k == 0, k == KT - 1
                        if start:
                            if first == PN2:
                                pe.wait_ge(nat_free.sem, nat_free.at(layer, o + 1))
                            elif o == 0:
                                pe.wait_ge(o_read.sem, o_read.at(layer, 0))
                        dst = bank[:, 0:width]
                        wv = slice(kw * width, (kw + 1) * width)
                        ops = [(act_hi[:, k, o * P:(o + 1) * P], whi[:, wv]),
                               (act_lo[:, k, o * P:(o + 1) * P], whi[:, wv]),
                               (act_hi[:, k, o * P:(o + 1) * P], wlo[:, wv])]
                        done = n == len(jobs) - 1
                    else:
                        r = first_output(p) + o
                        dst = ring[r % 3][:, :]
                        last_k = {PUKV: 0, PUQ: 1, PUQ + 1: 1}.get(p, BR - 1 if n_out == 2 else KT - 1)
                        start, stop = k == 0, k == last_k
                        done = stop
                        if start:
                            pe.wait_ge(proj_free.sem, proj_free.at(layer, r - 2))
                        if p == PUKV and o < 4:
                            ts = slice(o * P, (o + 1) * P)
                            wv = slice(512, 1024)
                            ops = [(lat_hi[:, 2, ts], whi[:, wv]), (lat_lo[:, 2, ts], whi[:, wv]),
                                   (lat_hi[:, 2, ts], wlo[:, wv])]
                        else:
                            if p == PUKV:
                                xh, xl, col = lat_hi[:, 2, :], lat_lo[:, 2, :], (o - 4) * P
                            elif p in (PUQ, PUQ + 1):
                                xh, xl, col = lat_hi[:, k, :], lat_lo[:, k, :], (k * 3 + o) * P
                            elif n_out == 2:
                                xh, xl, col = y_hi[:, k, :], y_lo[:, k, :], (k * 2 + o) * P
                            else:
                                xh, xl, col = act_hi[:, k, :], act_lo[:, k, :], k * P
                            wv = slice(col, col + P)
                            ops = [(whi[:, wv], xh), (whi[:, wv], xl), (wlo[:, wv], xh)]
                    if p == PX:
                        pe.wait_ge(x_lo.sem, x_lo.at(layer, k + 1))
                    elif p == PW:
                        pe.wait_ge(merge_lo.sem, merge_lo.at(layer, k + 1))
                    elif p == PUKV and n == 0:
                        pe.wait_ge(lat_lo_set.sem, lat_lo_set.at(layer, 3))
                    elif p in PO and n == 0:
                        pe.wait_ge(y_lo_set.sem, y_lo_set.at(layer, BR * (PO.index(p) + 1)))
                    for i, (stationary, moving) in enumerate(ops):
                        mm = pe.matmul(dst, stationary, moving, start=start and i == 0, stop=stop and i == 2)
                    if done:
                        mm.then_inc(proj_done.sem, 1)
                if p == PIECES - 1 and part < 3:
                    mm.then_inc(act_used.sem, 1)

            def aux_bank(layer, u):
                pe.wait_ge(aux_free.sem, aux_free.at(layer, u))

            pe.wait_ge(warm_set.sem, 1)
            for _ in range(WARM):
                pe.matmul(aux[:, 0:256], o_rstd[:, 0:P], o_rstd[:, 0:256], start=True, stop=True)
            pe.sem_inc(proj_done.sem, proj_done.before)
            pe.sem_inc(act_used.sem, act_used.before)
            with pe.Fori(0, DEPTH) as layer:
                u = 0
                for name, i in SCHEDULE:
                    if name == "quarter":
                        project(layer, i)
                        continue
                    if (name, i) == ("rms", 0):
                        aux_bank(layer, u)
                        pe.wait_ge(setup_loaded.sem, SETUP)
                        pe.wait_ge(x_acc.sem, x_acc.at(layer, LATE))
                        mm = pe.matmul(aux[:, :], ones, sq_sum, start=True, stop=True)
                    elif name == "rstd_nat":
                        aux_bank(layer, u)
                        pe.wait_ge(rstd_set.sem, rstd_set.at(layer, 1))
                        for t in range(TT):
                            mm = pe.transpose(aux[:, t * P:(t + 1) * P], rstd[:, t * P:(t + 1) * P], ident)
                    elif name == "gla_gate":
                        aux_bank(layer, u)
                        pe.wait_ge(proj_free.sem, proj_free.at(layer, first_output(PX) + 1))
                        for t in range(2):
                            ts = slice((2 * i + t) * P, (2 * i + t + 1) * P)
                            mm = pe.matmul(aux[:, t * 256:(t + 1) * 256], ab1[96:96 + B_RANK + 1, ts],
                                           w_alpha[96:96 + B_RANK + 1, :], start=True, stop=True)
                    elif name == "gla_decay":
                        aux_bank(layer, u)
                        for t in range(2):
                            mm = pe.matmul(aux[:, t * 256:(t + 1) * 256], later, log_a[:, 2 * i + t, :],
                                           start=True, stop=True)
                    elif name == "gla_end":
                        aux_bank(layer, u)
                        for j in range(2):
                            for t in range(TT):
                                mm = pe.matmul(aux[:, j * NC + 2 * t:j * NC + 2 * t + 2],
                                               log_a[:, t, j * P:(j + 1) * P], member, start=True, stop=True)
                    elif name == "latent":
                        aux_bank(layer, u)
                        if i == 0:
                            pe.wait_ge(lat_acc.sem, lat_acc.at(layer, 1))
                        else:
                            pe.wait_ge(lat_sq.sem, lat_sq.at(layer, 3))
                        mm = pe.matmul(aux[:, :], ones, sq_sum if i == 0 else sq[0], start=True, stop=True)
                    elif name == "gla_state":
                        ready, n = (nat_free, 8) if i < 2 else (state_set, 4 * (i - 1))
                        value = pe.snap(ready.at(layer, n))
                        pe.lower_val(value)
                        pe.wait_ge(setup_loaded.sem, SETUP)
                        pe.wait_ge(ready.sem, value)
                        for j in range(B_HEADS // 2):
                            for c, h in ((c, 2 * j + r) for c in range(2) for r in range(2)):
                                rows = slice(CHUNK * c, CHUNK * (c + 1))
                                bank = nat[2 * (i % 2) + c]
                                half = slice(64 * (h % 2), 64 * (h % 2) + 64)
                                col = j * P
                                mm = pe.matmul(bank[half, col:col + P], k_dec[rows, i, h * B_DK:(h + 1) * B_DK],
                                               v_b[rows, i, h * B_DV:(h + 1) * B_DV], start=True, stop=True)
                        mm.then_inc(state_in.sem, 1)
                    elif name == "gla_read":
                        if i == 0:
                            pe.wait_ge(state_set.sem, state_set.at(layer, 2 * NC))
                        pair, part = divmod(i, 2)
                        for c in range(NC // 2 * part, NC // 2 * (part + 1)):
                            cs = slice(CHUNK * c, CHUNK * (c + 1))
                            for h in range(2):
                                half = slice(64 * h, 64 * h + 64)
                                mm = pe.matmul(nat[2 * pair + h][:, cs], state[half, c, pair, :], q_b[half, pair, cs],
                                               start=True, stop=True)
                        mm.then_inc(read_done.sem, 1)
                    elif name == "gla_norm":
                        aux_bank(layer, u)
                        pe.wait_ge(read_sq.sem, read_sq.at(layer, i + 1))
                        mm = pe.matmul(aux[:, :], ones, o_sq[i % 2], start=True, stop=True)
                    elif name == "score_a":
                        qt, g = divmod(i, A_KV)
                        ready, n = (read_norm, B_HEADS) if i < 2 else (exp_done, i - 1)
                        value = pe.snap(ready.at(layer, n))
                        pe.lower_val(value)
                        pe.wait_ge(setup_loaded.sem, SETUP)
                        pe.wait_ge(ready.sem, value)
                        bank = nat[i % 2]
                        for hh in range(GROUP):
                            h = g * GROUP + hh
                            for c in range(2):
                                q0 = qt * P + c * CHUNK
                                k0, skip = (q0 - CHUNK, 0) if q0 else (0, CHUNK)
                                mm = pe.matmul(bank[c * 64:c * 64 + 64, hh * P + skip:(hh + 1) * P],
                                               q_a[:, h, q0:q0 + CHUNK],
                                               k_a[:, g, k0:q0 + CHUNK], start=True, stop=True)
                        mm.then_inc(scores_done.sem, 1)
                    elif name == "score_c":
                        qt, h = divmod(i, C_HEADS)
                        step, n = TT * A_KV + i, (qt + 1) * P
                        pe.wait_ge(exp_done.sem, exp_done.at(layer, step - 1))
                        if i == 0:
                            pe.wait_ge(proj_free.sem, proj_free.at(layer, first_output(PUQ + 2)))
                            pe.wait_ge(k_rope_placed.sem, k_rope_placed.at(layer, 16))
                            pe.wait_ge(q_rope_placed.sem, q_rope_placed.at(layer, 32))
                        mm = pe.matmul(nat[i % 2][:, 0:n], q_c[0:C_DH, h, qt * P:(qt + 1) * P],
                                       k_c[0:C_DH, h, 0:n], start=True, stop=True)
                        mm.then_inc(scores_done.sem, 1)
                    elif name == "turn":
                        kind, qt, h, _ = attention_of(i)
                        pe.wait_ge(divided.sem, divided.at(layer, i + 1))
                        if i > 0:
                            pe.wait_ge(turn_out.sem, turn_out.at(layer, i))
                        for b in range(GROUP if kind == "a" else qt + 1):
                            mm = pe.transpose(turn_bank[:, b * P:(b + 1) * P], prob[i % 3][:, b * P:(b + 1) * P], ident)
                        mm.then_inc(turn_done.sem, 1)
                    elif name == "value_a":
                        _, qt, h, q_all = attention_of(i)
                        if i == 0:
                            pe.wait_ge(v_shifted.sem, v_shifted.at(layer, 32))
                        if h == 0 and q_all > 0:
                            pe.wait_ge(o_read.sem, o_read.at(layer, q_all))
                        pe.wait_ge(turn_out.sem, turn_out.at(layer, i + 1))
                        pt = prob_t[i % 4].rearrange("p (a r c n) -> p r c a n", a=2, r=2, c=2)
                        for c in range(2):
                            for r in range(2):
                                mm = pe.matmul(o_t[r * 64:r * 64 + 64, 2 * h:2 * h + 2, c * 64:c * 64 + 64],
                                               (v_as, v_a)[c][:, qt, h * A_DH:(h + 1) * A_DH], pt[:, r, c],
                                               start=True, stop=True)
                        mm.then_inc(value_done.sem, 1)
                    elif name == "value_c":
                        qt, f = divmod(i, C_HEADS // 2)
                        if f == 0:
                            pe.wait_ge(o_read.sem, o_read.at(layer, TT + qt))
                        step = TT * A_KV + 2 * i
                        pe.wait_ge(turn_out.sem, turn_out.at(layer, step + 2))
                        for b in range(qt + 1):
                            for r in range(2):
                                h = 2 * f + r
                                mm = pe.matmul(o_t[r * 64:r * 64 + 64, f, :], v_c[:, b, h * C_V:(h + 1) * C_V],
                                               prob_t[(step + r) % 4][:, b * P:(b + 1) * P], start=b == 0, stop=b == qt)
                        mm.then_inc(value_done.sem, 1)
                    if (name, i) in AUX:
                        mm.then_inc(aux_ready.sem, 1)
                        u += 1
            pe.wait_ge(x_acc.sem, x_acc.at(DEPTH, LATE - 1))
            pe.wait_ge(aux_free.sem, aux_free.at(DEPTH, 0))
            pe.matmul(aux[:, :], ones, sq_sum, start=True, stop=False)
            pe.wait_ge(x_sq.sem, x_sq.at(DEPTH, LATE))
            pe.matmul(aux[:, :], ones, sq[LATE % 2], start=False, stop=True).then_inc(aux_ready.sem, 1)

        @block.scalar
        def _(act):
            def split_hi(layer, p):
                i = p % RAW
                act.wait_ge(raw_loaded[i].sem, raw_loaded[i].at(layer, 16 * (p // RAW + 1)))
                act.wait_ge(proj_done.sem, proj_done.at(layer, signals_before(p - HL + 1) if p >= HL else p - HL + 1))
                nc.scalar.activation(w_hi[:, p % HL, :], raw[:, i, :], ACT.Copy).then_inc(hi_split.sem, 1)

            def rms_of(layer, u, place, dst, n, tmp):
                act.wait_ge(aux_ready.sem, aux_ready.at(layer, u + 1))
                nc.scalar.activation(tmp, aux[:, :], ACT.Ln, scale=1.0 / n, bias=eps[:, 0:1]).then_inc(log_set.sem, 1)
                act.wait_ge(log_set.sem, log_set.at(layer, place + 1))
                nc.scalar.activation(dst, tmp, ACT.Exp, scale=-0.5).then_inc(rough_set.sem, 1)

            def square(layer, n, buffer_used=True):
                if buffer_used:
                    act.wait_ge(x_acc.sem, x_acc.at(layer, n - 2))
                nc.scalar.activation(sq[n % 2], xt[:, (n - 1 - LATE) % KT, :], ACT.Square).then_inc(x_sq.sem, 1)

            act.dma_start(par_all[:, :, :], params).then_inc(par_loaded.sem, 16)
            for j in range(KT // 2):
                act.dma_start(xt[:, 2 * j:2 * j + 2, :], x_t[:, 2 * j:2 * j + 2, :]).then_inc(x_loaded[j].sem, 16)
            act.dma_start(con[:, :], consts).then_inc(setup_loaded.sem, 16)
            act.dma_start(alpha_all[96:96 + B_RANK + 1, :, :], alpha).then_inc(setup_loaded.sem, 16)
            act.dma_start(fin_g[:, :], final_g).then_inc(setup_loaded.sem, 16)
            act.wait_ge(par_loaded.sem, 16)
            for n in range(LATE + 1, LATE + 1 + ACT_TILES):
                act.wait_ge(x_loaded[(n - 1 - LATE) // 2].sem, 16)
                square(-1, n, buffer_used=n > LATE + 2)
            with act.Fori(0, DEPTH) as layer:
                u = 0
                for name, i in SCHEDULE:
                    if name == "split_x":
                        nc.scalar.activation(par[:, :], par_all[:, bass.ds(layer, 1), :].rearrange("p a n -> p (a n)"),
                                             ACT.Copy).then_inc(par_set.sem, 1)
                        split_hi(layer, 0)
                        act.wait_ge(par_set.sem, par_set.at(layer, 1))
                        for j in range(KT):
                            act.wait_ge(x_loaded[j // 2].sem, 16)
                            act.wait_ge(proj_free.sem, proj_free.at(layer, j + 1 - KT))
                            if j < 6:
                                act.wait_ge(act_used.sem, act_used.at(layer, j // 2 - 2))
                            elif j == 6:
                                act.wait_ge(proj_done.sem, proj_done.at(layer, 0))
                            nc.scalar.activation(act_hi[:, j, :], xt[:, j, :], ACT.Copy,
                                                 scale=par[:, G_X + j:G_X + j + 1]).then_inc(x_hi.sem, 1)
                            if j == 2:
                                split_hi(layer, 1)
                        for n in range(1, LATE + 1):
                            square(layer, n)
                        split_hi(layer, 2)
                        act.wait_ge(setup_loaded.sem, SETUP)
                        nc.scalar.activation(w_alpha[96:96 + B_RANK + 1, :],
                                             alpha_all[96:96 + B_RANK + 1, bass.ds(layer, 1), :].rearrange(
                                                 "p a n -> p (a n)"), ACT.Copy).then_inc(par_set.sem, 1)
                    elif name == "quarter" and i % 4 == 3:
                        p = i // 4
                        if p + HL < PIECES:
                            split_hi(layer, p + HL)
                        if p in (PCQ, PCQ + 1, PCKV):
                            n = p - PCQ
                            act.wait_ge(proj_free.sem, proj_free.at(layer, first_output(p) + 1))
                            if n == 2:
                                act.wait_ge(lat_acc.sem, lat_acc.at(layer, 1))
                            elif n == 0:
                                act.wait_ge(x_acc.sem, x_acc.at(layer, LATE))
                            nc.scalar.activation(sq[n % 2], latent[:, n, :], ACT.Square).then_inc(lat_sq.sem, 1)
                        if p >= PO[2] and p < PO[2] + 4:
                            for o in range(2):
                                j = 2 * (p - PO[2]) + o
                                act.wait_ge(merged_set.sem, merged_set.at(layer, KT + j + 1))
                                nc.scalar.activation(act_hi[:, j, :], merged[:, j, :], ACT.Copy,
                                                     scale=0.5).then_inc(merge_hi.sem, 1)
                        if PW < p <= PW + KT - LATE:
                            act.wait_ge(proj_free.sem, proj_free.at(layer, first_output(p)))
                            square(layer, LATE + p - PW)
                        if p == PUKV:
                            act.wait_ge(k_rope_saved.sem, k_rope_saved.at(layer, 32))
                            act.wait_ge(read_done.sem, read_done.at(layer, 4))
                            act.dma_start(k_c[C_NOPE:C_DH, :, :],
                                          k_rope_dram.unsqueeze(1).broadcast_to([C_ROPE, C_HEADS, S])
                                          ).then_inc(k_rope_placed.sem, 16)
                        if p == PUQ:
                            act.wait_ge(rope_out.sem, rope_out.at(layer, 24))
                            for half in range(2):
                                act.dma_start(q_rope_dram[half], work[:, 2 * half, :]).then_inc(q_rope_saved.sem, 16)
                            act.wait_ge(q_rope_saved.sem, q_rope_saved.at(layer, 32))
                            for half in range(2):
                                rows = slice(C_NOPE + 16 * half, C_NOPE + 16 * half + 16)
                                act.dma_start(q_c[rows, :, :], q_rope_dram[half].rearrange("(h r) n -> r h n", h=C_HEADS)
                                              ).then_inc(q_rope_placed.sem, 16)
                        if p == PQA:
                            act.wait_ge(rope_out.sem, rope_out.at(layer, 6))
                            act.dma_start(k_rope_dram[0:16, :], second[64:80, :]).then_inc(k_rope_saved.sem, 16)
                            act.dma_start(k_rope_dram[16:32, :], work[64:80, 0, :]).then_inc(k_rope_saved.sem, 16)
                        if p == PN1 + 3:
                            act.wait_ge(nat_free.sem, nat_free.at(layer, 4))
                            act.wait_ge(v_cleared.sem, v_cleared.at(layer, 1))
                            act.dma_start(v_as[0:64, 1:TT, :], v_a[64:128, 0:TT - 1, :]).then_inc(v_shifted.sem, 16)
                            act.dma_start(v_as[64:128, :, :], v_a[0:64, :, :]).then_inc(v_shifted.sem, 16)
                    elif name == "tanh":
                        b, j = divmod(i, 12)
                        p = PG[b] + j if j < 4 else PM[b] + j - 4
                        act.wait_ge(proj_free.sem, proj_free.at(layer, first_output(p) + 1))
                        nc.scalar.activation(gates[:, j if j >= 4 else 8 + j, :], gates[:, j, :],
                                             ACT.Tanh).then_inc(gate_tanh.sem, 1)
                    elif name == "rms":
                        nc.scalar.preload_act_table_set(LN_EXP)
                        rms_of(layer, u, 0, rstd[:, :], D, ln_ms)
                    elif name == "gla_gate":
                        act.wait_ge(aux_ready.sem, aux_ready.at(layer, u + 1))
                        tile = soft[:, 2 * i:2 * i + 2, :].rearrange("p t n -> p (t n)")
                        nc.scalar.activation(tile, aux[:, :], ACT.Abs).then_inc(gla_soft.sem, 1)
                        act.wait_ge(gla_soft.sem, gla_soft.at(layer, 3 * i + 1))
                        nc.scalar.activation(tile, tile, ACT.Exp, scale=-1.0).then_inc(gla_soft.sem, 1)
                        act.wait_ge(gla_soft.sem, gla_soft.at(layer, 3 * i + 2))
                        nc.scalar.activation(tile, tile, ACT.Ln, bias=1.0).then_inc(gla_soft.sem, 1)
                    elif name == "gla_decay":
                        act.wait_ge(aux_ready.sem, aux_ready.at(layer, u + 1))
                        nc.scalar.activation(dec[:, 2 * i:2 * i + 2, :].rearrange("p t n -> p (t n)"), aux[:, :],
                                             ACT.Exp).then_inc(aux_free.sem, 1)
                    elif name == "gla_end":
                        act.wait_ge(aux_ready.sem, aux_ready.at(layer, u + 1))
                        nc.scalar.activation(decay[:, :], aux[:, 0:2 * NC], ACT.Exp).then_inc(aux_free.sem, 1)
                    elif name == "latent":
                        if i == 1:
                            act.wait_ge(lat_norm.sem, lat_norm.at(layer, 2))
                        rms_of(layer, u, 1 + i, lat_rstd, (C_QR, C_KVR)[i], ln_ms)
                    elif name == "latent_hi":
                        for n in ((0, 1), (2,))[i]:
                            act.wait_ge(lat_norm.sem, lat_norm.at(layer, n + 1))
                            nc.scalar.activation(lat_hi[:, n, :], latent[:, n, :], ACT.Copy).then_inc(lat_hi_set.sem, 1)
                    elif name == "gla_read":
                        act.wait_ge(read_done.sem, read_done.at(layer, i + 1))
                        if i == 1:
                            for h in range(2):
                                nc.scalar.activation(o_sq[h], nat[h][:, :], ACT.Square).then_inc(read_sq.sem, 1)
                    elif name == "gla_norm":
                        if i == 0:
                            nc.scalar.preload_act_table_set(LN_EXP)
                        else:
                            act.wait_ge(read_norm.sem, read_norm.at(layer, i))
                        rms_of(layer, u, 3 + i, o_rstd, B_DV, o_ln)
                        if i + 2 < B_HEADS:
                            nc.scalar.activation(o_sq[i % 2], nat[i + 2][:, :], ACT.Square).then_inc(read_sq.sem, 1)
                    elif name == "gla_hi":
                        act.wait_ge(y_pre_set.sem, y_pre_set.at(layer, i + 1))
                        nc.scalar.activation(y_hi[:, i, :], work[:, 2 + i % 2, :], ACT.Copy).then_inc(y_hi_set.sem, 1)
                    elif name in ("score_a", "score_c"):
                        step = i if name == "score_a" else TT * A_KV + i
                        kind, qt, h, q_all = attention_of(step)
                        act.wait_ge(neg_top_set.sem, neg_top_set.at(layer, step + 1))
                        if step >= 3:
                            act.wait_ge(turn_done.sem, turn_done.at(layer, step - 2))
                        if kind == "a":
                            for hh in range(GROUP):
                                nc.scalar.activation(prob[step % 3][:, hh * P:(hh + 1) * P],
                                                     nat[i % 2][:, hh * P:(hh + 1) * P], ACT.Exp, scale=A_SCALE,
                                                     bias=neg_top[:, step % 2, hh:hh + 1],
                                                     accum_out=sums[:, qt, h * GROUP + hh:h * GROUP + hh + 1])
                            nc.scalar.activation(sink_exp[:, qt, h * GROUP:(h + 1) * GROUP], sink_in[:, step % 2, :],
                                                 ACT.Exp).then_inc(exp_done.sem, 1)
                        else:
                            n = (qt + 1) * P
                            nc.scalar.activation(prob[step % 3][:, 0:n], nat[i % 2][:, 0:n], ACT.Exp, scale=C_SCALE,
                                                 bias=neg_top[:, step % 2, 0:1],
                                                 accum_out=sums[:, qt, h:h + 1]).then_inc(exp_done.sem, 1)
                    elif name == "turn":
                        kind, qt, _, _ = attention_of(i)
                        n = (GROUP if kind == "a" else qt + 1) * P
                        act.wait_ge(turn_done.sem, turn_done.at(layer, i + 1))
                        if i >= 4:
                            user, n_a = i - 4, TT * A_KV
                            used = user + 1 if user < n_a else n_a + (user - n_a) // 2 + 1
                            act.wait_ge(value_done.sem, value_done.at(layer, used))
                        nc.scalar.activation(prob_t[i % 4][:, 0:n], turn_bank[:, 0:n],
                                             ACT.Copy).then_inc(turn_out.sem, 1)
                    elif name == "y_hi":
                        act.wait_ge(o_read.sem, o_read.at(layer, i + 1))
                        if i % TT == 0:
                            act.wait_ge(proj_done.sem, proj_done.at(layer, signals_before(PO[i // TT] + 4)))
                        ts = slice((i % TT) * P, (i % TT + 1) * P)
                        nc.scalar.activation(y_hi[:, :, ts], y_pre[:, :].rearrange("p (f n) -> p f n", f=BR),
                                             ACT.Copy).then_inc(y_hi_set.sem, 1)
                    if (name, i) in AUX:
                        u += 1
            nc.scalar.preload_act_table_set(LN_EXP)
            for j in range(KT):
                act.wait_ge(proj_free.sem, proj_free.at(DEPTH, j + 1 - KT))
                if j >= KT - LATE:
                    square(DEPTH, j - (KT - LATE) + 1)
                nc.scalar.activation(gates[:, j, :], xt[:, j, :], ACT.Copy,
                                     scale=fin_g[:, j:j + 1]).then_inc(gained.sem, 1)
            rms_of(DEPTH, 0, 0, rstd[:, :], D, ln_ms)
            for j in range(DVE_TILES, KT):
                act.wait_ge(scaled_pool.sem, j - DVE_TILES + 1)
                act.dma_start(out_t[:, j, :], gates[:, j, :]).then_inc(out_sent[1].sem, 16)

        @block.vector
        def _(dve):
            def add_square(layer, n):
                dve.wait_ge(x_sq.sem, x_sq.at(layer, n))
                add(layer, n)

            def add(layer, n):
                if n == LATE + 1:
                    nc.vector.tensor_copy(sq_sum, sq[n % 2]).then_inc(x_acc.sem, 1)
                else:
                    dve.wait_ge(x_acc.sem, x_acc.at(layer, n - 1))
                    nc.vector.tensor_tensor(sq_sum, sq_sum, sq[n % 2], ALU.add).then_inc(x_acc.sem, 1)

            def refine(layer, u, place, y, n):
                dve.wait_ge(rough_set.sem, rough_set.at(layer, place + 1))
                nc.vector.tensor_tensor(y_pre[:, :], y, y, ALU.mult).then_inc(newton.sem, 1)
                dve.wait_ge(newton.sem, newton.at(layer, 2 * place + 1))
                nc.vector.scalar_tensor_tensor(y_pre[:, :], aux[:, :], n * EPS, y_pre[:, :], ALU.add,
                                               ALU.mult).then_inc(aux_free.sem, 1)
                dve.wait_ge(aux_free.sem, aux_free.at(layer, u + 1))
                nc.vector.tensor_scalar(y_pre[:, :], y_pre[:, :], -0.5 / n, 1.5, ALU.mult,
                                        ALU.add).then_inc(newton.sem, 1)
                dve.wait_ge(newton.sem, newton.at(layer, 2 * place + 2))
                return nc.vector.tensor_tensor(y, y_pre[:, :], y, ALU.mult)

            def rotary_products(layer, before, first, second_half, cos, sin, rows):
                if before:
                    dve.wait_ge(rope_out.sem, rope_out.at(layer, before))
                ops = [(0, first, cos), (1, second_half, sin), (2, second_half, cos), (3, first, sin)]
                for n, (slot, half, table) in enumerate(ops):
                    last = nc.vector.tensor_tensor(work[rows, slot, :], half, table, ALU.mult)
                    last.then_inc(rope_prod.sem, 1)

            def evacuated(layer, p, n=1):
                dve.wait_ge(proj_done.sem, proj_done.at(layer, signals_before(p) + n))

            def gate_branch(layer, i):
                dve.wait_ge(silu_set.sem, silu_set.at(layer, BR * (2 + i // TT)))
                if i > 0:
                    dve.wait_ge(y_lo_set.sem, y_lo_set.at(layer, BR + i))
                ts = slice((i % TT) * P, (i % TT + 1) * P)
                return nc.vector.tensor_tensor(y_pre[:, :].rearrange("p (f n) -> p f n", f=BR),
                                               o_t, gates[:, 0:BR, ts], ALU.mult)

            nc.vector.memset(o_rstd, 0.0).then_inc(warm_set.sem, 1)
            nc.vector.memset(eps[:, :], EPS).then_inc(eps_set.sem, 1)
            for free in (proj_free, aux_free, o_read):
                dve.sem_inc(free.sem, free.before)
            for n in range(LATE + 1, KT + 1):
                tile = n - 1 - LATE
                if tile < ACT_TILES:
                    dve.wait_ge(x_sq.sem, tile + 1)
                else:
                    dve.wait_ge(x_loaded[tile // 2].sem, 16)
                    dve.wait_ge(x_acc.sem, x_acc.at(-1, n - 2))
                    nc.vector.tensor_tensor(sq[n % 2], xt[:, tile, :], xt[:, tile, :], ALU.mult
                                            ).then_inc(dve_sq.sem, 1)
                    dve.wait_ge(dve_sq.sem, tile - ACT_TILES + 1)
                add(-1, n)
            with dve.Fori(0, DEPTH) as layer:
                u = 0
                for name, i in SCHEDULE:
                    if name == "split_x":
                        for j in range(KT):
                            dve.wait_ge(x_hi.sem, x_hi.at(layer, j + 1))
                            nc.vector.scalar_tensor_tensor(act_lo[:, j, :], xt[:, j, :], par[:, G_X + j:G_X + j + 1],
                                                           act_hi[:, j, :].bitcast(F32), ALU.mult,
                                                           ALU.subtract).then_inc(x_lo.sem, 1)
                        for n in range(1, LATE + 1):
                            add_square(layer, n)
                        nc.vector.tensor_scalar(neg_sink[:, :], par[:, SINKS:SINKS + A_HEADS], -1.0, None,
                                                ALU.mult).then_inc(sink_neg.sem, 1)
                        nc.vector.memset(ab1[96:128, :], 1.0).then_inc(ones_row.sem, 1)
                        nc.vector.memset(v_as[0:64, 0, :], 0.0).then_inc(v_cleared.sem, 1)
                    elif name == "rms":
                        refine(layer, u, 0, rstd[:, :], D).then_inc(rstd_set.sem, 1)
                        dve.wait_ge(rstd_set.sem, rstd_set.at(layer, 1))
                        dve.wait_ge(setup_loaded.sem, SETUP)
                        nc.vector.tensor_tensor(cos_r, rope[:, 0, :], rstd[:, :], ALU.mult).then_inc(rope_scaled.sem, 1)
                        nc.vector.tensor_tensor(sin_r, rope[:, 1, :], rstd[:, :], ALU.mult).then_inc(rope_scaled.sem, 1)
                    elif name == "rope_k":
                        dve.wait_ge(rope_scaled.sem, rope_scaled.at(layer, 2))
                        evacuated(layer, PY)
                        rx, ry = ring[first_output(PX) % 3], ring[first_output(PY) % 3]
                        rotary_products(layer, 0, rx[0:64, :], ry[0:64, :], cos_r[0:64, :], sin_r[0:64, :], slice(0, 64))
                        dve.wait_ge(ones_row.sem, ones_row.at(layer, 1))
                        nc.vector.tensor_tensor(ab1[64:112, :], rx[64:112, :], rstd[64:112, :],
                                                ALU.mult).then_inc(proj_free.sem, 1)
                        nc.vector.tensor_tensor(second[64:80, :], ry[64:80, :], rstd[64:80, :],
                                                ALU.mult).then_inc(proj_free.sem, 1)
                        dve.wait_ge(proj_free.sem, proj_free.at(layer, 2))
                        for g in range(A_KV):
                            rows = slice(32 * g, 32 * g + 32)
                            nc.vector.tensor_tensor(k_a[0:32, g, :], work[rows, 0, :], work[rows, 1, :],
                                                    ALU.subtract).then_inc(rope_out.sem, 1)
                            nc.vector.tensor_tensor(k_a[32:64, g, :], work[rows, 2, :], work[rows, 3, :],
                                                    ALU.add).then_inc(rope_out.sem, 1)
                        rows = slice(64, 80)
                        rotary_products(layer, 4, ab1[rows, :], second[rows, :], rope[rows, 2, :], rope[rows, 3, :], rows)
                        dve.wait_ge(rope_prod.sem, rope_prod.at(layer, 8))
                        nc.vector.tensor_tensor(second[rows, :], work[rows, 0, :], work[rows, 1, :],
                                                ALU.subtract).then_inc(rope_out.sem, 1)
                        dve.wait_ge(rope_out.sem, rope_out.at(layer, 5))
                        nc.vector.tensor_tensor(work[rows, 0, :], work[rows, 2, :], work[rows, 3, :],
                                                ALU.add).then_inc(rope_out.sem, 1)
                    elif name == "rstd_nat":
                        dve.wait_ge(aux_ready.sem, aux_ready.at(layer, u + 1))
                        nc.vector.tensor_copy(rstd_nat[:, :], aux[:, :].rearrange("p (t n) -> p t n", t=TT)[:, :, 0]
                                              ).then_inc(aux_free.sem, 1)
                    elif name == "gla_gate":
                        dve.wait_ge(gla_soft.sem, gla_soft.at(layer, 3 * i + 3))
                        nc.vector.scalar_tensor_tensor(
                            log_a[:, 2 * i:2 * i + 2, :].rearrange("p t n -> p (t n)"), aux[:, :], 0.0,
                            soft[:, 2 * i:2 * i + 2, :].rearrange("p t n -> p (t n)"), ALU.min,
                            ALU.subtract).then_inc(aux_free.sem, 1)
                    elif name == "latent_norm":
                        refine(layer, AUX.index(("latent", i)), 1 + i, lat_rstd, (C_QR, C_KVR)[i]).then_inc(lat_rs.sem, 1)
                        dve.wait_ge(lat_rs.sem, lat_rs.at(layer, i + 1))
                        for n in ((0, 1), (2,))[i]:
                            col = G_CQ + n
                            nc.vector.scalar_tensor_tensor(latent[:, n, :], latent[:, n, :], par[:, col:col + 1],
                                                           lat_rstd, ALU.mult, ALU.mult).then_inc(lat_norm.sem, 1)
                    elif name == "latent_lo":
                        for n in ((0, 1), (2,))[i]:
                            dve.wait_ge(lat_hi_set.sem, lat_hi_set.at(layer, n + 1))
                            nc.vector.tensor_tensor(lat_lo[:, n, :], latent[:, n, :], lat_hi[:, n, :].bitcast(F32),
                                                    ALU.subtract).then_inc(lat_lo_set.sem, 1)
                    elif name == "gla_state":
                        dve.wait_ge(state_in.sem, state_in.at(layer, i + 1))
                        if i == 0:
                            end = AUX.index(("gla_end", 0))
                            dve.wait_ge(aux_free.sem, aux_free.at(layer, end + 1))
                        for c in range(2 * i, 2 * i + 2):
                            for j in range(2):
                                new = nat[2 * (i % 2) + c % 2][:, j * P:(j + 1) * P]
                                if c == 0:
                                    nc.vector.tensor_copy(state[:, 0, j, :], new).then_inc(state_set.sem, 1)
                                else:
                                    dve.wait_ge(state_set.sem, state_set.at(layer, 2 * (c - 1) + j + 1))
                                    nc.vector.scalar_tensor_tensor(
                                        state[:, c, j, :], state[:, c - 1, j, :], decay[:, j * NC + c:j * NC + c + 1],
                                        new, ALU.mult, ALU.add).then_inc(state_set.sem, 1)
                    elif name == "silu":
                        b, j = divmod(i, BR)
                        dve.wait_ge(gate_tanh.sem, gate_tanh.at(layer, 12 * b + j + 1))
                        nc.vector.scalar_tensor_tensor(gates[:, j, :], gates[:, 8 + j, :], 1.0, gates[:, j, :], ALU.add,
                                                       ALU.mult).then_inc(silu_set.sem, 1)
                    elif name == "gla_out":
                        refine(layer, AUX.index(("gla_norm", i)), 3 + i, o_rstd, B_DV).then_inc(read_rs.sem, 1)
                        dve.wait_ge(read_rs.sem, read_rs.at(layer, i + 1))
                        nc.vector.tensor_tensor(work[:, i % 2, :], nat[i][:, :], o_rstd, ALU.mult
                                                ).then_inc(read_norm.sem, 1)
                        dve.wait_ge(read_norm.sem, read_norm.at(layer, i + 1))
                        if i == 0:
                            dve.wait_ge(silu_set.sem, silu_set.at(layer, BR))
                        nc.vector.scalar_tensor_tensor(work[:, 2 + i % 2, :], work[:, i % 2, :], par[:, G_BH:G_BH + 1],
                                                       gates[:, i, :], ALU.mult, ALU.mult).then_inc(y_pre_set.sem, 1)
                    elif name == "gla_lo":
                        dve.wait_ge(y_hi_set.sem, y_hi_set.at(layer, i + 1))
                        nc.vector.tensor_tensor(y_lo[:, i, :], work[:, 2 + i % 2, :], y_hi[:, i, :].bitcast(F32),
                                                ALU.subtract).then_inc(y_lo_set.sem, 1)
                    elif name in ("score_a", "score_c"):
                        step = i if name == "score_a" else TT * A_KV + i
                        kind, qt, h, q_all = attention_of(step)
                        par2 = step % 2
                        bank = nat[i % 2]
                        dve.wait_ge(scores_done.sem, scores_done.at(layer, step + 1))
                        if kind == "a":
                            sc = bank[:, :].rearrange("p (h n) -> p h n", h=GROUP)
                            if qt == 0:
                                nc.vector.memset(sc[0:64, :, 0:64], NEG).then_inc(masked.sem, 1)
                                dve.wait_ge(masked.sem, masked.at(layer, step + 1))
                            nc.vector.tensor_reduce(top[:, par2, :], sc, AX_X, ALU.max,
                                                    negate=True).then_inc(top_set.sem, 1)
                            dve.wait_ge(top_set.sem, top_set.at(layer, 2 * step + 1))
                            heads = slice(h * GROUP, (h + 1) * GROUP)
                            nc.vector.scalar_tensor_tensor(neg_top[:, par2, :], top[:, par2, :], A_SCALE,
                                                           neg_sink[:, heads], ALU.mult,
                                                           ALU.min).then_inc(top_set.sem, 1)
                            dve.wait_ge(top_set.sem, top_set.at(layer, 2 * step + 2))
                            nc.vector.tensor_tensor(sink_in[:, par2, :], neg_top[:, par2, :], neg_sink[:, heads],
                                                    ALU.subtract).then_inc(neg_top_set.sem, 1)
                        else:
                            n = (qt + 1) * P
                            nc.vector.memset(bank[0:64, n - 64:n], NEG).then_inc(masked.sem, 1)
                            dve.wait_ge(masked.sem, masked.at(layer, A_KV + i + 1))
                            nc.vector.tensor_reduce(top[:, par2, 0:1], bank[:, 0:n], AX_X, ALU.max,
                                                    negate=True).then_inc(top_set.sem, 1)
                            dve.wait_ge(top_set.sem, top_set.at(layer, 2 * TT * A_KV + i + 1))
                            nc.vector.tensor_scalar(neg_top[:, par2, 0:1], top[:, par2, 0:1], C_SCALE, None,
                                                    ALU.mult).then_inc(neg_top_set.sem, 1)
                    elif name == "divide":
                        kind, qt, h, _ = attention_of(i)
                        dve.wait_ge(exp_done.sem, exp_done.at(layer, i + 1))
                        if kind == "a":
                            heads = slice(h * GROUP, (h + 1) * GROUP)
                            nc.vector.tensor_tensor(recip[:, heads], sums[:, qt, heads], sink_exp[:, qt, heads],
                                                    ALU.add).then_inc(denom_set.sem, 1)
                            dve.wait_ge(denom_set.sem, denom_set.at(layer, 2 * i + 1))
                            nc.vector.reciprocal(recip[:, heads], recip[:, heads]).then_inc(denom_set.sem, 1)
                            dve.wait_ge(denom_set.sem, denom_set.at(layer, 2 * i + 2))
                            p4 = prob[i % 3].rearrange("p (h n) -> p h n", h=GROUP)
                            nc.vector.tensor_tensor(p4, p4, recip[:, heads].unsqueeze(2).broadcast_to([P, GROUP, P]),
                                                    ALU.mult).then_inc(divided.sem, 1)
                        else:
                            n = (qt + 1) * P
                            nc.vector.reciprocal(recip[:, h:h + 1], sums[:, qt, h:h + 1]).then_inc(denom_set.sem, 1)
                            dve.wait_ge(denom_set.sem, denom_set.at(layer, TT * A_KV + i + 1))
                            nc.vector.tensor_scalar(prob[i % 3][:, 0:n], prob[i % 3][:, 0:n], recip[:, h:h + 1], None,
                                                    ALU.mult).then_inc(divided.sem, 1)
                    elif name == "y_lo":
                        ts = slice((i % TT) * P, (i % TT + 1) * P)
                        pre = y_pre[:, :].rearrange("p (f n) -> p f n", f=BR)
                        dve.wait_ge(y_hi_set.sem, y_hi_set.at(layer, BR + i + 1))
                        nc.vector.tensor_tensor(y_lo[:, :, ts], pre, y_hi[:, :, ts].bitcast(F32),
                                                ALU.subtract).then_inc(y_lo_set.sem, 1)
                    elif name == "value_a" and i % A_KV == A_KV - 1:
                        dve.wait_ge(value_done.sem, value_done.at(layer, i + 1))
                        gate_branch(layer, i // A_KV).then_inc(o_read.sem, 1)
                    elif name == "value_c" and (i + 1) % (C_HEADS // 2) == 0:
                        dve.wait_ge(value_done.sem, value_done.at(layer, TT * A_KV + i + 1))
                        gate_branch(layer, TT + i // (C_HEADS // 2)).then_inc(o_read.sem, 1)
                    elif name == "quarter" and i % 4 == 3:
                        p = i // 4
                        res = ring[first_output(p) % 3][:, :]
                        g = gate_index(p)
                        if g is not None:
                            b, j = g
                            evacuated(layer, p)
                            if j >= 8:
                                dve.wait_ge(silu_set.sem, silu_set.at(layer, BR * b + j - 8 + 1))
                            nc.vector.scalar_tensor_tensor(gates[:, j, :], res, 0.5, rstd[:, :], ALU.mult,
                                                           ALU.mult).then_inc(proj_free.sem, 1)
                        elif p in (PQA + 1, PQA + 3):
                            n = (p - PQA) // 2
                            evacuated(layer, p)
                            ra, rb = (ring[first_output(q) % 3][:, :] for q in (p - 1, p))
                            if n == 0:
                                dve.wait_ge(k_rope_saved.sem, k_rope_saved.at(layer, 32))
                            dve.wait_ge(rope_out.sem, rope_out.at(layer, 6 + 8 * n))
                            nc.vector.tensor_tensor(work[:, 0, :], ra, cos_r, ALU.mult).then_inc(rope_prod.sem, 1)
                            nc.vector.tensor_tensor(work[:, 3, :], ra, sin_r, ALU.mult).then_inc(proj_free.sem, 1)
                            nc.vector.tensor_tensor(work[:, 1, :], rb, sin_r, ALU.mult).then_inc(rope_prod.sem, 1)
                            nc.vector.tensor_tensor(work[:, 2, :], rb, cos_r, ALU.mult).then_inc(proj_free.sem, 1)
                            dve.wait_ge(proj_free.sem, proj_free.at(layer, first_output(p) + 1))
                            for hh in range(4):
                                h = 4 * n + hh
                                rows = slice(32 * hh, 32 * hh + 32)
                                nc.vector.tensor_tensor(q_a[0:32, h, :], work[rows, 0, :],
                                                        work[rows, 1, :], ALU.subtract).then_inc(rope_out.sem, 1)
                                nc.vector.tensor_tensor(q_a[32:64, h, :], work[rows, 2, :],
                                                        work[rows, 3, :], ALU.add).then_inc(rope_out.sem, 1)
                        elif p == PN1 + 3:
                            evacuated(layer, p)
                            dve.wait_ge(aux_free.sem, aux_free.at(layer, AUX.index(("gla_decay", 1)) + 1))
                            for t in range(TT):
                                nc.vector.scalar_tensor_tensor(k_dec[:, t, :], nat[t][:, 0:256], rstd_nat[:, t:t + 1],
                                                               dec[:, t, :], ALU.mult, ALU.mult)
                                nc.vector.tensor_scalar(v_a[:, t, :], nat[t][:, 256:384], rstd_nat[:, t:t + 1], None,
                                                        ALU.mult).then_inc(nat_free.sem, 1)
                        elif p == PN2 + 3:
                            evacuated(layer, p)
                            for t in range(TT):
                                nc.vector.tensor_scalar(v_b[:, t, :], nat[t][:, :], rstd_nat[:, t:t + 1], None,
                                                        ALU.mult).then_inc(nat_free.sem, 1)
                        elif PQB <= p < PQB + 2:
                            evacuated(layer, p)
                            nc.vector.scalar_tensor_tensor(q_b[:, p - PQB, :], res, B_DK ** -0.5, rstd[:, :], ALU.mult,
                                                           ALU.mult).then_inc(proj_free.sem, 1)
                        elif PCQ <= p <= PCKV:
                            evacuated(layer, p)
                            nc.vector.tensor_tensor(latent[:, p - PCQ, :], res, rstd[:, :],
                                                    ALU.mult).then_inc(proj_free.sem, 1)
                            if p == PCQ + 1:
                                dve.wait_ge(lat_sq.sem, lat_sq.at(layer, 2))
                                nc.vector.tensor_tensor(sq_sum, sq[0], sq[1], ALU.add).then_inc(lat_acc.sem, 1)
                        elif any(o <= p < o + 4 for o in PO):
                            b = [o <= p < o + 4 for o in PO].index(True)
                            for o in range(2):
                                j = 2 * (p - PO[b]) + o
                                evacuated(layer, p, o + 1)
                                z = ring[(first_output(p) + o) % 3][:, :]
                                dve.wait_ge(gate_tanh.sem, gate_tanh.at(layer, 12 * b + 4 + j + 1))
                                tile = gates[:, 4 + j, :]
                                nc.vector.scalar_tensor_tensor(merged[:, j, :] if b == 0 else tile, tile, 1.0, z,
                                                               ALU.add, ALU.mult).then_inc(proj_free.sem, 1)
                                dve.wait_ge(proj_free.sem, proj_free.at(layer, first_output(p) + o + 1))
                                if b > 0:
                                    nc.vector.tensor_tensor(merged[:, j, :], merged[:, j, :], tile,
                                                            ALU.add).then_inc(merged_set.sem, 1)
                            if b == 2:
                                for o in range(2):
                                    j = 2 * (p - PO[b]) + o
                                    dve.wait_ge(merge_hi.sem, merge_hi.at(layer, j + 1))
                                    nc.vector.scalar_tensor_tensor(act_lo[:, j, :], merged[:, j, :], 0.5,
                                                                   act_hi[:, j, :].bitcast(F32), ALU.mult,
                                                                   ALU.subtract).then_inc(merge_lo.sem, 1)
                        elif p == PUKV:
                            dve.wait_ge(read_done.sem, read_done.at(layer, 4))
                            dve.wait_ge(value_done.sem, value_done.at(layer, TT * A_KV))
                            for o in range(8):
                                evacuated(layer, p, o + 1)
                                r = ring[(first_output(p) + o) % 3]
                                if o < 4:
                                    nc.vector.tensor_copy(v_c[:, o, :], r[:, :]).then_inc(proj_free.sem, 1)
                                else:
                                    h = 2 * (o - 4)
                                    nc.vector.tensor_copy(k_c[0:64, h, :], r[0:64, :])
                                    nc.vector.tensor_copy(k_c[0:64, h + 1, :], r[64:128, :]).then_inc(proj_free.sem, 1)
                        elif p in (PUQ, PUQ + 1):
                            if p == PUQ:
                                evacuated(layer, p, 2)
                                f = first_output(p)
                                ra, rb = ring[f % 3][:, :], ring[(f + 1) % 3][:, :]
                                cos, sin = rope[:, 2, :], rope[:, 3, :]
                                nc.vector.tensor_tensor(work[:, 0, :], ra, cos, ALU.mult).then_inc(rope_prod.sem, 1)
                                nc.vector.tensor_tensor(work[:, 3, :], ra, sin, ALU.mult).then_inc(proj_free.sem, 1)
                                nc.vector.tensor_tensor(work[:, 1, :], rb, sin, ALU.mult).then_inc(rope_prod.sem, 1)
                                nc.vector.tensor_tensor(work[:, 2, :], rb, cos, ALU.mult).then_inc(proj_free.sem, 1)
                                dve.wait_ge(proj_free.sem, proj_free.at(layer, f + 2))
                                nc.vector.tensor_tensor(work[:, 0, :], work[:, 0, :], work[:, 1, :],
                                                        ALU.subtract).then_inc(rope_out.sem, 1)
                                nc.vector.tensor_tensor(work[:, 2, :], work[:, 2, :], work[:, 3, :],
                                                        ALU.add).then_inc(rope_out.sem, 1)
                            for o in ((2,) if p == PUQ else (0, 1, 2)):
                                evacuated(layer, p, o + 1)
                                r = ring[(first_output(p) + o) % 3]
                                h = 0 if p == PUQ else 2 * (o + 1)
                                nc.vector.tensor_copy(q_c[0:64, h, :], r[0:64, :])
                                nc.vector.tensor_copy(q_c[0:64, h + 1, :], r[64:128, :]).then_inc(proj_free.sem, 1)
                        elif p >= PW:
                            evacuated(layer, p)
                            nc.vector.tensor_tensor(xt[:, p - PW, :], xt[:, p - PW, :], res,
                                                    ALU.add).then_inc(proj_free.sem, 1)
                            if PW < p <= PW + KT - LATE:
                                add_square(layer, LATE + p - PW)
                    if (name, i) in AUX:
                        u += 1
            for n in range(1, LATE):
                add_square(DEPTH, n)
            refine(DEPTH, 0, 0, rstd[:, :], D).then_inc(rstd_set.sem, 1)
            dve.wait_ge(rstd_set.sem, rstd_set.at(DEPTH, 1))
            for j in range(DVE_TILES):
                dve.wait_ge(gained.sem, j + 1)
                nc.vector.tensor_tensor(gates[:, j, :], gates[:, j, :], rstd[:, :],
                                        ALU.mult).then_inc(scaled_dve.sem, 1)


def pack_pieces(w_in, w_oa, w_ob, w_oc, w_uq, w_ukv, w_out):
    off = dict(zip(("qa", "ka", "va", "ga", "qb", "kb", "vb", "ab", "gb", "cq", "ckv", "kr", "gc", "mg"),
                   np.cumsum([0, 512, 128, 128, 512, 256, 256, 512, 16, 512, 256, 128, 32, 512])))
    out = np.zeros((DEPTH, PIECES, P, 1024), w_in.dtype)

    def put(layer, p, w, cols, tiles=None):
        w = w[:, cols].reshape(-1, P, len(cols))
        w = w if tiles is None else w[tiles]
        out[layer, p, :, :w.shape[0] * w.shape[2]] = w.transpose(1, 0, 2).reshape(P, -1)

    for l in range(DEPTH):
        w = w_in[l]
        for p, half in ((PX, 0), (PY, 1)):
            ka = [off["ka"] + 64 * g + 32 * half + r for g in range(A_KV) for r in range(32)]
            kr = [off["kr"] + 16 * half + r for r in range(16)]
            tile = out[l, p].reshape(P, KT, P)
            src = w.reshape(KT, P, -1).transpose(1, 0, 2)
            tile[:, :, 0:64] = src[:, :, ka]
            tile[:, :, 64:80] = src[:, :, kr]
            if half == 0:
                tile[:, :, 96:112] = src[:, :, off["ab"]:off["ab"] + B_RANK]
        for n in range(2):
            for half in range(2):
                put(l, PQA + 2 * n + half, w, [off["qa"] + 64 * (4 * n + h) + 32 * half + r
                                               for h in range(4) for r in range(32)])
        for n in range(4):
            put(l, PN1 + n, w, [*range(off["kb"], off["kb"] + 256), *range(off["va"], off["va"] + 128)],
                slice(2 * n, 2 * n + 2))
            put(l, PN2 + n, w, list(range(off["vb"], off["vb"] + 512)), slice(2 * n, 2 * n + 2))
        for n in range(2):
            put(l, PQB + n, w, list(range(off["qb"] + P * n, off["qb"] + P * n + P)))
            put(l, PCQ + n, w, list(range(off["cq"] + P * n, off["cq"] + P * n + P)))
        put(l, PCKV, w, list(range(off["ckv"], off["ckv"] + P)))
        for b, (gate, branch, wo) in enumerate((("gb", 1, w_ob), ("ga", 0, w_oa), ("gc", 2, w_oc))):
            for n in range(4):
                put(l, PG[b] + n, w, list(range(off[gate] + P * n, off[gate] + P * n + P)))
                put(l, PO[b] + n, wo[l], list(range(256 * n, 256 * n + 256)))
            for n in range(8):
                c = off["mg"] + D * branch + P * n
                put(l, PM[b] + n, w, list(range(c, c + P)))
        kv = C_NOPE + C_V
        put(l, PUKV, w_ukv[l], [kv * h + r for h in range(C_HEADS) for r in range(C_NOPE)]
            + [kv * h + C_NOPE + r for h in range(C_HEADS) for r in range(C_V)])
        first = [C_DH * h + C_NOPE + r for h in range(C_HEADS) for r in range(16)]
        nope = [C_DH * h + r for h in range(C_HEADS) for r in range(C_NOPE)]
        put(l, PUQ, w_uq[l], first + [c + 16 for c in first] + nope[0:P])
        put(l, PUQ + 1, w_uq[l], nope[P:])
        for n in range(KT):
            put(l, PW + n, w_out[l], list(range(P * n, P * n + P)))
    return out.reshape(DEPTH * PIECES, P, 1024)


def rotary_tables():
    out = np.zeros((P, 4, S), np.float32)
    pos = np.arange(S, dtype=np.float32)
    for n, dim in enumerate((A_DH, C_ROPE)):
        inv = (10000.0 ** (-np.arange(0, dim, 2) / dim)).astype(np.float32)
        ang = (inv[:, None] * pos[None, :]).astype(np.float32)
        reps = P // len(inv)
        out[:, 2 * n] = np.tile(np.cos(ang), (reps, 1))
        out[:, 2 * n + 1] = np.tile(np.sin(ang), (reps, 1))
    return out


def constant_table():
    t = np.arange(P)
    same = t[:, None] // CHUNK == t[None, :] // CHUNK
    out = np.zeros((P, CONSTS), np.float32)
    out[:, ONES:ONES + P] = 1.0
    out[:, IDENT:IDENT + P] = np.eye(P)
    out[:, LATER:LATER + P] = (same & (t[:, None] > t[None, :])) / B_TAU
    out[:, MEMBER:MEMBER + 2] = (t[:, None] // CHUNK == np.arange(2)[None, :]) / B_TAU
    return out


def kernel(x, norm_g, w_in, a_sinks, w_oa, w_alpha, b_alpha, b_head_g, w_ob, cq_g, w_uq, ckv_g, w_ukv, w_oc, w_out,
           final_g):
    import concourse.bacc as bacc
    from concourse.bass_utils import run_bass_kernel_spmd

    (x, norm_g, w_in, a_sinks, w_oa, w_alpha, b_alpha, b_head_g, w_ob, cq_g, w_uq, ckv_g, w_ukv, w_oc, w_out,
     final_g) = (np.asarray(a) for a in (x, norm_g, w_in, a_sinks, w_oa, w_alpha, b_alpha, b_head_g, w_ob, cq_g, w_uq,
                                         ckv_g, w_ukv, w_oc, w_out, final_g))
    params = np.zeros((P, DEPTH, PARAMS), x.dtype)
    for l in range(DEPTH):
        params[:, l, G_X:G_X + KT] = norm_g[l].reshape(KT, P).T
        params[:, l, G_BH] = b_head_g[l]
        params[:, l, G_CQ:G_CQ + 2] = cq_g[l].reshape(2, P).T
        params[:, l, G_CKV] = ckv_g[l]
        params[:, l, SINKS:SINKS + A_HEADS] = a_sinks[l][None, :]
    arrays = {
        "x_t": np.ascontiguousarray(x[0].T.reshape(KT, P, S).transpose(1, 0, 2)),
        "pieces": pack_pieces(w_in, w_oa, w_ob, w_oc, w_uq, w_ukv, w_out),
        "params": params,
        "alpha": np.ascontiguousarray(np.concatenate([w_alpha, b_alpha[:, None, :]], axis=1).transpose(1, 0, 2)),
        "tables": rotary_tables(),
        "consts": constant_table(),
        "final_gain": np.ascontiguousarray(final_g.reshape(KT, P).T),
    }
    nc = bacc.Bacc("TRN2", target_bir_lowering=False, num_devices=1, dynamic_dma_scratch_size=1024)
    aps = [nc.dram_tensor(name, a.shape, mybir.dt.from_np(a.dtype), kind="ExternalInput").ap()
           for name, a in arrays.items()]
    out_t = nc.dram_tensor("out_t", (P, KT, S), F32, kind="ExternalOutput").ap()
    k_rope_dram = nc.dram_tensor("k_rope_dram", (C_ROPE, S), F32, kind="Internal").ap()
    q_rope_dram = nc.dram_tensor("q_rope_dram", (2, P, S), F32, kind="Internal").ap()
    build_hybrid_trunk(nc, *aps, out_t, k_rope_dram, q_rope_dram)
    r = run_bass_kernel_spmd(nc, [arrays], core_ids=[0])
    got = r.results[0]["out_t"]
    return np.ascontiguousarray(got.transpose(1, 0, 2).reshape(D, S).T)[None]
```
